# Optimizing a Trainium2 kernel written in Bass

```python
import jax, jax.numpy as jnp
from jax import lax
import numpy as np
import math

D_MODEL = 1024
BATCH = 1
SEQ = 512
DEPTH = 2

GRID_W = 64
CTX_LEN = 256
HEAD_DIM = 64
GROUP_W = D_MODEL // 4
N_HEADS = GROUP_W // HEAD_DIM
N_KV_HEADS = N_HEADS // 2
GQ = N_HEADS // N_KV_HEADS
KV_W = N_KV_HEADS * HEAD_DIM
IN_W = 5 * GROUP_W + 2 * (GROUP_W + 2 * KV_W)
SHORT_CONV = 3
CONF_CONV = 31
WINDOW = 128
Q_BLOCK = 128
N_EXPERTS = 16
EXPERT_FF = D_MODEL
CAPACITY_FACTOR = 2
ROPE_THETA = 10000.0
EPS = 1e-6


def rms_norm(x, g):
    xf = x.astype(jnp.float32)
    y = xf * lax.rsqrt(jnp.mean(xf * xf, axis=-1, keepdims=True) + EPS)
    return (y * g.astype(jnp.float32)).astype(x.dtype)

def layer_norm(x, g, b):
    xf = x.astype(jnp.float32)
    mu = jnp.mean(xf, axis=-1, keepdims=True)
    var = jnp.mean(jnp.square(xf - mu), axis=-1, keepdims=True)
    y = (xf - mu) * lax.rsqrt(var + EPS)
    return (y * g.astype(jnp.float32) + b.astype(jnp.float32)).astype(x.dtype)

def dwconv(x, w):
    k = w.shape[0]
    return lax.conv_general_dilated(x, w[:, None, :].astype(x.dtype), (1,), [(k // 2, k // 2)],
                                    dimension_numbers=('NWC', 'WIO', 'NWC'),
                                    feature_group_count=x.shape[-1])

def split_proj(p):
    sizes = (GROUP_W,) * 5 + (GROUP_W, KV_W, KV_W) * 2
    return jnp.split(p, np.cumsum(sizes)[:-1].tolist(), axis=-1)

def q_heads(t):
    return t.reshape(*t.shape[:-1], N_KV_HEADS, GQ, HEAD_DIM)

def kv_heads(t):
    return t.reshape(*t.shape[:-1], N_KV_HEADS, HEAD_DIM)

def short_conv_mixer(b, c, h, w):
    return b * dwconv(c * h, w)

def conformer_conv(a, g, w, bias, ln_g, ln_b):
    u = a * jax.nn.sigmoid(g)
    u = dwconv(u, w) + bias
    return jax.nn.silu(layer_norm(u, ln_g, ln_b))

def rope_tables(s):
    rows = s // GRID_W
    row = jnp.repeat(jnp.arange(rows), GRID_W).astype(jnp.float32)
    col = (jnp.arange(rows * GRID_W) % GRID_W).astype(jnp.float32)
    quarter = HEAD_DIM // 4
    inv = ROPE_THETA ** (-jnp.arange(quarter, dtype=jnp.float32) / quarter)
    ar = row[:, None] * inv
    ac = col[:, None] * inv
    ang = jnp.concatenate([ar, ar, ac, ac], axis=-1)
    return jnp.cos(ang), jnp.sin(ang)

def apply_rope(x, cos, sin):
    bshape = (cos.shape[0],) + (1,) * (x.ndim - 3) + (HEAD_DIM,)
    c = cos.reshape(bshape).astype(x.dtype)
    s = sin.reshape(bshape).astype(x.dtype)
    xs = x.reshape(*x.shape[:-1], 2, 2, HEAD_DIM // 4)
    rot = jnp.stack([-xs[..., 1, :], xs[..., 0, :]], axis=-2).reshape(x.shape)
    return x * c + rot * s

def gqa_attend(q, k, v, sink=None):
    s = jnp.einsum('bqkgd,bjkd->bkgqj', q, k).astype(jnp.float32) * (HEAD_DIM ** -0.5)
    if sink is not None:
        sl = jnp.broadcast_to(sink.reshape(N_KV_HEADS, GQ)[None, :, :, None, None].astype(jnp.float32),
                              s.shape[:-1] + (1,))
        s = jnp.concatenate([s, sl], axis=-1)
    p = jax.nn.softmax(s, axis=-1)
    if sink is not None:
        p = p[..., :-1]
    return jnp.einsum('bkgqj,bjkd->bqkgd', p.astype(v.dtype), v)

def window_attention(q, k, v, kc, vc, sink):
    bsz, s = q.shape[:2]
    nb = s // Q_BLOCK
    qb = q.reshape(bsz, nb, Q_BLOCK, N_KV_HEADS, GQ, HEAD_DIM)

    def bands(t):
        tp = jnp.pad(t, ((0, 0), (Q_BLOCK, Q_BLOCK), (0, 0), (0, 0)))
        tp = tp.reshape(bsz, nb + 2, Q_BLOCK, N_KV_HEADS, HEAD_DIM)
        return jnp.concatenate([tp[:, :-2], tp[:, 1:-1], tp[:, 2:]], axis=2)

    kw, vw = bands(k), bands(v)
    scale = HEAD_DIM ** -0.5
    s_loc = jnp.einsum('bnqkgd,bnjkd->bnkgqj', qb, kw).astype(jnp.float32) * scale
    s_ctx = jnp.einsum('bnqkgd,bckd->bnkgqc', qb, kc).astype(jnp.float32) * scale
    blk = jnp.arange(nb)[:, None, None] * Q_BLOCK
    qpos = blk + jnp.arange(Q_BLOCK)[None, :, None]
    kpos = blk - Q_BLOCK + jnp.arange(3 * Q_BLOCK)[None, None, :]
    valid = (kpos >= 0) & (kpos < s) & (jnp.abs(qpos - kpos) <= WINDOW)
    s_loc = jnp.where(valid[None, :, None, None], s_loc, -jnp.inf)
    sl = jnp.broadcast_to(sink.reshape(N_KV_HEADS, GQ)[None, None, :, :, None, None].astype(jnp.float32),
                          s_loc.shape[:-1] + (1,))
    p = jax.nn.softmax(jnp.concatenate([s_loc, s_ctx, sl], axis=-1), axis=-1)
    n_loc = 3 * Q_BLOCK
    p_loc = p[..., :n_loc].astype(v.dtype)
    p_ctx = p[..., n_loc:n_loc + kc.shape[1]].astype(v.dtype)
    o = (jnp.einsum('bnkgqj,bnjkd->bnqkgd', p_loc, vw)
         + jnp.einsum('bnkgqc,bckd->bnqkgd', p_ctx, vc))
    return o.reshape(bsz, s, GROUP_W)

def global_attention(q, k, v, kc, vc):
    bsz, s = q.shape[:2]
    nb = s // Q_BLOCK
    kall = jnp.concatenate([k, kc], axis=1)
    vall = jnp.concatenate([v, vc], axis=1)
    qb = jnp.moveaxis(q.reshape(bsz, nb, Q_BLOCK, N_KV_HEADS, GQ, HEAD_DIM), 1, 0)
    o = lax.map(lambda qblk: gqa_attend(qblk, kall, vall), qb)
    return jnp.moveaxis(o, 0, 1).reshape(bsz, s, GROUP_W)

def expert_choice_ffn(h, router, w_gate, w_up, w_down):
    bsz, t, d = h.shape
    cap = CAPACITY_FACTOR * t // N_EXPERTS
    aff = jax.nn.softmax((h @ router).astype(jnp.float32), axis=-1)
    gates, idx = lax.top_k(jnp.swapaxes(aff, 1, 2), cap)
    xs = jax.vmap(lambda hb, ib: hb[ib])(h, idx)
    a = jnp.einsum('becd,edf->becf', xs, w_gate)
    u = jnp.einsum('becd,edf->becf', xs, w_up)
    y = jnp.einsum('becf,efd->becd', jax.nn.silu(a) * u, w_down)
    y = y * gates[..., None].astype(y.dtype)
    return jax.vmap(lambda ib, yb: jnp.zeros((t, d), yb.dtype).at[ib.reshape(-1)].add(yb.reshape(-1, d)))(idx, y)

def layer(x, xc, mods, cmods, n1, n2, w_in, conv_a, conv_b, conv_b_bias, cln_g, cln_b, sink,
          qn_g, kn_g, w_out, router, w_gate, w_up, w_down, cos, sin, need_ctx):
    sh1, sc1, g1, sh2, sc2, g2 = [m[:, None] for m in jnp.split(mods, 6, axis=-1)]
    csh1, csc1, cg1, csh2, csc2, cg2 = [m[:, None] for m in jnp.split(cmods, 6, axis=-1)]
    bsz, s = x.shape[:2]
    lc = xc.shape[1]

    h = rms_norm(x, n1) * (1 + sc1) + sh1
    hc = rms_norm(xc, n1) * (1 + csc1) + csh1
    a_b, a_c, a_h, b_v, b_g, c_q, c_k, c_v, d_q, d_k, d_v = split_proj(h @ w_in)
    ca_b, ca_c, ca_h, cb_v, cb_g, cc_q, cc_k, cc_v, cd_q, cd_k, cd_v = split_proj(hc @ w_in)

    kc_c, vc_c = kv_heads(cc_k), kv_heads(cc_v)
    kc_d, vc_d = rms_norm(kv_heads(cd_k), kn_g), kv_heads(cd_v)

    ya = short_conv_mixer(a_b, a_c, a_h, conv_a)
    yb = conformer_conv(b_v, b_g, conv_b, conv_b_bias, cln_g, cln_b)
    yc = window_attention(apply_rope(q_heads(c_q), cos, sin), apply_rope(kv_heads(c_k), cos, sin),
                          kv_heads(c_v), kc_c, vc_c, sink)
    yd = global_attention(apply_rope(rms_norm(q_heads(d_q), qn_g), cos, sin),
                          apply_rope(rms_norm(kv_heads(d_k), kn_g), cos, sin),
                          kv_heads(d_v), kc_d, vc_d)
    x_new = x + g1 * (jnp.concatenate([ya, yb, yc, yd], axis=-1) @ w_out)
    h2 = rms_norm(x_new, n2) * (1 + sc2) + sh2
    x_new = x_new + g2 * expert_choice_ffn(h2, router, w_gate, w_up, w_down)

    if need_ctx:
        yca = short_conv_mixer(ca_b, ca_c, ca_h, conv_a)
        ycb = conformer_conv(cb_v, cb_g, conv_b, conv_b_bias, cln_g, cln_b)
        ycc = gqa_attend(q_heads(cc_q), kc_c, vc_c, sink).reshape(bsz, lc, GROUP_W)
        ycd = gqa_attend(rms_norm(q_heads(cd_q), qn_g), kc_d, vc_d).reshape(bsz, lc, GROUP_W)
        xc = xc + cg1 * (jnp.concatenate([yca, ycb, ycc, ycd], axis=-1) @ w_out)
        hc2 = rms_norm(xc, n2) * (1 + csc2) + csh2
        xc = xc + cg2 * expert_choice_ffn(hc2, router, w_gate, w_up, w_down)
    return x_new, xc

def first_inputs(seed: int = 0) -> dict:
    key = jax.random.key(seed)
    ks = jax.random.split(key, 24)
    f32 = jnp.float32
    nrm = lambda k, shape, scale: jax.random.normal(k, shape, f32) * scale
    d = D_MODEL
    return {
        "x": nrm(ks[0], (BATCH, SEQ, d), 1.0),
        "c": nrm(ks[1], (BATCH, d), 1.0),
        "ctx": nrm(ks[2], (BATCH, CTX_LEN, d), 1.0),
        "c_ctx": nrm(ks[3], (d,), 1.0),
        "ada_w": nrm(ks[4], (DEPTH, d, 6 * d), 0.5 * d ** -0.5),
        "ada_b": nrm(ks[5], (DEPTH, 6 * d), 0.01),
        "norm1_g": 1.0 + nrm(ks[6], (DEPTH, d), 0.01),
        "norm2_g": 1.0 + nrm(ks[7], (DEPTH, d), 0.01),
        "w_in": nrm(ks[8], (DEPTH, d, IN_W), d ** -0.5),
        "conv_a_w": nrm(ks[9], (DEPTH, SHORT_CONV, GROUP_W), SHORT_CONV ** -0.5),
        "conv_b_w": nrm(ks[10], (DEPTH, CONF_CONV, GROUP_W), CONF_CONV ** -0.5),
        "conv_b_b": nrm(ks[11], (DEPTH, GROUP_W), 0.01),
        "conv_ln_g": 1.0 + nrm(ks[12], (DEPTH, GROUP_W), 0.01),
        "conv_ln_b": nrm(ks[13], (DEPTH, GROUP_W), 0.01),
        "sink": nrm(ks[14], (DEPTH, N_HEADS), 1.0),
        "q_norm_g": 1.0 + nrm(ks[15], (DEPTH, HEAD_DIM), 0.01),
        "k_norm_g": 1.0 + nrm(ks[16], (DEPTH, HEAD_DIM), 0.01),
        "w_out": nrm(ks[17], (DEPTH, d, d), d ** -0.5),
        "router_w": nrm(ks[18], (DEPTH, d, N_EXPERTS), d ** -0.5),
        "w_gate": nrm(ks[19], (DEPTH, N_EXPERTS, d, EXPERT_FF), d ** -0.5),
        "w_up": nrm(ks[20], (DEPTH, N_EXPERTS, d, EXPERT_FF), d ** -0.5),
        "w_down": nrm(ks[21], (DEPTH, N_EXPERTS, EXPERT_FF, d), EXPERT_FF ** -0.5),
        "final_g": 1.0 + nrm(ks[22], (d,), 0.01),
    }

def first_block(x, c, ctx, c_ctx, ada_w, ada_b, norm1_g, norm2_g, w_in, conv_a_w, conv_b_w, conv_b_b,
              conv_ln_g, conv_ln_b, sink, q_norm_g, k_norm_g, w_out, router_w, w_gate, w_up, w_down,
              final_g):
    cos, sin = rope_tables(x.shape[1])
    sc = jax.nn.silu(c)
    scc = jax.nn.silu(c_ctx)[None]
    xc = ctx
    for i in range(DEPTH):
        mods = sc @ ada_w[i] + ada_b[i]
        cmods = scc @ ada_w[i] + ada_b[i]
        x, xc = layer(x, xc, mods, cmods, norm1_g[i], norm2_g[i], w_in[i], conv_a_w[i], conv_b_w[i],
                      conv_b_b[i], conv_ln_g[i], conv_ln_b[i], sink[i], q_norm_g[i], k_norm_g[i],
                      w_out[i], router_w[i], w_gate[i], w_up[i], w_down[i], cos, sin,
                      i < DEPTH - 1)
    return rms_norm(x, final_g)


DEPTH_2 = 1

ROPE_THETA_2 = 500000.0
D_FF = 2816

MLA_HEADS = 8
MLA_Q_RANK = 256
MLA_KV_RANK = 128
MLA_NOPE = 64
MLA_ROPE = 32
MLA_V = 64
MLA_WIDTH = MLA_HEADS * MLA_V

DIFF_HEADS = 4
DIFF_HEAD_DIM = 64
DIFF_ROT = DIFF_HEAD_DIM // 4
DIFF_WIDTH = DIFF_HEADS * 2 * DIFF_HEAD_DIM

IN_SPLITS = (MLA_Q_RANK, MLA_KV_RANK, MLA_ROPE, DIFF_WIDTH, DIFF_WIDTH, DIFF_WIDTH, D_MODEL, D_MODEL)
IN_COLS = sum(IN_SPLITS)


def rms_norm_2(x, w):
    xf = x.astype(jnp.float32)
    y = xf * lax.rsqrt(jnp.mean(xf * xf, axis=-1, keepdims=True) + EPS)
    return (y * w.astype(jnp.float32)).astype(x.dtype)

def swiglu(x, w_gate, w_up, w_down):
    return (jax.nn.silu(x @ w_gate) * (x @ w_up)) @ w_down

def apply_rope_2(x, positions, rot_dim):
    half = rot_dim // 2
    inv_freq = jnp.power(jnp.float32(ROPE_THETA_2), -2.0 * jnp.arange(half, dtype=jnp.float32) / rot_dim)
    ang = positions.astype(jnp.float32)[..., None] * inv_freq
    cos = jnp.cos(ang)[:, :, None, :]
    sin = jnp.sin(ang)[:, :, None, :]
    xr = x[..., :rot_dim].astype(jnp.float32)
    x1, x2 = xr[..., :half], xr[..., half:]
    rot = jnp.concatenate([x1 * cos - x2 * sin, x2 * cos + x1 * sin], axis=-1).astype(x.dtype)
    return jnp.concatenate([rot, x[..., rot_dim:]], axis=-1)

def to_blocks(t):
    b, s, h, d = t.shape
    return t.reshape(b, s // Q_BLOCK, Q_BLOCK, h, d).transpose(1, 0, 3, 2, 4)

def from_blocks(t):
    nb, b, h, qb, d = t.shape
    return t.transpose(1, 0, 3, 2, 4).reshape(b, nb * qb, h, d)

def causal_probs(q_blk, k, blk_idx, scale):
    s = jnp.einsum('bhqd,bhkd->bhqk', q_blk, k).astype(jnp.float32) * scale
    q_pos = blk_idx * Q_BLOCK + jnp.arange(Q_BLOCK)
    k_pos = jnp.arange(k.shape[2])
    mask = k_pos[None, :] <= q_pos[:, None]
    s = jnp.where(mask, s, -jnp.inf)
    return jax.nn.softmax(s, axis=-1)

def mla_branch(c_q, c_kv, k_rope_raw, positions, q_norm, w_uq, kv_norm, w_ukv):
    b, s, _ = c_q.shape
    q = (rms_norm_2(c_q, q_norm) @ w_uq).reshape(b, s, MLA_HEADS, MLA_NOPE + MLA_ROPE)
    q = jnp.concatenate([q[..., :MLA_NOPE], apply_rope_2(q[..., MLA_NOPE:], positions, MLA_ROPE)], axis=-1)
    kv = (rms_norm_2(c_kv, kv_norm) @ w_ukv).reshape(b, s, MLA_HEADS, MLA_NOPE + MLA_V)
    k_nope, v = kv[..., :MLA_NOPE], kv[..., MLA_NOPE:]
    k_rope = apply_rope_2(k_rope_raw.reshape(b, s, 1, MLA_ROPE), positions, MLA_ROPE)
    k = jnp.concatenate([k_nope, jnp.broadcast_to(k_rope, (b, s, MLA_HEADS, MLA_ROPE))], axis=-1)
    kt = k.transpose(0, 2, 1, 3)
    vt = v.transpose(0, 2, 1, 3)
    scale = (MLA_NOPE + MLA_ROPE) ** -0.5

    def block(args):
        qb, i = args
        p = causal_probs(qb, kt, i, scale)
        return jnp.einsum('bhqk,bhkd->bhqd', p.astype(vt.dtype), vt)

    out = lax.map(block, (to_blocks(q), jnp.arange(s // Q_BLOCK)))
    return from_blocks(out).reshape(b, s, MLA_WIDTH)

def diff_branch(q, k, v, positions, lam_q1, lam_k1, lam_q2, lam_k2, subln, layer_idx):
    b, s, _ = q.shape
    hd = DIFF_HEAD_DIM
    q = apply_rope_2(q.reshape(b, s, 2 * DIFF_HEADS, hd), positions, DIFF_ROT).reshape(b, s, DIFF_HEADS, 2, hd)
    k = apply_rope_2(k.reshape(b, s, 2 * DIFF_HEADS, hd), positions, DIFF_ROT).reshape(b, s, DIFF_HEADS, 2, hd)
    v = v.reshape(b, s, DIFF_HEADS, 2 * hd)
    q1, q2 = q[..., 0, :], q[..., 1, :]
    k1t = k[..., 0, :].transpose(0, 2, 1, 3)
    k2t = k[..., 1, :].transpose(0, 2, 1, 3)
    vt = v.transpose(0, 2, 1, 3)
    lam_init = 0.8 - 0.6 * math.exp(-0.3 * (layer_idx - 1))
    f32 = jnp.float32
    lam = (jnp.exp(jnp.sum(lam_q1.astype(f32) * lam_k1.astype(f32)))
           - jnp.exp(jnp.sum(lam_q2.astype(f32) * lam_k2.astype(f32))) + lam_init)
    scale = hd ** -0.5

    def block(args):
        q1b, q2b, i = args
        a = causal_probs(q1b, k1t, i, scale) - lam * causal_probs(q2b, k2t, i, scale)
        return jnp.einsum('bhqk,bhkd->bhqd', a.astype(vt.dtype), vt)

    out = from_blocks(lax.map(block, (to_blocks(q1), to_blocks(q2), jnp.arange(s // Q_BLOCK))))
    out = rms_norm_2(out, subln) * (1.0 - lam_init)
    return out.reshape(b, s, DIFF_WIDTH)

def hybrid_layer(x, positions, layer_idx,
                 ffn1_norm, ffn1_w_gate, ffn1_w_up, ffn1_w_down,
                 mix_norm, w_in,
                 mla_q_norm, mla_w_uq, mla_kv_norm, mla_w_ukv,
                 diff_lam_q1, diff_lam_k1, diff_lam_q2, diff_lam_k2, diff_subln,
                 w_proj_mla, w_proj_diff, w_out,
                 ffn2_norm, ffn2_w_gate, ffn2_w_up, ffn2_w_down):
    x = x + 0.5 * swiglu(rms_norm_2(x, ffn1_norm), ffn1_w_gate, ffn1_w_up, ffn1_w_down)

    h = rms_norm_2(x, mix_norm)
    z = h @ w_in
    cuts = []
    acc = 0
    for n in IN_SPLITS[:-1]:
        acc += n
        cuts.append(acc)
    c_q, c_kv, k_rope_raw, dq, dk, dv, gate_mla, gate_diff = jnp.split(z, cuts, axis=-1)

    y_mla = mla_branch(c_q, c_kv, k_rope_raw, positions, mla_q_norm, mla_w_uq, mla_kv_norm, mla_w_ukv)
    y_diff = diff_branch(dq, dk, dv, positions, diff_lam_q1, diff_lam_k1, diff_lam_q2, diff_lam_k2,
                         diff_subln, layer_idx)

    merged = (jax.nn.sigmoid(gate_mla) * (y_mla @ w_proj_mla)
              + jax.nn.sigmoid(gate_diff) * (y_diff @ w_proj_diff))
    x = x + merged @ w_out

    x = x + 0.5 * swiglu(rms_norm_2(x, ffn2_norm), ffn2_w_gate, ffn2_w_up, ffn2_w_down)
    return x

def second_inputs(seed: int = 0) -> dict:
    key = jax.random.key(seed)
    ks = jax.random.split(key, 32)
    f32 = jnp.float32

    def w(k, fan_in, fan_out):
        return jax.random.normal(k, (DEPTH_2, fan_in, fan_out), f32) * fan_in ** -0.5

    def gain(k, n):
        return 1.0 + 0.01 * jax.random.normal(k, (DEPTH_2, n), f32)

    x = jax.random.normal(ks[0], (BATCH, SEQ, D_MODEL), f32)
    offsets = jax.random.randint(ks[1], (BATCH, 1), 0, 1024, dtype=jnp.int32)
    positions = jnp.arange(SEQ, dtype=jnp.int32)[None, :] + offsets
    return {
        "x": x,
        "positions": positions,
        "ffn1_norm": gain(ks[2], D_MODEL),
        "ffn1_w_gate": w(ks[3], D_MODEL, D_FF),
        "ffn1_w_up": w(ks[4], D_MODEL, D_FF),
        "ffn1_w_down": w(ks[5], D_FF, D_MODEL),
        "mix_norm": gain(ks[6], D_MODEL),
        "w_in": w(ks[7], D_MODEL, IN_COLS),
        "mla_q_norm": gain(ks[8], MLA_Q_RANK),
        "mla_w_uq": w(ks[9], MLA_Q_RANK, MLA_HEADS * (MLA_NOPE + MLA_ROPE)),
        "mla_kv_norm": gain(ks[10], MLA_KV_RANK),
        "mla_w_ukv": w(ks[11], MLA_KV_RANK, MLA_HEADS * (MLA_NOPE + MLA_V)),
        "diff_lam_q1": 0.1 * jax.random.normal(ks[12], (DEPTH_2, DIFF_HEAD_DIM), f32),
        "diff_lam_k1": 0.1 * jax.random.normal(ks[13], (DEPTH_2, DIFF_HEAD_DIM), f32),
        "diff_lam_q2": 0.1 * jax.random.normal(ks[14], (DEPTH_2, DIFF_HEAD_DIM), f32),
        "diff_lam_k2": 0.1 * jax.random.normal(ks[15], (DEPTH_2, DIFF_HEAD_DIM), f32),
        "diff_subln": gain(ks[16], 2 * DIFF_HEAD_DIM),
        "w_proj_mla": w(ks[17], MLA_WIDTH, D_MODEL),
        "w_proj_diff": w(ks[18], DIFF_WIDTH, D_MODEL),
        "w_out": w(ks[19], D_MODEL, D_MODEL),
        "ffn2_norm": gain(ks[20], D_MODEL),
        "ffn2_w_gate": w(ks[21], D_MODEL, D_FF),
        "ffn2_w_up": w(ks[22], D_MODEL, D_FF),
        "ffn2_w_down": w(ks[23], D_FF, D_MODEL),
        "final_norm": 1.0 + 0.01 * jax.random.normal(ks[24], (D_MODEL,), f32),
    }

def second_block(x, positions,
              ffn1_norm, ffn1_w_gate, ffn1_w_up, ffn1_w_down,
              mix_norm, w_in,
              mla_q_norm, mla_w_uq, mla_kv_norm, mla_w_ukv,
              diff_lam_q1, diff_lam_k1, diff_lam_q2, diff_lam_k2, diff_subln,
              w_proj_mla, w_proj_diff, w_out,
              ffn2_norm, ffn2_w_gate, ffn2_w_up, ffn2_w_down,
              final_norm):
    for l in range(DEPTH_2):
        x = hybrid_layer(
            x, positions, l + 1,
            ffn1_norm[l], ffn1_w_gate[l], ffn1_w_up[l], ffn1_w_down[l],
            mix_norm[l], w_in[l],
            mla_q_norm[l], mla_w_uq[l], mla_kv_norm[l], mla_w_ukv[l],
            diff_lam_q1[l], diff_lam_k1[l], diff_lam_q2[l], diff_lam_k2[l], diff_subln[l],
            w_proj_mla[l], w_proj_diff[l], w_out[l],
            ffn2_norm[l], ffn2_w_gate[l], ffn2_w_up[l], ffn2_w_down[l])
    return rms_norm_2(x, final_norm)


_first_inputs = second_inputs


def second_inputs(seed=0):
    import zlib

    import numpy as np

    out = dict(_first_inputs(seed))
    spreads = {}
    factors = {'ffn1_norm': 8.0,
     'mix_norm': 7.404,
     'mla_q_norm': 24.101,
     'mla_kv_norm': 25.779,
     'diff_lam_q2': 64.0,
     'diff_subln': 64.0,
     'ffn2_norm': 48.128,
     'final_norm': 32.499,
     'diff_lam_q1': 5.482}
    for name, (base, spread) in spreads.items():
        noise = np.random.default_rng([zlib.crc32(name.encode()), seed]).standard_normal(out[name].shape)
        drawn = base * np.exp(spread * noise) if base else spread * noise
        out[name] = __import__('jax').numpy.asarray(drawn.astype(out[name].dtype))
    for name, factor in factors.items():
        out[name] = (out[name] * factor).astype(out[name].dtype)
    return out


_narrow_inputs = second_inputs


def second_inputs(seed=0):

    out = dict(_narrow_inputs(seed))
    wider = {'diff_lam_q2': 12.0, 'diff_subln': 5.72, 'ffn2_norm': 4.72, 'final_norm': 6.41}
    for name, times in wider.items():
        mean = out[name].mean()
        out[name] = (mean + times * (out[name] - mean)).astype(out[name].dtype)
    return out


def setup_inputs(seed=0):
    out = dict(first_inputs(seed))
    for name, value in second_inputs(seed + 1).items():
        if name != "x":
            out[name + "_2"] = value
    return out


def reference(
    x, c, ctx, c_ctx, ada_w, ada_b, norm1_g, norm2_g, w_in, conv_a_w, conv_b_w, conv_b_b,
    conv_ln_g, conv_ln_b, sink, q_norm_g, k_norm_g, w_out, router_w, w_gate, w_up, w_down,
    final_g, positions_2, ffn1_norm_2, ffn1_w_gate_2, ffn1_w_up_2, ffn1_w_down_2, mix_norm_2,
    w_in_2, mla_q_norm_2, mla_w_uq_2, mla_kv_norm_2, mla_w_ukv_2, diff_lam_q1_2, diff_lam_k1_2,
    diff_lam_q2_2, diff_lam_k2_2, diff_subln_2, w_proj_mla_2, w_proj_diff_2, w_out_2,
    ffn2_norm_2, ffn2_w_gate_2, ffn2_w_up_2, ffn2_w_down_2, final_norm_2,
):
    x = first_block(
        x, c, ctx, c_ctx, ada_w, ada_b, norm1_g, norm2_g, w_in, conv_a_w, conv_b_w, conv_b_b,
        conv_ln_g, conv_ln_b, sink, q_norm_g, k_norm_g, w_out, router_w, w_gate, w_up, w_down,
        final_g,
    )
    return second_block(
        x, positions_2, ffn1_norm_2, ffn1_w_gate_2, ffn1_w_up_2, ffn1_w_down_2, mix_norm_2,
        w_in_2, mla_q_norm_2, mla_w_uq_2, mla_kv_norm_2, mla_w_ukv_2, diff_lam_q1_2,
        diff_lam_k1_2, diff_lam_q2_2, diff_lam_k2_2, diff_subln_2, w_proj_mla_2, w_proj_diff_2,
        w_out_2, ffn2_norm_2, ffn2_w_gate_2, ffn2_w_up_2, ffn2_w_down_2, final_norm_2,
    )


_drawn_inputs = setup_inputs


def setup_inputs(seed=0):
    import zlib

    import numpy as np

    out = dict(_drawn_inputs(seed))
    spreads = {}
    factors = {'sink': 8.0,
     'q_norm_g': 8.0,
     'k_norm_g': 8.0,
     'diff_lam_q2_2': 7.208,
     'diff_lam_k2_2': 7.208}
    for name, (base, spread) in spreads.items():
        noise = np.random.default_rng([zlib.crc32(name.encode()), seed]).standard_normal(out[name].shape)
        drawn = base * np.exp(spread * noise) if base else spread * noise
        out[name] = __import__('jax').numpy.asarray(drawn.astype(out[name].dtype))
    for name, factor in factors.items():
        out[name] = (out[name] * factor).astype(out[name].dtype)
    return out
```

```python
from contextlib import ExitStack

import numpy as np
import concourse.bass as bass
from concourse import mybir

F32 = mybir.dt.float32
U32 = mybir.dt.uint32
I32 = mybir.dt.int32
BF16 = mybir.dt.bfloat16
ALU = mybir.AluOpType
ACT = mybir.ActivationFunctionType
AX = mybir.AxisListType

P = 128
D = 1024
KD = D // P
SEQ = 512
CTX = 256
ST = SEQ // P
CT = CTX // P
NTOK = SEQ + CTX
LAYERS = 2
HD = 64
HEADS = 4
EPS = 1e-6
GRID_W = 64
EXPERTS = 16
CAP_X = 2 * SEQ // EXPERTS
CAP_C = 2 * CTX // EXPERTS
TAPS_A = 3
TAPS_B = 31
CONV_COLS = 5 * (D // 4)
BANKS = 8
BANK = 512
SLOTS = 4
SLOT = KD * 512
MASKED = -1.0e30

D_FF = 2816
F_CHUNKS = D_FF // P
Q_RANK, KV_RANK = 256, 128
L_HEADS, NOPE, ROT, L_V = 8, 64, 32, 64
L_QK = NOPE + ROT
LATENT = Q_RANK + KV_RANK + ROT
D_HEADS, D_ROT = 4, 16
D_W = D_HEADS * 2 * HD
GATES = LATENT + 3 * D_W
THETA = 500000.0
ANGLES = ROT // 2 + D_ROT // 2
LAM_INIT = 0.2
ROUND = 12582912.0


class Stage:

    def __init__(self, name, layer=0, bank_uses=(), signals=None, units=(), repeat_units=0, **facts):
        self.name, self.layer, self.facts = name, layer, facts
        self.signals = dict(signals or {})
        for b, n in enumerate(bank_uses):
            if n:
                self.signals[f"bank{b}"] = n
        self.units = list(units)
        self.repeat_units = repeat_units
        self.base = {}
        self.number = 0

    def at(self, signal, n):
        return self.base.get(signal, 0) + n


def place_stages(stages):
    total = {}
    unit = 0
    for number, stage in enumerate(stages):
        stage.number = number
        stage.base = dict(total)
        stage.first_unit = unit
        unit += len(stage.units) + stage.repeat_units
        for name, n in stage.signals.items():
            total[name] = total.get(name, 0) + n
    return total


def heads_of(layer):
    tiles = ST + CT if layer == 0 else ST
    return [(qt, kind, h) for qt in range(tiles) for kind in range(2) for h in range(HEADS)]


def key_tiles(qt, kind):
    context = list(range(ST, ST + CT))
    if qt >= ST:
        return context
    if kind:
        return list(range(ST)) + context
    return list(range(max(0, qt - 1), min(ST, qt + 2))) + context


class Steps:

    def __init__(self, eng, sem):
        self.eng, self.sem, self.n, self.turns = eng, sem, 0, 0

    def __call__(self, ins):
        ins.then_inc(self.sem, 1)
        self.n += 1
        self.eng.wait_ge(self.sem, self.turns + self.n)

    def later(self, ins):
        ins.then_inc(self.sem, 1)
        self.n += 1

    def wait_for(self, behind):
        self.eng.wait_ge(self.sem, self.turns + self.n - behind)

    def begin_loop(self, turn, per_turn):
        self.turns, self.start, self.per_turn = turn * per_turn, self.n, per_turn

    def end_loop(self, turns):
        assert self.n - self.start == self.per_turn, (self.n - self.start, self.per_turn)
        self.n, self.turns = self.start + self.per_turn * turns, 0


def block_one_stages(a):
    stages = []

    def weight_unit(source, cols):
        lo, hi = cols

        def load(slot):
            out = slot.rearrange("p (k n) -> p k n", k=KD)[:, :, 0:hi - lo]
            return out, source[:, lo:hi].rearrange("(k p) n -> p k n", p=P)

        return load

    for l in range(LAYERS):
        tiles = ST + CT if l == 0 else ST
        all_tiles = ST + CT
        n_ada = 6 * D // 512
        stages.append(Stage(
            "ada", l, bank_uses=[(n_ada - b + BANKS - 1) // BANKS for b in range(BANKS)],
            signals=dict(rows_loaded=32, mods_rows=1, mods_stored=16),
            units=[(weight_unit(a["ada_w"][l], (512 * n, 512 * n + 512)), (n % BANKS, n // BANKS))
                   for n in range(n_ada)]))
        for first, last, row in ((0, ST, 0), (ST, ST + CT, 1)):
            stages.append(norm_stage("norm", l, range(first, last), row=row, scale=1, shift=0, store=False))
        n_chunks = CONV_COLS // P
        parts = 2 if l == 0 else 1
        groups = n_chunks * parts
        spans = [(0, 512), (512, 1024), (1024, CONV_COLS)]
        units = []
        for lo, hi in spans:
            g = (hi // P) * parts - 1
            units.append((weight_unit(a["w_in"][l], (lo, hi)), (g % BANKS, g // BANKS)))
        stages.append(Stage("conv_in", l, bank_uses=[(groups - b + BANKS - 1) // BANKS for b in range(BANKS)],
                            units=units, parts=parts))
        last_pair = ((all_tiles - 1) % 3 * 2, (all_tiles - 1) // 3)
        stages.append(Stage(
            "qkv", l, bank_uses=[2, 0, 2, 0, 2, 0, all_tiles, all_tiles],
            signals=dict(head_sums=all_tiles, head_roots=all_tiles, qk_ready=all_tiles),
            units=[(weight_unit(a["w_in"][l], (CONV_COLS + 512 * j, CONV_COLS + 512 * j + 512)), last_pair)
                   for j in range(2)]))
        units = heads_of(l)
        n_units = len(units)
        groups = n_units // HEADS
        wide = [len(key_tiles(qt, kind)) > 4 for qt, kind, _ in units]
        sinks = sum(kind == 0 for _, kind, _ in units)
        stages.append(Stage(
            "attend", l, bank_uses=[n_units // 2, 0, n_units // 2, 0, n_units, sum(wide), groups, groups],
            signals=dict(neg_max=n_units, sink_exp=sinks),
            wide=wide))
        stages.append(Stage("conv_out", l, bank_uses=[2], signals=dict(centered=1, squared=2, normed=2)))
        uses = [0] * BANKS
        for i in range(tiles):
            uses[2 * (i % 4)] += 1
        last_pair = (2 * ((tiles - 1) % 4), (tiles - 1) // 4)
        stages.append(Stage(
            "w_out", l, bank_uses=uses, signals=dict(rows_loaded=32),
            units=[(weight_unit(a["w_out"][l], (512 * j, 512 * j + 512)), last_pair) for j in range(2)], tiles=tiles))
        stages.append(norm_stage("norm", l, range(0, ST), row=0, scale=4, shift=3, store=True))
        if l == 0:
            stages.append(norm_stage("norm", l, range(ST, ST + CT), row=1, scale=4, shift=3, store=True))
        stages.append(Stage("route", l, bank_uses=[1, 1, 1 if l == 0 else 0, 1],
                            signals=dict(logit_exp=1, affinity=1, ranked=1), tiles=tiles))
        uses = [EXPERTS + 1, EXPERTS + 1] + [EXPERTS] * 6
        stages.append(Stage("experts", l, bank_uses=uses, repeat_units=6 * EXPERTS,
                            signals=dict(gathered=16 * (EXPERTS + 1), scattered=16 * EXPERTS), tiles=tiles))
        stages.append(Stage("combine", l, signals=dict(rows_loaded=32, moe_rows0=16 * (tiles // 2), moe_rows1=16 * (tiles // 2), added=tiles), tiles=tiles))
    return stages


def block_two_stages(a):
    def unit(source, rows, cols):
        (r0, r1), (c0, c1) = rows, cols
        k = (r1 - r0) // P

        def load(slot):
            out = slot[:, 0:k * (c1 - c0)].rearrange("p (k n) -> p k n", k=k)
            return out, source[r0:r1, c0:c1].rearrange("(k p) n -> p k n", p=P)

        return load

    def gain_norm(gain, turned=True):
        st = norm_stage("norm" if turned else "norm_rows", 0, range(ST), row=0, scale=0, shift=None, store=False)
        st.facts["gain"] = gain
        if not turned:
            st.signals = dict(rows_loaded=16, mean_root=ST)
        return st

    def ffn(which):
        units = []
        for u in range((F_CHUNKS + 3) // 4):
            last = min(F_CHUNKS, 4 * u + 4) - 1
            for n, name in enumerate(("gate", "up")):
                units.append((unit(a[f"ffn{which}_w_{name}_2"], (0, D), (512 * u, 128 * (last + 1))),
                              (2 * (last % 4) + n, last // 4)))
        up = Stage("ffn_up", which, bank_uses=[len(range(b // 2, F_CHUNKS, 4)) for b in range(BANKS)], units=units)
        units = []
        for half in range(2):
            for n in range(3):
                k0, k1 = 8 * n, min(F_CHUNKS, 8 * n + 8)
                reader = (4 * half + ST - 1, 0) if n == 2 else ("down_read", 2 * half + n)
                units.append((unit(a[f"ffn{which}_w_down_2"], (k0 * P, k1 * P), (512 * half, 512 * half + 512)), reader))
        down = Stage("ffn_down", which, bank_uses=[1] * BANKS, signals=dict(down_read=4), units=units)
        return [up, down]

    w_in = a["w_in_2"]
    merge_units = []
    for half in range(2):
        c = 4 * half + 3
        cols = (512 * half, 512 * half + 512)
        merge_units.append((unit(a["w_proj_2"], (0, D), cols), (4 * (c % 2) + 3, c // 2)))
        for n, start in enumerate((GATES, GATES + D)):
            merge_units.append((unit(w_in, (0, D), (start + cols[0], start + cols[1])), (4 * (c % 2) + 2 * n, c // 2)))
    groups = 4 * L_HEADS // 2 + 4 * D_HEADS
    n_units = 2 * groups
    last_pair = (2 * (ST - 1), 0)
    return [
        gain_norm("final_g", turned=False),
        Stage("angles", signals=dict(tables_loaded=16 * 5, angles=1, sines=1, lam_sum=1, lam_exp=1)),
        gain_norm("ffn1_norm_2"), *ffn(1),
        gain_norm("mix_norm_2"),
        Stage("latent_in", bank_uses=[ST // 2, ST // 2, ST // 2, ST // 2], signals=dict(latent_root=2 * ST, latent_sum=2 * ST, latent=ST),
              units=[(unit(w_in, (0, D), (0, LATENT)), ((ST - 1) % 2, (ST - 1) // 2))]),
        Stage("latent_qk", bank_uses=[ST, 0, ST, 0, ST, ST, ST, ST], signals=dict(q_rows=ST, k_rows=ST),
              units=[(unit(a["mla_w_uq_2"], (0, Q_RANK), (0, L_HEADS * L_QK)), (0, ST - 1)),
                     (unit(a["mla_w_ukv_2"], (0, KV_RANK), (0, L_HEADS * (NOPE + L_V))), (2, ST - 1))]),
        Stage("diff_in", bank_uses=[ST, 0, ST, 0, ST, ST], signals=dict(qk_rows=ST),
              units=[(unit(w_in, (0, D), (LATENT + D_W * j, LATENT + D_W * j + D_W)), (0 if j < 2 else 2, ST - 1))
                     for j in range(3)]),
        Stage("attend_two", bank_uses=[n_units // 2] * 4 + [groups // 2] * 4,
              signals=dict(neg_max=n_units, y_sum=4 * D_HEADS, y_root=4 * D_HEADS, y_rows=groups)),
        Stage("merge", bank_uses=[KD // 2] * BANKS, signals=dict(merged=KD), units=merge_units),
        Stage("project", bank_uses=[1, 0, 1, 0, 1, 0, 1, 0],
              units=[(unit(a["w_out_2"], (0, D), (512 * j, 512 * j + 512)), last_pair) for j in range(2)]),
        gain_norm("ffn2_norm_2"), *ffn(2),
        gain_norm("final_norm_2", turned=False),
        Stage("store", signals=dict(stored=16)),
    ]


def units_two():
    latent = [(0, qt, 2 * pair + s, s) for qt in range(ST) for pair in range(L_HEADS // 2) for s in range(2)]
    diff = [(1, qt, h, s) for qt in range(ST) for h in range(D_HEADS) for s in range(2)]
    return latent + diff


def norm_stage(name, layer, tiles, row, scale, shift, store):
    tiles = list(tiles)
    uses = [0] * BANKS
    for i in range(len(tiles)):
        uses[2 * (i % 4)] += 1
        uses[2 * (i % 4) + 1] += 1
    signals = dict(rows_loaded=32 if shift is not None else 16, mean_root=len(tiles), h_ready=len(tiles))
    if store:
        for q in range(2):
            signals[f"h_stored{q}"] = 16 * len(tiles[q::2])
    return Stage(name, layer, bank_uses=uses, signals=signals, tiles=tiles, row=row, scale=scale, shift=shift, store=store)


def two_blocks_kernel(nc, a, out, stages):
    with ExitStack() as ctx:
        def sb(name, shape, dtype=F32):
            return ctx.enter_context(nc.sbuf_tensor(name, shape, dtype))

        class Semaphores(dict):

            def __missing__(self, name):
                self[name] = ctx.enter_context(nc.semaphore(name))
                return self[name]

        sem = Semaphores()

        mods_rows = [nc.dram_tensor(f"mods_rows{l}", [2, 6 * D], F32).ap() for l in range(LAYERS)]
        h_rows = [nc.dram_tensor(f"h_rows{l}", [NTOK, D], F32).ap() for l in range(LAYERS)]
        moe_rows = [nc.dram_tensor(f"moe_rows{l}", [NTOK, D], F32).ap() for l in range(LAYERS)]

        bank = ctx.enter_context(nc.psum_tensor("bank", [P, BANKS, BANK], F32))

        slots = sb("slots", [P, SLOTS, SLOT])
        X = sb("X", [P, ST + CT, D])
        HT = sb("HT", [P, KD, NTOK])
        ident = sb("ident", [P, P])
        band = sb("band", [P, 2, P])
        mean_of = sb("mean_of", [P, P])
        rope_cos = sb("rope_cos", [P, ST, HD])
        rope_sin = sb("rope_sin", [P, ST, HD])
        head_gain = sb("head_gain", [P, LAYERS, 6, HD])
        conv_a_w = sb("conv_a_w", [P, LAYERS, 2, TAPS_A])
        conv_b_w = sb("conv_b_w", [P, LAYERS, 2, TAPS_B])
        conv_vec = sb("conv_vec", [P, 3, LAYERS, 2])
        sink = sb("sink", [P, LAYERS, HEADS])
        router = sb("router", [P, LAYERS, KD, EXPERTS])
        silu_c = sb("silu_c", [P, KD, 2])
        eps = sb("eps", [P, 1])
        junk = sb("junk", [P, D], BF16)
        small = sb("small", [P, 96])
        done_mark = sb("done_mark", [P, 4])
        arena = sb("arena", [P, 20800])

        at = [0]

        def carve(*shape):
            n = int(np.prod(shape))
            v = arena[:, at[0]:at[0] + n]
            at[0] += n
            assert at[0] <= arena.shape[1], at[0]
            if len(shape) == 2:
                return v.rearrange("p (a b) -> p a b", a=shape[0])
            if len(shape) == 3:
                return v.rearrange("p (a b c) -> p a b c", a=shape[0], b=shape[1])
            return v

        PAD_A, PAD_B = TAPS_A // 2, TAPS_B // 2
        LEN_A, LEN_B = NTOK + 4 * PAD_A, NTOK + 4 * PAD_B
        conv_a_in = carve(2, LEN_A)
        conv_b_in = carve(2, LEN_B)
        conv_a_gate = carve(2, NTOK)
        V = carve(ST + CT, 2 * P)
        h_tok = carve(2, D)
        mod = carve(2, D)
        probs = carve(2, NTOK)
        probsT = carve(2, NTOK)
        at_moe = at[0]
        QKT = carve(6, NTOK)
        ada_bias = arena[:, at_moe - 6 * D:at_moe]
        norm_gain = QKT.rearrange("p a b -> p (a b)")[:, 0:2 * D].rearrange("p (a b) -> p a b", a=2)
        sig = h_tok.rearrange("p a b -> p (a b)")[:, 0:2 * NTOK].rearrange("p (a b) -> p a b", a=2)
        z_tok = sig
        tap_out = h_tok.rearrange("p a b -> p (a b)")[:, 0:3 * SEQ].rearrange("p (a b) -> p a b", a=3)
        qk_tok = mod.rearrange("p a b -> p (a b)")[:, 0:2 * NTOK].rearrange("p (a b) -> p a b", a=2)
        rope_a, rope_b = probs[:, 0, :], probs[:, 1, :]
        squares = probsT[:, 0, 0:6 * HD]
        y_tok = mod.rearrange("p a b -> p (a b)")[:, 0:4 * P].rearrange("p (a b) -> p a b", a=2)
        u_sq = sig
        u_rstd = mod.rearrange("p a b -> p (a b)")[:, 0:NTOK]
        at[0] = at_moe
        xs = carve(D)
        NS = CAP_X + CAP_C
        xsT = carve(KD, NS)
        gateT = carve(2, 4 * NS)
        actT = carve(KD, NS)
        y_rows = carve(D)
        aff = carve(ST + CT, EXPERTS)
        affT = carve(NTOK)
        top = carve(NS)
        top_at = carve(NS)
        index_t = carve(EXPERTS + 1).bitcast(U32)
        gate_t = carve(EXPERTS)
        now = carve(4)


        at[0] = 0
        q_latT = carve(L_HEADS, SEQ)
        k_latT = carve(L_HEADS, SEQ)
        v_lat = carve(ST, L_HEADS * L_V)
        q_diffT = carve(D_HEADS, SEQ)
        k_diffT = carve(D_HEADS, SEQ)
        v_diff = carve(ST, D_HEADS * 2 * HD)
        at_y = at[0]
        yT = carve(KD, SEQ)
        y_rows2 = carve(2, P)
        at[0] = at_y
        q_rows = carve(2, L_HEADS * L_QK)
        k_rows = carve(2, L_HEADS * L_QK)
        z_lat = q_rows[:, :, 0:LATENT]
        turn_a, turn_b = carve(L_HEADS * ROT), carve(L_HEADS * ROT)
        at[0] = at_y
        qk_diff = carve(2, 2 * D_W)
        at[0] = 0
        ffnT = carve(F_CHUNKS, SEQ)
        ffn_gate = carve(2, SEQ)
        at[0] = 0
        mergedT = carve(KD, SEQ)
        merge_gate = carve(2, 2 * SEQ)
        spare = X[:, ST:ST + CT, :].rearrange("p t d -> p (t d)")
        latentT = spare[:, 0:3 * SEQ].rearrange("p (k n) -> p k n", k=3)
        rot_k = spare[:, 3 * SEQ:3 * SEQ + ST * ROT].rearrange("p (t n) -> p t n", t=ST)
        probs2 = spare[:, 0:2 * SEQ].rearrange("p (a n) -> p a n", a=2)
        probs2T = spare[:, 2 * SEQ:4 * SEQ].rearrange("p (a n) -> p a n", a=2)
        cos2 = sb("cos2", [P, ST, ANGLES])
        sin2 = sb("sin2", [P, ST, ANGLES])
        lam = sb("lam", [P, 4])
        latent_gain = sb("latent_gain", [P, 3])
        subln = sb("subln", [P, 2 * HD])
        squares2 = sb("squares2", [P, 2 * HD])
        positions = h_tok[:, 0, 0:ST].bitcast(I32)
        pos_f = h_tok[:, 0, 8:8 + ST]
        freq = h_tok[:, 0, 16:16 + ANGLES]
        angle = h_tok[:, 0, 128:128 + ST * ANGLES].rearrange("p (t n) -> p t n", t=ST)
        whole = h_tok[:, 0, 256:256 + ST * ANGLES].rearrange("p (t n) -> p t n", t=ST)
        lam_in = h_tok[:, 0, 512:512 + 4 * HD].rearrange("p (a n) -> p a n", a=4)
        def at_bank(stage, b, use):
            return stage.at(f"bank{b}", use + 1)

        def pe_may_fill(pe, stage, b, use):
            if isinstance(use, int) and stage.at(f"bank{b}", use) == 0:
                return
            pe.wait_ge(sem[f"free{b}"], stage.at(f"bank{b}", use))

        def slot_of(unit):
            return slots[:, unit % SLOTS, :]

        def pe_wait_unit(pe, unit, turn=0, per_turn=0):
            pe.wait_ge(sem[f"loaded{unit % SLOTS}"], turn * (16 * per_turn) + 16 * (unit // SLOTS + 1))

        def enter(eng, stage):
            if stage.number:
                for other in ("scalar", "vector", "gpsimd"):
                    eng.wait_ge(sem[f"{other}_finished"], stage.number)

        def tile_cols(t):
            return slice(t * P, t * P + P)

        block = ctx.enter_context(nc.Block())

        @block.sync
        def _(sp):
            readers = []

            def load(stage, unit, out_in, turn=0):
                out_, in_ = out_in
                if unit >= SLOTS:
                    name, value = readers[unit - SLOTS]
                    sp.wait_ge(name, value)
                sp.dma_start(out_, in_).then_inc(sem[f"loaded{unit % SLOTS}"], 16)

            for stage in stages:
                for j, (make, (b, use)) in enumerate(stage.units):
                    unit = stage.first_unit + j
                    load(stage, unit, make(slot_of(unit)))
                    if isinstance(b, int):
                        readers.append((sem[f"full{b}"], at_bank(stage, b, use)))
                    else:
                        readers.append((sem[b], stage.at(b, use + 1)))
                if stage.name != "experts":
                    continue
                l, first = stage.layer, stage.first_unit
                mats = (a["w_gate"], a["w_up"], a["w_gate"], a["w_up"], a["w_down"], a["w_down"])

                def part(expert, j):
                    half = j // 2 if j < 4 else j - 4
                    source = mats[j][l]
                    if isinstance(expert, int):
                        source = source[expert]
                    else:
                        source = source[bass.ds(expert, 1), :, :].rearrange("a d f -> (a d) f")
                    slot = slot_of(first + 6 * (0 if not isinstance(expert, int) else expert) + j)
                    return source[:, 512 * half:512 * half + 512].rearrange("(k p) n -> p k n", p=P)

                def reader(e, j):
                    return (2 + j if j < 4 else 6 + j - 4), e

                for u in range(SLOTS):
                    unit = first + u
                    load(stage, unit, (slot_of(unit).rearrange("p (k n) -> p k n", k=KD), part(0, u)))
                    readers.append(None)

                def rest_of_pair(pair, last):
                    for u in range(SLOTS, 12 if last else 12 + SLOTS):
                        b, e = reader((u - SLOTS) // 6, (u - SLOTS) % 6)
                        sp.wait_ge(sem[f"full{b}"], at_bank(stage, b, 2 * pair + e))
                        unit = first + u
                        sp.dma_start(slot_of(unit).rearrange("p (k n) -> p k n", k=KD),
                                     part(2 * pair + u // 6, u % 6)).then_inc(sem[f"loaded{unit % SLOTS}"], 16)

                with sp.Fori(0, EXPERTS // 2 - 1) as pair:
                    rest_of_pair(pair, False)
                rest_of_pair(EXPERTS // 2 - 1, True)
                del readers[-SLOTS:]
                for e in range(EXPERTS):
                    for j in range(6):
                        b, use = reader(e, j)
                        readers.append((sem[f"full{b}"], at_bank(stage, b, use)))

        @block.tensor
        def _(pe):
            def product(out_, pairs, signal=None):
                for n, (lhsT, rhs) in enumerate(pairs):
                    mm = pe.matmul(out_, lhsT, rhs, start=(n == 0), stop=(n == len(pairs) - 1))
                if signal is not None:
                    mm.then_inc(signal, 1)

            def ada(st):
                pe.wait_ge(sem["silu_c"], 1)
                for n in range(6 * D // 512):
                    unit, b = st.first_unit + n, n % BANKS
                    pe_wait_unit(pe, unit)
                    pe_may_fill(pe, st, b, n // BANKS)
                    w = slot_of(unit).rearrange("p (k n) -> p k n", k=KD)
                    product(bank[0:2, b, :], [(silu_c[:, k, :], w[:, k, :]) for k in range(KD)], sem[f"full{b}"])

            def norm(st):
                for i, t in enumerate(st.facts["tiles"]):
                    pe.wait_ge(sem["h_ready"], st.at("h_ready", i + 1))
                    for half in range(2):
                        b = 2 * (i % 4) + half
                        pe_may_fill(pe, st, b, i // 4)
                        for c in range(4):
                            k = 4 * half + c
                            mm = pe.transpose(bank[:, b, tile_cols(c)], h_tok[:, i % 2, tile_cols(k)], ident[:, :])
                        mm.then_inc(sem[f"full{b}"], 1)

            def conv_in(st):
                parts = st.facts["parts"]
                for c in range(CONV_COLS // P):
                    unit = st.first_unit + c // 4
                    pe_wait_unit(pe, unit)
                    w = slot_of(unit).rearrange("p (k n) -> p k n", k=KD)[:, :, tile_cols(c % 4)]
                    for part in range(parts):
                        g = c * parts + part
                        b = g % BANKS
                        lo, hi = (0, SEQ) if part == 0 else (SEQ, NTOK)
                        pe_may_fill(pe, st, b, g // BANKS)
                        product(bank[:, b, 0:hi - lo], [(w[:, k, :], HT[:, k, lo:hi]) for k in range(KD)],
                                sem[f"full{b}"])

            def qkv(st):
                def turned(i):
                    pe.wait_ge(sem["qk_ready"], st.at("qk_ready", i + 1))
                    keys_only = st.layer == 1 and i >= ST
                    for kind in range(2):
                        pe_may_fill(pe, st, 6 + kind, i)
                        for c in ([2] if keys_only else range(3)):
                            mm = pe.transpose(bank[:, 6 + kind, tile_cols(c)],
                                              qk_tok[:, i % 2, tile_cols(3 * kind + c)], ident[:, :])
                        mm.then_inc(sem[f"full{6 + kind}"], 1)

                for i in range(ST + CT):
                    b, use = 2 * (i % 3), i // 3
                    lo = 256 if st.layer == 1 and i >= ST else 0
                    pe_may_fill(pe, st, b, use)
                    for j in range(2):
                        pe_wait_unit(pe, st.first_unit + j)
                        w = slot_of(st.first_unit + j).rearrange("p (k n) -> p k n", k=KD)
                        product(bank[:, b + j, lo:512], [(HT[:, k, tile_cols(i)], w[:, k, lo:512]) for k in range(KD)],
                                sem[f"full{b}"] if j else None)
                    if i:
                        turned(i - 1)
                turned(ST + CT - 1)

            def attend(st):
                units = heads_of(st.layer)
                wide = st.facts["wide"]

                def scores(i):
                    qt, kind, h = units[i]
                    b, g = 2 * (i % 2), h // 2
                    rows = slice(HD * g, HD * g + HD)
                    q = QKT[rows, 3 * kind + h % 2, tile_cols(qt)]
                    kT = QKT[rows, 3 * kind + 2, :]
                    pe_may_fill(pe, st, b, i // 2)
                    local = key_tiles(qt, kind)[:-CT]
                    if kind:
                        if local:
                            pe.matmul(bank[:, b, :], q, kT[:, 0:SEQ], start=True, stop=True)
                    else:
                        for n, t in enumerate(local):
                            scores_of_tile = bank[:, b, BANK - (len(local) - n) * P:][:, 0:P]
                            pe.matmul(scores_of_tile, q, kT[:, tile_cols(t)], start=True, stop=(t == qt))
                            if t != qt:
                                pe.matmul(scores_of_tile, ident[:, :], band[:, 0 if t < qt else 1, :], start=False, stop=True)
                    pe.matmul(bank[:, b + 1, 0:CTX], q, kT[:, SEQ:NTOK], start=True, stop=True).then_inc(sem[f"full{b}"], 1)

                def turn_probs(i):
                    n = len(key_tiles(*units[i][:2]))
                    b = 2 * (i % 2)
                    pe.wait_ge(sem[f"free{b}"], at_bank(st, b, i // 2))
                    pe_may_fill(pe, st, 4, i)
                    for c in range(min(n, 4)):
                        mm = pe.transpose(bank[:, 4, tile_cols(c)], probs[:, i % 2, tile_cols(c)], ident[:, :])
                    mm.then_inc(sem["full4"], 1)
                    if wide[i]:
                        pe_may_fill(pe, st, 5, sum(wide[:i]))
                        for c in range(4, n):
                            mm = pe.transpose(bank[:, 5, tile_cols(c - 4)], probs[:, i % 2, tile_cols(c)], ident[:, :])
                        mm.then_inc(sem["full5"], 1)

                def mix(i):
                    qt, kind, h = units[i]
                    tiles = key_tiles(qt, kind)
                    pe.wait_ge(sem["free4"], at_bank(st, 4, i))
                    if wide[i]:
                        pe.wait_ge(sem["free5"], at_bank(st, 5, sum(wide[:i])))
                    if h == 0:
                        pe_may_fill(pe, st, 6, i // HEADS)
                    v0 = P * kind + HD * (h // 2)
                    product(bank[:, 6, h * HD:h * HD + HD],
                            [(probsT[:, i % 2, tile_cols(c)], V[:, t, v0:v0 + HD]) for c, t in enumerate(tiles)],
                            sem["full6"] if h == HEADS - 1 else None)

                def turn_y(g):
                    pe.wait_ge(sem["free6"], at_bank(st, 6, g))
                    pe_may_fill(pe, st, 7, g)
                    for c in range(2):
                        mm = pe.transpose(bank[:, 7, tile_cols(c)], y_tok[:, g % 2, tile_cols(c)], ident[:, :])
                    mm.then_inc(sem["full7"], 1)

                n = len(units)
                for i in range(n + 3):
                    if i < n:
                        scores(i)
                    if 1 <= i <= n:
                        turn_probs(i - 1)
                    if 2 <= i <= n + 1:
                        mix(i - 2)
                    if i >= 3 and (i - 3) % HEADS == HEADS - 1:
                        turn_y((i - 3) // HEADS)

            def conv_out(st):
                parts = [(0, SEQ)] + ([(SEQ, NTOK)] if st.layer == 0 else [])
                for n, (source, ready) in enumerate((([HT[:, 2, :], HT[:, 3, :]], None),
                                                     ([u_sq[:, 0, :], u_sq[:, 1, :]], "squared"))):
                    if ready:
                        pe.wait_ge(sem[ready], st.at(ready, 2))
                    pe_may_fill(pe, st, 0, n)
                    for q, (lo, hi) in enumerate(parts):
                        product(bank[:, q, 0:hi - lo], [(mean_of[:, :], s[:, lo:hi]) for s in source],
                                sem["full0"] if q == len(parts) - 1 else None)

            def w_out(st):
                for i in range(st.facts["tiles"]):
                    b = 2 * (i % 4)
                    pe_may_fill(pe, st, b, i // 4)
                    for j in range(2):
                        pe_wait_unit(pe, st.first_unit + j)
                        w = slot_of(st.first_unit + j).rearrange("p (k n) -> p k n", k=KD)
                        product(bank[:, b + j, :], [(HT[:, k, tile_cols(i)], w[:, k, :]) for k in range(KD)],
                                sem[f"full{b}"] if j else None)

            def route(st):
                tiles = st.facts["tiles"]
                pe_may_fill(pe, st, 0, 0)
                for t in range(tiles):
                    product(bank[:, 0, t * EXPERTS:(t + 1) * EXPERTS],
                            [(HT[:, k, tile_cols(t)], router[:, st.layer, k, :]) for k in range(KD)],
                            sem["full0"] if t == tiles - 1 else None)
                pe.wait_ge(sem["affinity"], st.at("affinity", 1))
                pe_may_fill(pe, st, 1, 0)
                for t in range(ST):
                    mm = pe.transpose(bank[0:EXPERTS, 1, tile_cols(t)], aff[:, t, :], ident[:, :])
                mm.then_inc(sem["full1"], 1)
                if tiles > ST:
                    pe_may_fill(pe, st, 2, 0)
                    for t in range(CT):
                        mm = pe.transpose(bank[0:EXPERTS, 2, tile_cols(t)], aff[:, ST + t, :], ident[:, :])
                    mm.then_inc(sem["full2"], 1)
                n = NS if tiles > ST else CAP_X
                pe.wait_ge(sem["ranked"], st.at("ranked", 1))
                pe_may_fill(pe, st, 3, 0)
                pe.transpose(bank[0:n, 3, 0:EXPERTS], top_at[0:EXPERTS, 0:n], ident[0:EXPERTS, 0:EXPERTS])
                pe.transpose(bank[0:n, 3, EXPERTS:2 * EXPERTS], top[0:EXPERTS, 0:n],
                             ident[0:EXPERTS, 0:EXPERTS]).then_inc(sem["full3"], 1)

            def experts(st):
                n = NS if st.facts["tiles"] > ST else CAP_X
                first = st.first_unit

                def turn_rows(e):
                    pe.wait_ge(sem["gathered"], st.at("gathered", 0) + (e + 1) * 16)
                    for b in range(2):
                        pe_may_fill(pe, st, b, e)
                        for c in range(4):
                            mm = pe.matmul(bank[:, b, c * n:(c + 1) * n], xs[0:n, tile_cols(4 * b + c)],
                                           ident[0:n, 0:n], start=True, stop=True)
                        mm.then_inc(sem[f"full{b}"], 1)

                turn_rows(0)
                with pe.Fori(0, EXPERTS // 2) as pair:
                    for h in range(2):
                        e = pair * 2 + h
                        for b in range(2):
                            pe.wait_ge(sem[f"free{b}"], at_bank(st, b, e))
                        for j in range(4):
                            unit = first + 6 * h + j
                            pe_wait_unit(pe, unit, pair, 12 // SLOTS)
                            pe_may_fill(pe, st, 2 + j, e)
                            w = slot_of(unit).rearrange("p (k n) -> p k n", k=KD)
                            for c in range(4):
                                product(bank[:, 2 + j, c * n:(c + 1) * n],
                                        [(w[:, k, tile_cols(c)], xsT[:, k, 0:n]) for k in range(KD)],
                                        sem[f"full{2 + j}"] if c == 3 else None)
                        turn_rows(e + 1)
                        for j in range(2):
                            unit = first + 6 * h + 4 + j
                            pe_wait_unit(pe, unit, pair, 12 // SLOTS)
                            pe_may_fill(pe, st, 6 + j, e)
                            w = slot_of(unit).rearrange("p (k n) -> p k n", k=KD)
                            for k in range(KD):
                                if j == 0 and k % 4 == 0:
                                    b = 3 if k == 0 else 5
                                    pe.wait_ge(sem[f"free{b}"], at_bank(st, b, e))
                                mm = pe.matmul(bank[0:n, 6 + j, :], actT[:, k, 0:n], w[:, k, :],
                                               start=(k == 0), stop=(k == KD - 1))
                            mm.then_inc(sem[f"full{6 + j}"], 1)

            def ffn_up(st):
                for c in range(F_CHUNKS):
                    u, b = c // 4, 2 * (c % 4)
                    width = min(512, D_FF - 512 * u)
                    for n in range(2):
                        unit = st.first_unit + 2 * u + n
                        pe_wait_unit(pe, unit)
                        pe_may_fill(pe, st, b + n, c // 4)
                        w = slot_of(unit)[:, 0:KD * width].rearrange("p (k n) -> p k n", k=KD)
                        product(bank[:, b + n, :], [(w[:, k, tile_cols(c % 4)], HT[:, k, 0:SEQ]) for k in range(KD)],
                                sem[f"full{b + n}"])

            def ffn_down(st):
                for half in range(2):
                    for n in range(3):
                        unit = st.first_unit + 3 * half + n
                        k1 = min(F_CHUNKS, 8 * n + 8)
                        pe_wait_unit(pe, unit)
                        w = slot_of(unit)[:, 0:(k1 - 8 * n) * 512].rearrange("p (k n) -> p k n", n=512)
                        for t in range(ST):
                            b = 4 * half + t
                            if n == 0:
                                pe_may_fill(pe, st, b, 0)
                            for k in range(8 * n, k1):
                                mm = pe.matmul(bank[:, b, :], ffnT[:, k, tile_cols(t)], w[:, k - 8 * n, :],
                                               start=(k == 0), stop=(k == F_CHUNKS - 1))
                            if n == 2:
                                mm.then_inc(sem[f"full{b}"], 1)
                        if n < 2:
                            mm.then_inc(sem["down_read"], 1)

            def latent_in(st):
                pe_wait_unit(pe, st.first_unit)
                w = slot_of(st.first_unit)[:, 0:KD * LATENT].rearrange("p (k n) -> p k n", k=KD)

                def turned(i):
                    b = 2 + i % 2
                    pe.wait_ge(sem["latent"], st.at("latent", i + 1))
                    pe_may_fill(pe, st, b, i // 2)
                    for c in range(3):
                        mm = pe.transpose(bank[:, b, tile_cols(c)], z_lat[:, i % 2, tile_cols(c)], ident[:, :])
                    mm.then_inc(sem[f"full{b}"], 1)

                for i in range(ST):
                    b = i % 2
                    pe_may_fill(pe, st, b, i // 2)
                    product(bank[:, b, 0:LATENT], [(HT[:, k, tile_cols(i)], w[:, k, :]) for k in range(KD)], sem[f"full{b}"])
                    if i:
                        turned(i - 1)
                turned(ST - 1)

            def latent_qk(st):
                pe_wait_unit(pe, st.first_unit)
                pe_wait_unit(pe, st.first_unit + 1)
                n_q = L_HEADS * L_QK
                w_q = slot_of(st.first_unit)[:, 0:2 * n_q].rearrange("p (k n) -> p k n", k=2)
                w_kv = slot_of(st.first_unit + 1)

                def turned(i):
                    for n, (rows, name) in enumerate(((q_rows, "q_rows"), (k_rows, "k_rows"))):
                        pe.wait_ge(sem[name], st.at(name, i + 1))
                        for half in range(2):
                            b = 4 + 2 * n + half
                            pe_may_fill(pe, st, b, i)
                            for c in range(4):
                                h = 4 * half + c
                                mm = pe.transpose(bank[0:L_QK, b, tile_cols(c)], rows[:, i % 2, h * L_QK:(h + 1) * L_QK], ident[:, :])
                            mm.then_inc(sem[f"full{b}"], 1)

                for i in range(ST):
                    pe_may_fill(pe, st, 0, i)
                    for j, (lo, hi) in enumerate(((0, 512), (512, n_q))):
                        product(bank[:, j, 0:hi - lo], [(latentT[:, k, tile_cols(i)], w_q[:, k, lo:hi]) for k in range(2)],
                                sem["full0"] if j else None)
                    pe_may_fill(pe, st, 2, i)
                    for j in range(2):
                        product(bank[:, 2 + j, :], [(latentT[:, 2, tile_cols(i)], w_kv[:, 512 * j:512 * j + 512])],
                                sem["full2"] if j else None)
                    if i:
                        turned(i - 1)
                turned(ST - 1)

            def diff_in(st):
                def turned(i):
                    pe.wait_ge(sem["qk_rows"], st.at("qk_rows", i + 1))
                    for n in range(2):
                        pe_may_fill(pe, st, 4 + n, i)
                        for c in range(4):
                            mm = pe.transpose(bank[:, 4 + n, tile_cols(c)], qk_diff[:, i % 2, tile_cols(4 * n + c)], ident[:, :])
                        mm.then_inc(sem[f"full{4 + n}"], 1)

                for i in range(ST):
                    for j in range(3):
                        if j != 1:
                            pe_may_fill(pe, st, j, i)
                        pe_wait_unit(pe, st.first_unit + j)
                        w = slot_of(st.first_unit + j).rearrange("p (k n) -> p k n", k=KD)
                        product(bank[:, j, :], [(HT[:, k, tile_cols(i)], w[:, k, :]) for k in range(KD)],
                                None if j == 0 else sem["full0" if j == 1 else "full2"])
                    if i:
                        turned(i - 1)
                turned(ST - 1)

            def attend_two(st):
                units = units_two()

                def scores(i):
                    kind, qt, h, s = units[i]
                    rows = slice(0, L_QK) if kind == 0 else slice(HD * s, HD * s + HD)
                    qT, kT = (q_latT, k_latT) if kind == 0 else (q_diffT, k_diffT)
                    b = i % 2
                    q = qT[rows, h, tile_cols(qt)]
                    pe_may_fill(pe, st, b, i // 2)
                    if qt:
                        pe.matmul(bank[:, b, 0:qt * P], q, kT[rows, h, 0:qt * P], start=True, stop=True)
                    pe.matmul(bank[:, b, tile_cols(qt)], q, kT[rows, h, tile_cols(qt)], start=True, stop=False)
                    pe.matmul(bank[:, b, tile_cols(qt)], ident[:, :], band[:, 1, :], start=False, stop=True)\
                        .then_inc(sem[f"full{b}"], 1)

                def turn_probs(i):
                    qt, b = units[i][1], 2 + i % 2
                    pe.wait_ge(sem[f"free{i % 2}"], at_bank(st, i % 2, i // 2))
                    pe_may_fill(pe, st, b, i // 2)
                    for c in range(qt + 1):
                        mm = pe.transpose(bank[:, b, tile_cols(c)], probs2[:, i % 2, tile_cols(c)], ident[:, :])
                    mm.then_inc(sem[f"full{b}"], 1)

                def mix(i):
                    kind, qt, h, s = units[i]
                    g = i // 2
                    b = 4 + g % 2
                    pe.wait_ge(sem[f"free{2 + i % 2}"], at_bank(st, 2 + i % 2, i // 2))
                    if s == 0:
                        pe_may_fill(pe, st, b, g // 2)
                    v, width = (v_lat, L_V) if kind == 0 else (v_diff, 2 * HD)
                    product(bank[:, b, s * width:(s + 1) * width],
                            [(probs2T[:, i % 2, tile_cols(c)], v[:, c, h * width:(h + 1) * width]) for c in range(qt + 1)],
                            sem[f"full{b}"] if s else None)

                def turn_y(g):
                    b = 6 + g % 2
                    pe.wait_ge(sem["y_rows"], st.at("y_rows", g + 1))
                    pe_may_fill(pe, st, b, g // 2)
                    pe.transpose(bank[:, b, 0:P], y_rows2[:, g % 2, :], ident[:, :]).then_inc(sem[f"full{b}"], 1)

                n = len(units)
                for i in range(n + 4):
                    if i < n:
                        scores(i)
                    if 1 <= i <= n:
                        turn_probs(i - 1)
                    if 2 <= i <= n + 1:
                        mix(i - 2)
                    if i >= 4 and (i - 4) % 2 == 1:
                        turn_y((i - 4) // 2)

            def merge(st):
                for c in range(KD):
                    half, b = c // 4, 4 * (c % 2)
                    cols = tile_cols(c % 4)
                    u = st.first_unit + 3 * half
                    w = [slot_of(u + n).rearrange("p (k n) -> p k n", k=KD) for n in range(3)]
                    for n, (m, pairs) in enumerate((
                            (1, [(w[1][:, k, cols], HT[:, k, 0:SEQ]) for k in range(KD)]),
                            (0, [(w[0][:, k, cols], yT[:, k, :]) for k in range(4)]),
                            (2, [(w[2][:, k, cols], HT[:, k, 0:SEQ]) for k in range(KD)]),
                            (0, [(w[0][:, 4 + k, cols], yT[:, 4 + k, :]) for k in range(4)]))):
                        pe_wait_unit(pe, u + m)
                        pe_may_fill(pe, st, b + n, c // 2)
                        product(bank[:, b + n, :], pairs, sem[f"full{b + n}"])

            def project(st):
                for i in range(ST):
                    b = 2 * i
                    pe_may_fill(pe, st, b, 0)
                    for j in range(2):
                        pe_wait_unit(pe, st.first_unit + j)
                        w = slot_of(st.first_unit + j).rearrange("p (k n) -> p k n", k=KD)
                        product(bank[:, b + j, :], [(mergedT[:, k, tile_cols(i)], w[:, k, :]) for k in range(KD)],
                                sem[f"full{b}"] if j else None)

            programs = dict(ada=ada, norm=norm, conv_in=conv_in, qkv=qkv, attend=attend, conv_out=conv_out,
                            w_out=w_out, route=route, experts=experts, ffn_up=ffn_up, ffn_down=ffn_down,
                            latent_in=latent_in, latent_qk=latent_qk, diff_in=diff_in, attend_two=attend_two,
                            merge=merge, project=project)
            for st in stages:
                enter(pe, st)
                if st.name in programs:
                    programs[st.name](st)

        @block.scalar
        def _(act):
            step = Steps(act, sem["scalar_steps"])
            flat_bank = bank[:, :, :].rearrange("p b n -> p (b n)")

            def init(st):
                act.wait_ge(sem["constants"], CONSTANTS * 16)
                act.activation(silu_c[:, :, :], silu_c[:, :, :], ACT.Silu).then_inc(sem["silu_c"], 1)

            def norm(st):
                tiles = st.facts["tiles"]
                for i, t in enumerate(tiles):
                    step(act.activation(junk[:, :], X[:, t, :], ACT.Square, accum_out=small[:, i:i + 1]))
                    act.activation(small[:, 8 + i:9 + i], small[:, i:i + 1], ACT.Sqrt, bias=eps[:, :],
                                   scale=1.0 / D).then_inc(sem["mean_root"], 1)
                for i, t in enumerate(tiles):
                    b = 2 * (i % 4)
                    act.wait_ge(sem[f"full{b}"], at_bank(st, b, i // 4))
                    act.activation(HT[:, 0:4, tile_cols(t)], bank[:, b, :].rearrange("p (k n) -> p k n", k=4),
                                   ACT.Copy).then_inc(sem[f"free{b}"], 1)

            def conv_in(st):
                parts = st.facts["parts"]
                for c in range(CONV_COLS // P):
                    what, half = c // 2, c % 2
                    if what not in (0, 1, 4):
                        continue
                    for part in range(parts):
                        g = c * parts + part
                        b = g % BANKS
                        lo, hi = (0, SEQ) if part == 0 else (SEQ, NTOK)
                        start = part * (SEQ + 2 * PAD_A) + PAD_A
                        act.wait_ge(sem[f"full{b}"], at_bank(st, b, g // BANKS))
                        dst, func = {0: (conv_a_gate[:, half, lo:hi], ACT.Copy),
                                     1: (conv_a_in[:, half, start:start + hi - lo], ACT.Copy),
                                     4: (sig[:, half, lo:hi], ACT.Sigmoid)}[what]
                        act.activation(dst, bank[:, b, 0:hi - lo], func).then_inc(sem[f"free{b}"], 1)

            def qkv(st):
                def take_turned(i):
                    keys_only = st.layer == 1 and i >= ST
                    c0 = 2 if keys_only else 0
                    for kind in range(2):
                        b = 6 + kind
                        act.wait_ge(sem[f"full{b}"], at_bank(st, b, i))
                        act.activation(QKT[:, 3 * kind + c0:3 * kind + 3, tile_cols(i)],
                                       bank[:, b, c0 * P:3 * P].rearrange("p (k n) -> p k n", n=P),
                                       ACT.Copy).then_inc(sem[f"free{b}"], 1)

                for i in range(ST + CT):
                    b, use = 2 * (i % 3), i // 3
                    lo = 256 if st.layer == 1 and i >= ST else 0
                    act.wait_ge(sem[f"full{b}"], at_bank(st, b, use))
                    if i >= 2:
                        act.wait_ge(sem["qk_ready"], st.at("qk_ready", i - 1))
                    z = z_tok[:, i % 2, :].rearrange("p (a n) -> p a n", a=2)
                    act.activation(z[:, :, lo:384], bank[:, b:b + 2, lo:384], ACT.Copy)
                    act.activation(V[:, i, :].rearrange("p (a n) -> p a n", a=2), bank[:, b:b + 2, 384:512],
                                   ACT.Copy).then_inc(sem[f"free{b}"], 1)
                    act.wait_ge(sem["head_sums"], st.at("head_sums", i + 1))
                    act.activation(small[:, 8:14], small[:, 0:6], ACT.Sqrt, bias=eps[:, :],
                                   scale=1.0 / HD).then_inc(sem["head_roots"], 1)
                    if i:
                        take_turned(i - 1)
                take_turned(ST + CT - 1)

            def attend(st):
                units = heads_of(st.layer)
                wide = st.facts["wide"]

                def exponentials(i):
                    qt, kind, h = units[i]
                    n = len(key_tiles(qt, kind)) * P
                    b, g = 2 * (i % 2), i // HEADS
                    act.wait_ge(sem["neg_max"], st.at("neg_max", i + 1))
                    if i >= 2:
                        act.wait_ge(sem["full4"], at_bank(st, 4, i - 2))
                        if wide[i - 2]:
                            act.wait_ge(sem["full5"], at_bank(st, 5, sum(wide[:i - 2])))
                    lo = (b + 1) * BANK + CTX - n
                    col = 16 + 4 * (g % 2) + h
                    act.activation(probs[:, i % 2, 0:n], flat_bank[:, lo:lo + n], ACT.Exp, bias=small[:, i % 8:i % 8 + 1],
                                   scale=HD ** -0.5, accum_out=small[:, col:col + 1]).then_inc(sem[f"free{b}"], 1)
                    if kind == 0:
                        act.activation(small[:, col + 8:col + 9], sink[:, st.layer, h:h + 1], ACT.Exp,
                                       bias=small[:, i % 8:i % 8 + 1]).then_inc(sem["sink_exp"], 1)

                def take_probs(i):
                    n = len(key_tiles(*units[i][:2]))
                    act.wait_ge(sem["full5"], at_bank(st, 5, sum(wide[:i])))
                    act.activation(probsT[:, i % 2, 4 * P:n * P], bank[:, 5, 0:(n - 4) * P], ACT.Copy)\
                       .then_inc(sem["free5"], 1)

                def take_y(g):
                    qt, kind, _ = units[g * HEADS]
                    act.wait_ge(sem["full7"], at_bank(st, 7, g))
                    act.activation(HT[:, 4 + 2 * kind:6 + 2 * kind, tile_cols(qt)],
                                   bank[:, 7, 0:2 * P].rearrange("p (k n) -> p k n", k=2), ACT.Copy)\
                       .then_inc(sem["free7"], 1)

                n = len(units)
                for i in range(n + 3):
                    if i < n:
                        exponentials(i)
                    if 1 <= i <= n and wide[i - 1]:
                        take_probs(i - 1)
                    if i >= 3 and (i - 3) % HEADS == HEADS - 1:
                        take_y((i - 3) // HEADS)

            def conv_out(st):
                n = NTOK if st.layer == 0 else SEQ
                for c in range(2):
                    if c == 0:
                        act.wait_ge(sem["centered"], st.at("centered", 1))
                    else:
                        act.wait_ge(sem["free0"], at_bank(st, 0, 0))
                    act.activation(u_sq[:, c, 0:n], HT[:, 2 + c, 0:n], ACT.Square).then_inc(sem["squared"], 1)
                act.wait_ge(sem["full0"], at_bank(st, 0, 1))
                act.activation(u_rstd[:, 0:n], flat_bank[:, 0:n], ACT.Sqrt, bias=eps[:, :]).then_inc(sem["free0"], 1)
                for c in range(2):
                    act.wait_ge(sem["normed"], st.at("normed", c + 1))
                    act.activation(HT[:, 2 + c, 0:n], HT[:, 2 + c, 0:n], ACT.Silu, bias=conv_vec[:, 2, st.layer, c:c + 1],
                                   scale=conv_vec[:, 1, st.layer, c:c + 1])

            def route(st):
                act.wait_ge(sem["free0"], at_bank(st, 0, 0))
                v = aff[:, 0:st.facts["tiles"], :]
                act.activation(v, v, ACT.Exp).then_inc(sem["logit_exp"], 1)

            def experts(st):
                n = NS if st.facts["tiles"] > ST else CAP_X

                def take_rows(e):
                    act.wait_ge(sem["full0"], at_bank(st, 0, e))
                    act.activation(xsT[:, 0:4, 0:n], bank[:, 0, 0:4 * n].rearrange("p (k n) -> p k n", k=4), ACT.Copy)\
                       .then_inc(sem["free0"], 1)

                take_rows(0)
                with act.Fori(0, EXPERTS) as e:
                    for half in range(2):
                        b = 2 + 2 * half
                        act.wait_ge(sem[f"full{b}"], at_bank(st, b, e))
                        act.wait_ge(sem[f"free{b + 1}"], st.at(f"bank{b + 1}", e))
                        act.activation(gateT[:, half, 0:4 * n], bank[:, b, 0:4 * n], ACT.Silu)\
                           .then_inc(sem[f"free{b}"], 1)
                    take_rows(e + 1)

            def norm_rows(st):
                for t in range(ST):
                    step(act.activation(junk[:, :], X[:, t, :], ACT.Square, accum_out=small[:, t:t + 1]))
                    act.activation(small[:, 8 + t:9 + t], small[:, t:t + 1], ACT.Sqrt, bias=eps[:, :],
                                   scale=1.0 / D).then_inc(sem["mean_root"], 1)

            def angles(st):
                act.wait_ge(sem["lam_sum"], st.at("lam_sum", 1))
                act.activation(lam[:, 0:2], lam[:, 0:2], ACT.Exp).then_inc(sem["lam_exp"], 1)
                act.wait_ge(sem["angles"], st.at("angles", 1))
                act.activation(cos2[:, :, :], cos2[:, :, :], ACT.Sin)
                act.activation(sin2[:, :, :], sin2[:, :, :], ACT.Sin).then_inc(sem["sines"], 1)

            def ffn_up(st):
                for c in range(F_CHUNKS):
                    b = 2 * (c % 4)
                    act.wait_ge(sem[f"full{b}"], at_bank(st, b, c // 4))
                    if c >= 2:
                        q = 2 * ((c - 2) % 4) + 1
                        act.wait_ge(sem[f"free{q}"], at_bank(st, q, (c - 2) // 4))
                    act.activation(ffn_gate[:, c % 2, :], bank[:, b, :], ACT.Silu).then_inc(sem[f"free{b}"], 1)

            def latent_in(st):
                def take(i):
                    b = 2 + i % 2
                    act.wait_ge(sem[f"full{b}"], at_bank(st, b, i // 2))
                    for c in range(3):
                        ins = act.activation(latentT[:, c, tile_cols(i)], bank[:, b, tile_cols(c)], ACT.Copy,
                                             scale=latent_gain[:, c:c + 1])
                    ins.then_inc(sem[f"free{b}"], 1)

                for i in range(ST):
                    b = i % 2
                    act.wait_ge(sem[f"full{b}"], at_bank(st, b, i // 2))
                    for n, (lo, width) in enumerate(((0, Q_RANK), (Q_RANK, KV_RANK))):
                        act.activation(junk[:, 0:width], bank[:, b, lo:lo + width], ACT.Square,
                                       accum_out=small[:, 2 * i + n:2 * i + n + 1]).then_inc(sem["latent_sum"], 1)
                        act.wait_ge(sem["latent_sum"], st.at("latent_sum", 2 * i + n + 1))
                        act.activation(small[:, 16 + 2 * i + n:17 + 2 * i + n], small[:, 2 * i + n:2 * i + n + 1], ACT.Sqrt,
                                       bias=eps[:, :], scale=1.0 / width).then_inc(sem["latent_root"], 1)
                    if i:
                        take(i - 1)
                take(ST - 1)

            def latent_qk(st):
                def take(i):
                    for b, dst in ((4, q_latT), (5, q_latT), (6, k_latT), (7, k_latT)):
                        act.wait_ge(sem[f"full{b}"], at_bank(st, b, i))
                        act.activation(dst[0:L_QK, 4 * (b % 2):4 * (b % 2) + 4, tile_cols(i)],
                                       bank[0:L_QK, b, :].rearrange("p (h n) -> p h n", h=4), ACT.Copy)\
                            .then_inc(sem[f"free{b}"], 1)

                for i in range(ST):
                    act.wait_ge(sem["free2"], at_bank(st, 2, i))
                    if i:
                        take(i - 1)
                take(ST - 1)

            def diff_in(st):
                def take(i):
                    for n, dst in enumerate((q_diffT, k_diffT)):
                        b = 4 + n
                        act.wait_ge(sem[f"full{b}"], at_bank(st, b, i))
                        act.activation(dst[:, :, tile_cols(i)], bank[:, b, :].rearrange("p (h n) -> p h n", h=4), ACT.Copy)\
                            .then_inc(sem[f"free{b}"], 1)

                for i in range(ST):
                    act.wait_ge(sem["full2"], at_bank(st, 2, i))
                    act.activation(v_diff[:, i, :], bank[:, 2, :], ACT.Copy).then_inc(sem["free2"], 1)
                    if i:
                        take(i - 1)
                take(ST - 1)

            def attend_two(st):
                units = units_two()
                scales = (L_QK ** -0.5, HD ** -0.5)

                def exponentials(i):
                    kind, qt, h, s = units[i]
                    n, b = (qt + 1) * P, i % 2
                    act.wait_ge(sem["neg_max"], st.at("neg_max", i + 1))
                    if i >= 2:
                        act.wait_ge(sem[f"full{2 + b}"], at_bank(st, 2 + b, i // 2 - 1))
                    act.activation(probs2[:, b, 0:n], bank[:, b, 0:n], ACT.Exp, bias=small[:, i % 8:i % 8 + 1],
                                   scale=scales[kind], accum_out=small[:, 16 + i % 8:17 + i % 8]).then_inc(sem[f"free{b}"], 1)

                def root(g):
                    k = g - 4 * L_HEADS // 2
                    act.wait_ge(sem["y_sum"], st.at("y_sum", k + 1))
                    act.activation(small[:, 64 + g % 2:65 + g % 2], small[:, 62 + g % 2:63 + g % 2], ACT.Sqrt,
                                   bias=eps[:, :], scale=1.0 / (2 * HD)).then_inc(sem["y_root"], 1)

                def take_y(g):
                    kind, qt, h, _ = units[2 * g]
                    b = 6 + g % 2
                    act.wait_ge(sem[f"full{b}"], at_bank(st, b, g // 2))
                    chunk = h // 2 if kind == 0 else 4 + h
                    act.activation(yT[:, chunk, tile_cols(qt)], bank[:, b, 0:P], ACT.Copy).then_inc(sem[f"free{b}"], 1)

                n = len(units)
                for i in range(n + 4):
                    if i < n:
                        exponentials(i)
                    if i >= 3 and (i - 3) % 2 == 0 and (i - 3) // 2 < n // 2 and units[i - 3][0]:
                        root((i - 3) // 2)
                    if i >= 4 and (i - 4) % 2 == 1:
                        take_y((i - 4) // 2)

            def merge(st):
                for c in range(KD):
                    b, use = 4 * (c % 2), c // 2
                    for n in range(2):
                        act.wait_ge(sem[f"full{b + 2 * n}"], at_bank(st, b + 2 * n, use))
                        if c >= 2:
                            act.wait_ge(sem["merged"], st.at("merged", c - 1))
                        act.activation(merge_gate[:, c % 2, n * SEQ:(n + 1) * SEQ], bank[:, b + 2 * n, :], ACT.Sigmoid)\
                            .then_inc(sem[f"free{b + 2 * n}"], 1)

            programs = dict(init=init, norm=norm, conv_in=conv_in, qkv=qkv, attend=attend, conv_out=conv_out,
                            route=route, experts=experts, norm_rows=norm_rows, angles=angles, ffn_up=ffn_up,
                            latent_in=latent_in, latent_qk=latent_qk, diff_in=diff_in, attend_two=attend_two, merge=merge)
            for st in stages:
                enter(act, st)
                if st.name in programs:
                    programs[st.name](st)
                act.activation(done_mark[:, 0:1], eps[:, :], ACT.Copy).then_inc(sem["scalar_finished"], 1)

        @block.vector
        def _(dve):
            step = Steps(dve, sem["vector_steps"])
            flat_bank = bank[:, :, :].rearrange("p b n -> p (b n)")

            def per_row(column, n, m):
                return column.unsqueeze(2).broadcast_to([P, n, m])

            def init(st):
                dve.memset(mean_of[:, :], 1.0 / (D // 4))
                dve.memset(conv_a_in[:, :, :], 0.0)
                dve.memset(conv_b_in[:, :, :], 0.0)

            def ada(st):
                l = st.layer
                rows = HT[:, :, :].rearrange("p k n -> p (k n)")
                dve.wait_ge(sem["rows_loaded"], st.at("rows_loaded", 32))
                for n in range(6 * D // 512):
                    b = n % BANKS
                    cols = slice(512 * n, 512 * n + 512)
                    dve.wait_ge(sem[f"full{b}"], at_bank(st, b, n // BANKS))
                    dve.tensor_tensor(rows[0:2, cols], bank[0:2, b, :], ada_bias[0:2, cols], ALU.add)\
                       .then_inc(sem[f"free{b}"], 1)
                for b in range(BANKS):
                    dve.wait_ge(sem[f"free{b}"], st.at(f"bank{b}", st.signals[f"bank{b}"]))
                for n, comp in enumerate((1, 4)):
                    v = rows[0:2, comp * D:comp * D + D]
                    ins = dve.scalar_tensor_tensor(v, v, 1.0, norm_gain[0:2, n, :], ALU.add, ALU.mult)
                ins.then_inc(sem["mods_rows"], 1)

            def norm(st):
                tiles, shift = st.facts["tiles"], st.facts["shift"]

                def take(i):
                    b = 2 * (i % 4) + 1
                    dve.wait_ge(sem[f"full{b}"], at_bank(st, b, i // 4))
                    dve.tensor_copy(HT[:, 4:8, tile_cols(tiles[i])], bank[:, b, :].rearrange("p (k n) -> p k n", k=4))\
                       .then_inc(sem[f"free{b}"], 1)

                dve.wait_ge(sem["rows_loaded"], st.at("rows_loaded", 32 if shift is not None else 16))
                for i, t in enumerate(tiles):
                    dve.wait_ge(sem["mean_root"], st.at("mean_root", i + 1))
                    step(dve.reciprocal(small[:, 16 + i:17 + i], small[:, 8 + i:9 + i]))
                    if i >= 2:
                        b = 2 * ((i - 2) % 4) + 1
                        dve.wait_ge(sem[f"full{b}"], at_bank(st, b, (i - 2) // 4))
                        if st.facts["store"]:
                            dve.wait_ge(sem[f"h_stored{i % 2}"], st.at(f"h_stored{i % 2}", 16 * (i // 2)))
                    h = h_tok[:, i % 2, :]
                    ins = dve.scalar_tensor_tensor(h, X[:, t, :], small[:, 16 + i:17 + i], mod[:, 0, :], ALU.mult, ALU.mult)
                    if shift is not None:
                        step(ins)
                        ins = dve.tensor_tensor(h, h, mod[:, 1, :], ALU.add)
                    ins.then_inc(sem["h_ready"], 1)
                    if i:
                        take(i - 1)
                take(len(tiles) - 1)

            def conv_in(st):
                parts = st.facts["parts"]

                def group(c, part):
                    g = c * parts + part
                    return g % BANKS, g // BANKS

                for c in range(4, CONV_COLS // P):
                    what, half = c // 2, c % 2
                    for part in range(parts):
                        b, use = group(c, part)
                        lo, hi = (0, SEQ) if part == 0 else (SEQ, NTOK)
                        n = hi - lo
                        start_a = part * (SEQ + 2 * PAD_A) + PAD_A
                        start_b = part * (SEQ + 2 * PAD_B) + PAD_B
                        va = conv_a_in[:, half, start_a:start_a + n]
                        vb = conv_b_in[:, half, start_b:start_b + n]
                        if what == 2:
                            b_c, use_c = group(c - 2, part)
                            dve.wait_ge(sem[f"free{b_c}"], at_bank(st, b_c, use_c))
                            dve.wait_ge(sem[f"full{b}"], at_bank(st, b, use))
                            dve.tensor_tensor(va, bank[:, b, 0:n], va, ALU.mult).then_inc(sem[f"free{b}"], 1)
                        elif what == 3:
                            dve.wait_ge(sem[f"full{b}"], at_bank(st, b, use))
                            dve.tensor_copy(vb, bank[:, b, 0:n]).then_inc(sem[f"free{b}"], 1)
                        else:
                            b_v, use_v = group(c - 2, part)
                            dve.wait_ge(sem[f"free{b_v}"], at_bank(st, b_v, use_v))
                            dve.wait_ge(sem[f"free{b}"], at_bank(st, b, use))
                            dve.tensor_tensor(vb, vb, sig[:, half, lo:hi], ALU.mult)

            def qkv(st):
                l = st.layer
                for i in range(ST + CT):
                    b, use = 2 * (i % 3), i // 3
                    keys_only = l == 1 and i >= ST
                    h0 = 4 if keys_only else 0
                    nh = 6 - h0
                    z = z_tok[:, i % 2, :].rearrange("p (a n) -> p a n", a=2)
                    heads = z[:, 1, h0 * HD:].rearrange("p (h d) -> p h d", d=HD)
                    sq = squares[:, h0 * HD:].rearrange("p (h d) -> p h d", d=HD)
                    dve.wait_ge(sem[f"free{b}"], at_bank(st, b, use))
                    step(dve.tensor_tensor(sq, heads, heads, ALU.mult))
                    dve.tensor_reduce(small[:, h0:6], sq, AX.X, ALU.add).then_inc(sem["head_sums"], 1)
                    dve.wait_ge(sem["head_roots"], st.at("head_roots", i + 1))
                    step(dve.reciprocal(small[:, 16 + h0:22], small[:, 8 + h0:14]))
                    step(dve.tensor_tensor(heads, heads, per_row(small[:, 16 + h0:22], nh, HD), ALU.mult))
                    step(dve.tensor_tensor(heads, heads, head_gain[:, l, h0:6, :], ALU.mult))
                    if i < ST:
                        all_heads = z_tok[:, i % 2, :].rearrange("p (h d) -> p h d", d=HD)
                        swap = z_tok[:, i % 2, :].rearrange("p (h b d) -> p h b d", b=2, d=HD // 4)
                        turned = rope_b.rearrange("p (h b d) -> p h b d", b=2, d=HD // 4)
                        sin = rope_sin[:, i, :].rearrange("p (a b d) -> p a b d", a=2, b=2)
                        step(dve.tensor_tensor(rope_a.rearrange("p (h d) -> p h d", d=HD), all_heads,
                                               rope_cos[:, i, :].unsqueeze(1).broadcast_to([P, 12, HD]), ALU.mult))
                        for a_ in range(2):
                            for to in range(2):
                                step(dve.tensor_tensor(
                                    turned[:, a_::2, to, :], swap[:, a_::2, 1 - to, :],
                                    sin[:, a_, to, :].unsqueeze(1).broadcast_to([P, 12, HD // 4]), ALU.mult))
                    if i >= 2:
                        for kind in range(2):
                            dve.wait_ge(sem[f"full{6 + kind}"], at_bank(st, 6 + kind, i - 2))
                    for kind in range(2):
                        c0 = 384 * kind
                        pieces = [(slice(c0 + 256, c0 + 384), None)]
                        if not keys_only:
                            pieces.append((slice(c0, c0 + 256), "q"))
                        for cols, q in pieces:
                            def view(v, order):
                                v = v[:, cols]
                                return v.rearrange(order, g=2, j=2) if q else v
                            dst = view(qk_tok[:, i % 2, :], "p (j g d) -> p g j d")
                            if i < ST:
                                ins = dve.tensor_tensor(dst, view(rope_a, "p (g j d) -> p g j d"),
                                                        view(rope_b, "p (g j d) -> p g j d"), ALU.add)
                            else:
                                ins = dve.tensor_copy(dst, view(z_tok[:, i % 2, :], "p (g j d) -> p g j d"))
                    ins.then_inc(sem["qk_ready"], 1)
                    dve.wait_ge(sem["qk_ready"], st.at("qk_ready", i + 1))

            def attend(st):
                l = st.layer
                units = heads_of(l)

                def maximum(i):
                    qt, kind, h = units[i]
                    n = len(key_tiles(qt, kind)) * P
                    b = 2 * (i % 2)
                    lo = (b + 1) * BANK + CTX - n
                    dve.wait_ge(sem[f"full{b}"], at_bank(st, b, i // 2))
                    m = small[:, 40 + i % 8:41 + i % 8]
                    step(dve.tensor_reduce(m, flat_bank[:, lo:lo + n], AX.X, ALU.max))
                    scale = -HD ** -0.5
                    if kind == 0:
                        step(dve.tensor_scalar(m, m, -scale, sink[:, l, h:h + 1], ALU.mult, ALU.max))
                        scale = -1.0
                    dve.tensor_scalar(small[:, i % 8:i % 8 + 1], m, scale, None, ALU.mult).then_inc(sem["neg_max"], 1)

                def tap(k):
                    for part, (lo, hi) in enumerate([(0, SEQ)] + ([(SEQ, NTOK)] if l == 0 else [])):
                        start = part * (SEQ + 2 * PAD_B)
                        dst = HT[:, 3, lo:hi]
                        v, w = conv_b_in[:, 1, start + k:start + k + hi - lo], conv_b_w[:, l, 1, k:k + 1]
                        if k:
                            step.later(dve.scalar_tensor_tensor(dst, v, w, dst, ALU.mult, ALU.add))
                        else:
                            step.later(dve.tensor_scalar(dst, v, w, conv_vec[:, 0, l, 1:2], ALU.mult, ALU.add))

                def take_probs(i):
                    n = min(4, len(key_tiles(*units[i][:2])))
                    dve.wait_ge(sem["full4"], at_bank(st, 4, i))
                    dve.tensor_copy(probsT[:, i % 2, 0:n * P], bank[:, 4, 0:n * P]).then_inc(sem["free4"], 1)

                def rows_of_y(g):
                    kind = units[g * HEADS][1]
                    c = 16 + 4 * (g % 2)
                    total = small[:, c:c + 4]
                    dve.wait_ge(sem["full6"], at_bank(st, 6, g))
                    if kind == 0:
                        sinks = sum(k == 0 for _, k, _ in units[:(g + 1) * HEADS])
                        dve.wait_ge(sem["sink_exp"], st.at("sink_exp", sinks))
                        step(dve.tensor_tensor(total, total, small[:, c + 8:c + 12], ALU.add))
                    step(dve.reciprocal(small[:, c + 16:c + 20], total))
                    if g >= 2:
                        dve.wait_ge(sem["full7"], at_bank(st, 7, g - 2))
                    dve.tensor_tensor(y_tok[:, g % 2, :].rearrange("p (h d) -> p h d", d=HD),
                                      bank[:, 6, 0:HEADS * HD].rearrange("p (h d) -> p h d", d=HD),
                                      per_row(small[:, c + 16:c + 20], HEADS, HD), ALU.mult).then_inc(sem["free6"], 1)

                n = len(units)
                for i in range(n + 2):
                    if i < n:
                        maximum(i)
                    if 1 <= i <= n:
                        take_probs(i - 1)
                    if i < TAPS_B:
                        tap(i)
                    if i >= 2 and (i - 2) % HEADS == HEADS - 1:
                        rows_of_y((i - 2) // HEADS)

            def conv_out(st):
                n = NTOK if st.layer == 0 else SEQ
                dve.wait_ge(sem["full0"], at_bank(st, 0, 0))
                for c in range(2):
                    ins = dve.tensor_tensor(HT[:, 2 + c, 0:n], HT[:, 2 + c, 0:n], flat_bank[:, 0:n], ALU.subtract)
                    ins.then_inc(sem["centered" if c == 0 else "free0"], 1)
                dve.wait_ge(sem["free0"], at_bank(st, 0, 1))
                step(dve.reciprocal(u_rstd[:, 0:n], u_rstd[:, 0:n]))
                for c in range(2):
                    dve.tensor_tensor(HT[:, 2 + c, 0:n], HT[:, 2 + c, 0:n], u_rstd[:, 0:n], ALU.mult)\
                       .then_inc(sem["normed"], 1)

            def w_out(st):
                dve.wait_ge(sem["rows_loaded"], st.at("rows_loaded", 32))
                for i in range(st.facts["tiles"]):
                    b = 2 * (i % 4)
                    dve.wait_ge(sem[f"full{b}"], at_bank(st, b, i // 4))
                    dve.tensor_tensor(h_tok[:, i % 2, :], flat_bank[:, b * BANK:b * BANK + D],
                                      mod[:, 0 if i < ST else 1, :], ALU.mult).then_inc(sem[f"free{b}"], 1)
                    dve.wait_ge(sem[f"free{b}"], at_bank(st, b, i // 4))
                    step(dve.tensor_tensor(X[:, i, :], X[:, i, :], h_tok[:, i % 2, :], ALU.add))

            def route(st):
                tiles = st.facts["tiles"]
                dve.wait_ge(sem["full0"], at_bank(st, 0, 0))
                logits = bank[:, 0, 0:tiles * EXPERTS].rearrange("p (t e) -> p t e", e=EXPERTS)
                v = aff[:, 0:tiles, :]
                step(dve.tensor_reduce(small[:, 0:tiles], logits, AX.X, ALU.max))
                dve.tensor_tensor(v, logits, per_row(small[:, 0:tiles], tiles, EXPERTS), ALU.subtract)\
                   .then_inc(sem["free0"], 1)
                dve.wait_ge(sem["logit_exp"], st.at("logit_exp", 1))
                step(dve.tensor_reduce(small[:, 8:8 + tiles], v, AX.X, ALU.add))
                step(dve.reciprocal(small[:, 16:16 + tiles], small[:, 8:8 + tiles]))
                dve.tensor_tensor(v, v, per_row(small[:, 16:16 + tiles], tiles, EXPERTS), ALU.mult)\
                   .then_inc(sem["affinity"], 1)
                places = y_rows[0:EXPERTS, 0:NS].bitcast(U32)
                for part, (lo, hi, cap, c0) in enumerate(((0, SEQ, CAP_X, 0), (SEQ, NTOK, CAP_C, CAP_X))):
                    if part * ST >= tiles:
                        continue
                    b = 1 + part
                    values = affT[0:EXPERTS, lo:hi]
                    dve.wait_ge(sem[f"full{b}"], at_bank(st, b, 0))
                    dve.tensor_copy(values, bank[0:EXPERTS, b, 0:hi - lo]).then_inc(sem[f"free{b}"], 1)
                    dve.wait_ge(sem[f"free{b}"], at_bank(st, b, 0))
                    for r in range(cap // 8):
                        cols = slice(c0 + 8 * r, c0 + 8 * r + 8)
                        step(dve.max(top[0:EXPERTS, cols], values))
                        step(dve.max_index(places[:, cols], top[0:EXPERTS, cols], values))
                        step(dve.match_replace(values, top[0:EXPERTS, cols], values, -1.0))
                n = NS if tiles > ST else CAP_X
                ins = dve.tensor_copy(top_at[0:EXPERTS, 0:n], places[:, 0:n])
                if tiles > ST:
                    step(ins)
                    v = top_at[0:EXPERTS, CAP_X:NS]
                    ins = dve.tensor_scalar(v, v, float(SEQ), None, ALU.add)
                ins.then_inc(sem["ranked"], 1)
                dve.wait_ge(sem["full3"], at_bank(st, 3, 0))
                dve.tensor_copy(index_t[0:n, 0:EXPERTS], bank[0:n, 3, 0:EXPERTS])
                dve.tensor_copy(index_t[0:n, EXPERTS:EXPERTS + 1], bank[0:n, 3, 0:1])
                dve.tensor_copy(gate_t[0:n, :], bank[0:n, 3, EXPERTS:2 * EXPERTS]).then_inc(sem["free3"], 1)

            def experts(st):
                n = NS if st.facts["tiles"] > ST else CAP_X

                def take_rows(e):
                    dve.wait_ge(sem["full1"], at_bank(st, 1, e))
                    dve.tensor_copy(xsT[:, 4:8, 0:n], bank[:, 1, 0:4 * n].rearrange("p (k n) -> p k n", k=4))\
                       .then_inc(sem["free1"], 1)

                take_rows(0)
                with dve.Fori(0, EXPERTS) as e:
                    step.begin_loop(e, 1)
                    dve.wait_ge(sem["full7"], st.at("bank7", e))
                    for half in range(2):
                        b = 3 + 2 * half
                        dve.wait_ge(sem[f"free{b - 1}"], at_bank(st, b - 1, e))
                        dve.wait_ge(sem[f"full{b}"], at_bank(st, b, e))
                        dve.tensor_tensor(actT[:, 4 * half:4 * half + 4, 0:n],
                                          bank[:, b, 0:4 * n].rearrange("p (k n) -> p k n", k=4),
                                          gateT[:, half, 0:4 * n].rearrange("p (k n) -> p k n", k=4), ALU.mult)\
                           .then_inc(sem[f"free{b}"], 1)
                    take_rows(e + 1)
                    step(dve.tensor_copy(now[0:n, 0:1], gate_t[0:n, bass.ds(e, 1)]))
                    dve.wait_ge(sem["scattered"], st.at("scattered", 0) + e * 16)
                    for j in range(2):
                        dve.wait_ge(sem[f"full{6 + j}"], at_bank(st, 6 + j, e))
                        dve.tensor_scalar(y_rows[0:n, 512 * j:512 * j + 512], bank[0:n, 6 + j, :], now[0:n, 0:1], None,
                                          ALU.mult).then_inc(sem[f"free{6 + j}"], 1)
                step.end_loop(EXPERTS)

            def combine(st):
                dve.wait_ge(sem["rows_loaded"], st.at("rows_loaded", 32))
                for i in range(st.facts["tiles"]):
                    q = i % 2
                    dve.wait_ge(sem[f"moe_rows{q}"], st.at(f"moe_rows{q}", 16 * (i // 2 + 1)))
                    h = h_tok[:, q, :]
                    step(dve.tensor_tensor(h, h, mod[:, 0 if i < ST else 1, :], ALU.mult))
                    dve.tensor_tensor(X[:, i, :], X[:, i, :], h, ALU.add).then_inc(sem["added"], 1)

            def norm_rows(st):
                dve.wait_ge(sem["rows_loaded"], st.at("rows_loaded", 16))
                for t in range(ST):
                    dve.wait_ge(sem["mean_root"], st.at("mean_root", t + 1))
                    step(dve.reciprocal(small[:, 16 + t:17 + t], small[:, 8 + t:9 + t]))
                    step(dve.scalar_tensor_tensor(X[:, t, :], X[:, t, :], small[:, 16 + t:17 + t], mod[:, 0, :],
                                                  ALU.mult, ALU.mult))

            def angles(st):
                dve.wait_ge(sem["tables_loaded"], st.at("tables_loaded", 16 * 5))
                step(dve.tensor_tensor(lam_in[:, 0:2, :], lam_in[:, 0:2, :], lam_in[:, 2:4, :], ALU.mult))
                dve.tensor_reduce(lam[:, 0:2], lam_in[:, 0:2, :], AX.X, ALU.add).then_inc(sem["lam_sum"], 1)
                step(dve.tensor_copy(pos_f, positions))
                step(dve.tensor_tensor(angle, pos_f.unsqueeze(2).broadcast_to([P, ST, ANGLES]),
                                       freq.unsqueeze(1).broadcast_to([P, ST, ANGLES]), ALU.mult))
                turn = 2 * np.pi
                parts = [6.28125]
                parts.append(float(np.float32(np.round((turn - parts[0]) * 2 ** 21) / 2 ** 21)))
                parts.append(float(np.float32(turn - parts[0] - parts[1])))
                for table, quarter in ((sin2, 0.0), (cos2, 0.25)):
                    v = table[:, :, :]
                    step(dve.tensor_scalar(whole, angle, float(1 / turn), quarter, ALU.mult, ALU.add))
                    step(dve.tensor_scalar(whole, whole, ROUND, None, ALU.add))
                    step(dve.tensor_scalar(whole, whole, ROUND, None, ALU.subtract))
                    source = angle
                    for part in parts:
                        step(dve.scalar_tensor_tensor(v, whole, -part, source, ALU.mult, ALU.add))
                        source = v
                    step(dve.tensor_scalar(v, v, float(quarter * turn), None, ALU.add))
                    ins = dve.tensor_scalar(v, v, 3.1415925, -3.1415925, ALU.min, ALU.max)
                    if table is sin2:
                        step(ins)
                ins.then_inc(sem["angles"], 1)
                dve.wait_ge(sem["lam_exp"], st.at("lam_exp", 1))
                step(dve.tensor_tensor(lam[:, 2:3], lam[:, 1:2], lam[:, 0:1], ALU.subtract))
                step(dve.tensor_scalar(lam[:, 2:3], lam[:, 2:3], LAM_INIT, None, ALU.subtract))
                step(dve.tensor_scalar(subln[:, :], subln[:, :], 1.0 - LAM_INIT, None, ALU.mult))

            def ffn_up(st):
                for c in range(F_CHUNKS):
                    b = 2 * (c % 4)
                    dve.wait_ge(sem[f"free{b}"], at_bank(st, b, c // 4))
                    dve.wait_ge(sem[f"full{b + 1}"], at_bank(st, b + 1, c // 4))
                    dve.tensor_tensor(ffnT[:, c, :], bank[:, b + 1, :], ffn_gate[:, c % 2, :], ALU.mult)\
                        .then_inc(sem[f"free{b + 1}"], 1)

            def ffn_down(st):
                for half in range(2):
                    for t in range(ST):
                        b = 4 * half + t
                        v = X[:, t, 512 * half:512 * half + 512]
                        dve.wait_ge(sem[f"full{b}"], at_bank(st, b, 0))
                        dve.scalar_tensor_tensor(v, bank[:, b, :], 0.5, v, ALU.mult, ALU.add).then_inc(sem[f"free{b}"], 1)

            def rotate(i, dst, src, heads, half, first):
                def per_head(table):
                    return table[:, i, first:first + half].unsqueeze(1).broadcast_to([P, heads, half])

                def temp(v):
                    return v[:, 0:heads * half].rearrange("p (h d) -> p h d", d=half)
                x1, x2 = src[:, :, 0:half], src[:, :, half:2 * half]
                ta, tb = temp(turn_a), temp(turn_b)
                step(dve.tensor_tensor(ta, x2, per_head(sin2), ALU.mult))
                step(dve.tensor_tensor(tb, x1, per_head(sin2), ALU.mult))
                step(dve.tensor_tensor(dst[:, :, 0:half], x1, per_head(cos2), ALU.mult))
                step(dve.tensor_tensor(dst[:, :, half:2 * half], x2, per_head(cos2), ALU.mult))
                step(dve.tensor_tensor(dst[:, :, 0:half], dst[:, :, 0:half], ta, ALU.subtract))
                return dve.tensor_tensor(dst[:, :, half:2 * half], dst[:, :, half:2 * half], tb, ALU.add)

            def latent_in(st):
                for i in range(ST):
                    b = i % 2
                    dve.wait_ge(sem["latent_root"], st.at("latent_root", 2 * i + 2))
                    r = small[:, 32 + 2 * i:34 + 2 * i]
                    step(dve.reciprocal(r, small[:, 16 + 2 * i:18 + 2 * i]))
                    if i >= 2:
                        dve.wait_ge(sem[f"full{2 + b}"], at_bank(st, 2 + b, i // 2 - 1))
                    step(dve.tensor_scalar(z_lat[:, b, 0:Q_RANK], bank[:, b, 0:Q_RANK], r[:, 0:1], None, ALU.mult))
                    dve.tensor_scalar(z_lat[:, b, Q_RANK:Q_RANK + KV_RANK], bank[:, b, Q_RANK:Q_RANK + KV_RANK], r[:, 1:2],
                                      None, ALU.mult).then_inc(sem["latent"], 1)
                    step(dve.tensor_copy(z_lat[:, b, Q_RANK + KV_RANK:LATENT], bank[:, b, Q_RANK + KV_RANK:LATENT]))
                    step(rotate(i, rot_k[:, i:i + 1, :], z_lat[:, b, Q_RANK + KV_RANK:LATENT].unsqueeze(1), 1, ROT // 2, 0))
                    dve.memset(small[:, 90:91], 0.0).then_inc(sem[f"free{b}"], 1)

            def latent_qk(st):
                for i in range(ST):
                    q = q_rows[:, i % 2, :].rearrange("p (h d) -> p h d", d=L_QK)
                    k = k_rows[:, i % 2, :].rearrange("p (h d) -> p h d", d=L_QK)
                    if i >= 2:
                        for b in range(4, 8):
                            dve.wait_ge(sem[f"full{b}"], at_bank(st, b, i - 2))
                    dve.wait_ge(sem["full0"], at_bank(st, 0, i))
                    dve.tensor_copy(q_rows[:, i % 2, :], flat_bank[:, 0:L_HEADS * L_QK]).then_inc(sem["free0"], 1)
                    dve.wait_ge(sem["free0"], at_bank(st, 0, i))
                    rotate(i, q[:, :, NOPE:L_QK], q[:, :, NOPE:L_QK], L_HEADS, ROT // 2, 0).then_inc(sem["q_rows"], 1)
                    dve.wait_ge(sem["q_rows"], st.at("q_rows", i + 1))
                    kv = flat_bank[:, 2 * BANK:2 * BANK + L_HEADS * (NOPE + L_V)].rearrange("p (h d) -> p h d", h=L_HEADS)
                    dve.wait_ge(sem["full2"], at_bank(st, 2, i))
                    dve.tensor_copy(k[:, :, 0:NOPE], kv[:, :, 0:NOPE])
                    dve.tensor_copy(v_lat[:, i, :].rearrange("p (h d) -> p h d", h=L_HEADS), kv[:, :, NOPE:])\
                        .then_inc(sem["free2"], 1)
                    dve.tensor_copy(k[:, :, NOPE:L_QK], rot_k[:, i:i + 1, :].broadcast_to([P, L_HEADS, ROT]))\
                        .then_inc(sem["k_rows"], 1)

            def diff_in(st):
                for i in range(ST):
                    rows = qk_diff[:, i % 2, :]
                    heads = rows.rearrange("p (h d) -> p h d", d=HD)
                    if i >= 2:
                        for b in (4, 5):
                            dve.wait_ge(sem[f"full{b}"], at_bank(st, b, i - 2))
                    dve.wait_ge(sem["full0"], at_bank(st, 0, i))
                    dve.tensor_copy(rows, flat_bank[:, 0:2 * D_W]).then_inc(sem["free0"], 1)
                    dve.wait_ge(sem["free0"], at_bank(st, 0, i))
                    n = 2 * D_W // HD
                    rotate(i, heads[:, :, 0:D_ROT], heads[:, :, 0:D_ROT], n, D_ROT // 2, ROT // 2)\
                        .then_inc(sem["qk_rows"], 1)
                    dve.wait_ge(sem["qk_rows"], st.at("qk_rows", i + 1))

            def attend_two(st):
                units = units_two()
                scales = (L_QK ** -0.5, HD ** -0.5)

                def maximum(i):
                    kind, qt, h, s = units[i]
                    n, b = (qt + 1) * P, i % 2
                    dve.wait_ge(sem[f"full{b}"], at_bank(st, b, i // 2))
                    m = small[:, 40 + i % 8:41 + i % 8]
                    step(dve.tensor_reduce(m, bank[:, b, 0:n], AX.X, ALU.max))
                    dve.tensor_scalar(small[:, i % 8:i % 8 + 1], m, -scales[kind], None, ALU.mult).then_inc(sem["neg_max"], 1)

                def take_probs(i):
                    n, b = (units[i][1] + 1) * P, 2 + i % 2
                    dve.wait_ge(sem[f"full{b}"], at_bank(st, b, i // 2))
                    dve.tensor_copy(probs2T[:, i % 2, 0:n], bank[:, b, 0:n]).then_inc(sem[f"free{b}"], 1)

                def rows_of_y(g):
                    kind = units[2 * g][0]
                    b = 4 + g % 2
                    c = 2 * (g % 4)
                    r = small[:, 24 + c:26 + c]
                    y = y_rows2[:, g % 2, :]
                    dve.wait_ge(sem[f"full{b}"], at_bank(st, b, g // 2))
                    step(dve.reciprocal(r, small[:, 16 + c:18 + c]))
                    if g >= 2:
                        dve.wait_ge(sem[f"full{6 + g % 2}"], at_bank(st, 6 + g % 2, g // 2 - 1))
                    if kind == 0:
                        step(dve.tensor_tensor(y.rearrange("p (s d) -> p s d", s=2),
                                               bank[:, b, 0:P].rearrange("p (s d) -> p s d", s=2), per_row(r, 2, L_V), ALU.mult))
                    else:
                        step(dve.tensor_tensor(small[:, 60:61], r[:, 1:2], lam[:, 2:3], ALU.mult))
                        step(dve.tensor_scalar(y, bank[:, b, 0:P], r[:, 0:1], None, ALU.mult))
                        step(dve.scalar_tensor_tensor(y, bank[:, b, P:2 * P], small[:, 60:61], y, ALU.mult, ALU.add))
                        step(dve.tensor_tensor(squares2[:, :], y, y, ALU.mult))
                        k = g - 4 * L_HEADS // 2
                        dve.tensor_reduce(small[:, 62 + g % 2:63 + g % 2], squares2[:, :], AX.X, ALU.add).then_inc(sem["y_sum"], 1)
                        dve.wait_ge(sem["y_root"], st.at("y_root", k + 1))
                        step(dve.reciprocal(small[:, 66:67], small[:, 64 + g % 2:65 + g % 2]))
                        step(dve.scalar_tensor_tensor(y, y, small[:, 66:67], subln[:, :], ALU.mult, ALU.mult))
                    dve.memset(small[:, 90:91], 0.0).then_inc(sem[f"free{b}"], 1)
                    dve.wait_ge(sem[f"free{b}"], at_bank(st, b, g // 2))
                    dve.memset(small[:, 90:91], 0.0).then_inc(sem["y_rows"], 1)
                    dve.wait_ge(sem["y_rows"], st.at("y_rows", g + 1))

                n = len(units)
                for i in range(n + 2):
                    if i < n:
                        maximum(i)
                    if 1 <= i <= n:
                        take_probs(i - 1)
                    if i >= 2 and (i - 2) % 2 == 1:
                        rows_of_y((i - 2) // 2)

            def merge(st):
                for c in range(KD):
                    b, use = 4 * (c % 2), c // 2
                    gates = merge_gate[:, c % 2, :].rearrange("p (a n) -> p a n", a=2)
                    out_ = mergedT[:, c, :]
                    for n in range(2):
                        dve.wait_ge(sem[f"free{b + 2 * n}"], at_bank(st, b + 2 * n, use))
                        dve.wait_ge(sem[f"full{b + 2 * n + 1}"], at_bank(st, b + 2 * n + 1, use))
                        dve.tensor_tensor(gates[:, n, :] if n else out_, bank[:, b + 2 * n + 1, :], gates[:, n, :], ALU.mult)\
                            .then_inc(sem[f"free{b + 2 * n + 1}"], 1)
                    dve.wait_ge(sem[f"free{b + 3}"], at_bank(st, b + 3, use))
                    dve.tensor_tensor(out_, out_, gates[:, 1, :], ALU.add).then_inc(sem["merged"], 1)

            def project(st):
                for i in range(ST):
                    b = 2 * i
                    dve.wait_ge(sem[f"full{b}"], at_bank(st, b, 0))
                    dve.tensor_tensor(X[:, i, :], X[:, i, :], flat_bank[:, b * BANK:b * BANK + D], ALU.add)\
                        .then_inc(sem[f"free{b}"], 1)

            programs = dict(init=init, ada=ada, norm=norm, conv_in=conv_in, qkv=qkv, attend=attend, conv_out=conv_out,
                            w_out=w_out, route=route, experts=experts, combine=combine, norm_rows=norm_rows,
                            angles=angles, ffn_up=ffn_up, ffn_down=ffn_down, latent_in=latent_in, latent_qk=latent_qk,
                            diff_in=diff_in, attend_two=attend_two, merge=merge, project=project)
            for st in stages:
                enter(dve, st)
                if st.name in programs:
                    programs[st.name](st)
                dve.memset(done_mark[:, 1:2], 0.0).then_inc(sem["vector_finished"], 1)

        @block.gpsimd
        def _(pool):
            step = Steps(pool, sem["gpsimd_steps"])

            def init(st):
                step(pool.memset(eps[:, :], EPS))
                count = 0
                for dst, src in (
                        (silu_c, a["c_pair"]), (ident, a["ident"]), (band, a["band"]), (rope_cos, a["rope_cos"]),
                        (rope_sin, a["rope_sin"]), (head_gain, a["head_gain"]), (conv_a_w, a["conv_a_w"]),
                        (conv_b_w, a["conv_b_w"]), (conv_vec, a["conv_vec"]), (sink, a["sink"]), (router, a["router_w"])):
                    pool.dma_start(dst[tuple([slice(None)] * len(dst.shape))], src).then_inc(sem["constants"], 16)
                    count += 1
                pool.dma_start(X[:, 0:ST, :], a["x"].rearrange("(t p) d -> p t d", p=P)).then_inc(sem["constants"], 16)
                pool.dma_start(X[:, ST:ST + CT, :], a["ctx"].rearrange("(t p) d -> p t d", p=P)).then_inc(sem["constants"], 16)
                assert count + 2 == CONSTANTS
                pool.wait_ge(sem["constants"], CONSTANTS * 16)
                step(pool.memset(h_tok[:, 0, :], 0.0))
                for l in range(LAYERS):
                    for t in range(ST + CT if l == 0 else ST):
                        pool.dma_start(moe_rows[l][t * P:(t + 1) * P, :], h_tok[:, 0, :]).then_inc(sem["moe_cleared"], 16)
                pool.wait_ge(sem["moe_cleared"], 16 * (ST + CT + ST))

            def load_mods(st, rows):
                for n, (row, comp) in enumerate(rows):
                    pool.dma_start(mod[:, n, :], mods_rows[st.layer][row, comp * D:comp * D + D].partition_broadcast(P))\
                        .then_inc(sem["rows_loaded"], 16)

            def ada(st):
                pool.dma_start(ada_bias[0:2, :], a["ada_b"][st.layer]).then_inc(sem["rows_loaded"], 16)
                pool.dma_start(norm_gain[0:2, :, :], a["norm_gains"][st.layer]).then_inc(sem["rows_loaded"], 16)
                pool.wait_ge(sem["mods_rows"], st.at("mods_rows", 1))
                pool.dma_start(mods_rows[st.layer], HT[0:2, :, :].rearrange("p k n -> p (k n)")).then_inc(sem["mods_stored"], 16)
                pool.wait_ge(sem["mods_stored"], st.at("mods_stored", 16))

            def norm(st):
                tiles, row = st.facts["tiles"], st.facts["row"]
                if st.facts["shift"] is not None:
                    load_mods(st, [(row, st.facts["scale"]), (row, st.facts["shift"])])
                if st.facts["store"]:
                    for i, t in enumerate(tiles):
                        pool.wait_ge(sem["h_ready"], st.at("h_ready", i + 1))
                        pool.dma_start(h_rows[st.layer][t * P:(t + 1) * P, :], h_tok[:, i % 2, :])\
                            .then_inc(sem[f"h_stored{i % 2}"], 16)
                    for q in range(2):
                        pool.wait_ge(sem[f"h_stored{q}"], st.at(f"h_stored{q}", 16 * len(tiles[q::2])))
                elif st.facts["shift"] is None:
                    pool.dma_start(mod[:, 0, :], a[st.facts["gain"]].partition_broadcast(P)).then_inc(sem["rows_loaded"], 16)
                pool.wait_ge(sem["rows_loaded"], st.at("rows_loaded", st.signals["rows_loaded"]))

            def angles(st):
                for dst, src in ((positions, a["positions_2"]), (freq, a["freq"]), (lam_in, a["lam_2"]),
                                 (latent_gain[:, :], a["latent_gain"]), (subln[:, :], a["subln_2"])):
                    pool.dma_start(dst, src).then_inc(sem["tables_loaded"], 16)
                pool.wait_ge(sem["tables_loaded"], st.at("tables_loaded", 16 * 5))

            def attend(st):
                l = st.layer
                parts = [(0, SEQ)] + ([(SEQ, NTOK)] if l == 0 else [])
                for part, (lo, hi) in enumerate(parts):
                    n = hi - lo
                    for c, source, weights, taps, pad, dst in (
                            (0, conv_a_in, conv_a_w, TAPS_A, PAD_A, HT[:, 0, lo:hi]),
                            (1, conv_a_in, conv_a_w, TAPS_A, PAD_A, HT[:, 1, lo:hi]),
                            (0, conv_b_in, conv_b_w, TAPS_B, PAD_B, HT[:, 2, lo:hi])):
                        start = part * (SEQ + 2 * pad)

                        def tap(k, dst):
                            return pool.tensor_tensor(dst, source[:, c, start + k:start + k + n],
                                                      weights[:, l, c, k:k + 1].broadcast_to([P, n]), ALU.mult)

                        step.later(tap(0, dst))
                        step.later(tap(1, tap_out[:, 1, 0:n]))
                        for k in range(1, taps):
                            if k + 1 < taps:
                                step.later(tap(k + 1, tap_out[:, (k + 1) % 3, 0:n]))
                            step.wait_for(1 if k + 1 < taps else 0)
                            step.later(pool.tensor_tensor(dst, dst, tap_out[:, k % 3, 0:n], ALU.add))
                        step.wait_for(0)
                        other = conv_vec[:, 0, l, 0:1].broadcast_to([P, n]) if taps == TAPS_B else conv_a_gate[:, c, lo:hi]
                        step(pool.tensor_tensor(dst, dst, other, ALU.add if taps == TAPS_B else ALU.mult))

            def w_out(st):
                load_mods(st, [(0, 2), (1, 2)])
                pool.wait_ge(sem["rows_loaded"], st.at("rows_loaded", 32))

            def experts(st):
                n = NS if st.facts["tiles"] > ST else CAP_X
                tail = now.bitcast(U32)
                tokens = st.facts["tiles"] * P
                rows, sums = h_rows[st.layer][0:tokens, :], moe_rows[st.layer][0:tokens, :]

                def gather(index):
                    pool.indirect_dma_start(xs[0:n, :], None, rows, bass.IndirectOffsetOnAxis(ap=index, axis=0))\
                        .then_inc(sem["gathered"], 16)

                def index_ready():
                    step.later(pool.tensor_tensor(done_mark[:, 3:4], eps[:, :], eps[:, :], ALU.add))

                gather(index_t[0:n, 0:1])
                with pool.Fori(0, EXPERTS) as e:
                    step.begin_loop(e, 4)
                    pool.wait_ge(sem["full1"], at_bank(st, 1, e))
                    pool.wait_ge(sem["full0"], at_bank(st, 0, e))
                    step(pool.tensor_copy(tail[0:n, 1:2], index_t[0:n, bass.ds(e + 1, 1)]))
                    index_ready()
                    gather(tail[0:n, 1:2])
                    step(pool.tensor_copy(tail[0:n, 2:3], index_t[0:n, bass.ds(e, 1)]))
                    for j in range(2):
                        pool.wait_ge(sem[f"free{6 + j}"], at_bank(st, 6 + j, e))
                    index_ready()
                    pool.indirect_dma_start(sums, bass.IndirectOffsetOnAxis(ap=tail[0:n, 2:3], axis=0), y_rows[0:n, :],
                                            None, compute_op=ALU.add).then_inc(sem["scattered"], 16)
                    pool.wait_ge(sem["scattered"], st.at("scattered", 16) + e * 16)
                step.end_loop(EXPERTS)
                pool.wait_ge(sem["gathered"], st.at("gathered", 16 * (EXPERTS + 1)))

            def combine(st):
                load_mods(st, [(0, 5), (1, 5)])
                for i in range(st.facts["tiles"]):
                    q = i % 2
                    if i >= 2:
                        pool.wait_ge(sem["added"], st.at("added", i - 1))
                    pool.dma_start(h_tok[:, q, :], moe_rows[st.layer][i * P:(i + 1) * P, :]).then_inc(sem[f"moe_rows{q}"], 16)
                pool.wait_ge(sem["rows_loaded"], st.at("rows_loaded", 32))

            def store(st):
                pool.dma_start(out.rearrange("(t p) d -> p t d", p=P), X[:, 0:ST, :]).then_inc(sem["stored"], 16)
                pool.wait_ge(sem["stored"], 16)

            programs = dict(init=init, ada=ada, norm=norm, attend=attend, w_out=w_out, experts=experts,
                            combine=combine, store=store, norm_rows=norm, angles=angles)
            for st in stages:
                enter(pool, st)
                if st.name in programs:
                    programs[st.name](st)
                pool.memset(done_mark[:, 2:3], 0.0).then_inc(sem["gpsimd_finished"], 1)


CONSTANTS = 13


def rope_tables():
    quarter = HD // 4
    inv = np.float32(10000.0) ** (-np.arange(quarter, dtype=np.float32) / np.float32(quarter))
    row = np.repeat(np.arange(SEQ // GRID_W), GRID_W).astype(np.float32)
    col = (np.arange(SEQ) % GRID_W).astype(np.float32)
    ar, ac = row[:, None] * inv, col[:, None] * inv
    ang = np.concatenate([ar, ar, ac, ac], axis=-1)
    sign = np.repeat(np.array([-1, 1, -1, 1], np.float32), quarter)
    return np.cos(ang), np.sin(ang) * sign


def host_arrays(i):
    def tiles(v):
        return np.ascontiguousarray(v.reshape(ST, P, -1).transpose(1, 0, 2))

    def by_channel(v):
        v = v.reshape(LAYERS, 2, P, *v.shape[2:])
        return np.ascontiguousarray(np.moveaxis(v, 2, 0))

    cos, sin = rope_tables()
    j, q = np.arange(P)[None, :], np.arange(P)[:, None]
    band = np.stack([np.where(j >= q, 0.0, MASKED), np.where(j <= q, 0.0, MASKED)], 1).astype(np.float32)
    pair = np.stack([i["c"].reshape(D), i["c_ctx"]])
    gains = np.concatenate([np.repeat(i["q_norm_g"][:, None], 4, 1), np.repeat(i["k_norm_g"][:, None], 2, 1)], 1)
    host = dict(
        x=i["x"][0], ctx=i["ctx"][0], c_pair=np.ascontiguousarray(pair.reshape(2, KD, P).transpose(2, 1, 0)),
        ident=np.eye(P, dtype=np.float32), band=band, rope_cos=tiles(cos), rope_sin=tiles(sin),
        head_gain=np.ascontiguousarray(np.broadcast_to(gains[None], (P, LAYERS, 6, HD))),
        conv_a_w=by_channel(i["conv_a_w"].transpose(0, 2, 1)), conv_b_w=by_channel(i["conv_b_w"].transpose(0, 2, 1)),
        conv_vec=np.ascontiguousarray(np.stack([by_channel(i[n]) for n in ("conv_b_b", "conv_ln_g", "conv_ln_b")], 1)),
        sink=np.ascontiguousarray(np.broadcast_to(i["sink"][None], (P, LAYERS, HEADS))),
        router_w=np.ascontiguousarray(i["router_w"].reshape(LAYERS, KD, P, EXPERTS).transpose(2, 0, 1, 3)),
        ada_b=np.ascontiguousarray(np.broadcast_to(i["ada_b"][:, None], (LAYERS, 2, 6 * D))),
        norm_gains=np.ascontiguousarray(np.broadcast_to(
            np.stack([i["norm1_g"], i["norm2_g"]], 1)[:, None], (LAYERS, 2, 2, D))))
    inv = np.concatenate([np.power(np.float32(THETA), np.float32(-2.0) * np.arange(r // 2, dtype=np.float32) / np.float32(r))
                          for r in (ROT, D_ROT)]).astype(np.float32)
    lams = np.stack([i[f"diff_lam_{n}_2"][0] for n in ("q1", "q2", "k1", "k2")])

    def rows(v):
        return np.ascontiguousarray(np.broadcast_to(v[None], (P, *v.shape)))

    host.update(
        freq=rows(inv), lam_2=rows(lams), subln_2=rows(i["diff_subln_2"][0]),
        positions_2=np.ascontiguousarray(i["positions_2"].reshape(ST, P).T),
        latent_gain=np.ascontiguousarray(np.concatenate([i["mla_q_norm_2"][0], i["mla_kv_norm_2"][0]]).reshape(3, P).T),
        w_proj_2=np.concatenate([i["w_proj_mla_2"][0], i["w_proj_diff_2"][0]]), final_g=i["final_g"],
        ffn1_norm_2=i["ffn1_norm_2"][0], mix_norm_2=i["mix_norm_2"][0], ffn2_norm_2=i["ffn2_norm_2"][0],
        final_norm_2=i["final_norm_2"])
    for name in ("ffn1_w_gate_2", "ffn1_w_up_2", "ffn1_w_down_2", "w_in_2", "mla_w_uq_2", "mla_w_ukv_2", "w_out_2",
                 "ffn2_w_gate_2", "ffn2_w_up_2", "ffn2_w_down_2"):
        host[name] = i[name][0]
    for name in ("ada_w", "w_in", "w_out", "w_gate", "w_up", "w_down"):
        host[name] = i[name]
    return host


def kernel(**inputs):
    import concourse.bacc as bacc
    from concourse.bass_utils import run_bass_kernel_spmd

    host = host_arrays({name: np.asarray(v) for name, v in inputs.items()})
    nc = bacc.Bacc("TRN2", target_bir_lowering=False, num_devices=1)
    arrays, dram = {}, {}
    for name, v in host.items():
        v = np.ascontiguousarray(v)
        arrays[f"in_{name}_dram"] = v
        dram[name] = nc.dram_tensor(f"in_{name}_dram", v.shape, mybir.dt.from_np(v.dtype), kind="ExternalInput").ap()
    out = nc.dram_tensor("out_dram", (SEQ, D), F32, kind="ExternalOutput").ap()
    stages = [Stage("init")] + block_one_stages(dram) + block_two_stages(dram)
    place_stages(stages)
    two_blocks_kernel(nc, dram, out, stages)
    result = run_bass_kernel_spmd(nc, [arrays], core_ids=[0])
    return result.results[0]["out_dram"].reshape(1, SEQ, D)
```

```python
from contextlib import ExitStack

import numpy as np
import concourse.bass as bass
from concourse import mybir

F32 = mybir.dt.float32
U32 = mybir.dt.uint32
I32 = mybir.dt.int32
F32R = mybir.dt.float32r
BF16 = mybir.dt.bfloat16
ALU = mybir.AluOpType
ACT = mybir.ActivationFunctionType
AX = mybir.AxisListType

P = 128
D = 1024
KD = D // P
SEQ = 512
CTX = 256
ST = SEQ // P
CT = CTX // P
NTOK = SEQ + CTX
LAYERS = 2
HD = 64
HEADS = 4
EPS = 1e-6
GRID_W = 64
EXPERTS = 16
CAP_X = 2 * SEQ // EXPERTS
CAP_C = 2 * CTX // EXPERTS
TAPS_A = 3
TAPS_B = 31
CONV_COLS = 5 * (D // 4)
BANKS = 8
BANK = 512
SLOTS = 4
SLOT = KD * 512
MASKED = -1.0e30

D_FF = 2816
F_CHUNKS = D_FF // P
SPLIT_RING = 8
Q_RANK, KV_RANK = 256, 128
L_HEADS, NOPE, ROT, L_V = 8, 64, 32, 64
L_QK = NOPE + ROT
LATENT = Q_RANK + KV_RANK + ROT
D_HEADS, D_ROT = 4, 16
D_W = D_HEADS * 2 * HD
GATES = LATENT + 3 * D_W
THETA = 500000.0
ANGLES = ROT // 2 + D_ROT // 2
LAM_INIT = 0.2
ROUND = 12582912.0


class Stage:

    def __init__(self, name, layer=0, bank_uses=(), signals=None, units=(), repeat_units=0, **facts):
        self.name, self.layer, self.facts = name, layer, facts
        self.signals = dict(signals or {})
        for b, n in enumerate(bank_uses):
            if n:
                self.signals[f"bank{b}"] = n
        self.units = list(units)
        self.repeat_units = repeat_units
        self.base = {}
        self.number = 0

    def at(self, signal, n):
        return self.base.get(signal, 0) + n


def place_stages(stages):
    total = {}
    unit = 0
    for number, stage in enumerate(stages):
        stage.number = number
        stage.base = dict(total)
        stage.first_unit = unit
        unit += len(stage.units) + stage.repeat_units
        for name, n in stage.signals.items():
            total[name] = total.get(name, 0) + n
    return total


def heads_of(layer):
    tiles = ST + CT if layer == 0 else ST
    return [(qt, kind, h) for qt in range(tiles) for kind in range(2) for h in range(HEADS)]


def key_tiles(qt, kind):
    context = list(range(ST, ST + CT))
    if qt >= ST:
        return context
    if kind:
        return list(range(ST)) + context
    return list(range(max(0, qt - 1), min(ST, qt + 2))) + context


class Steps:

    def __init__(self, eng, sem):
        self.eng, self.sem, self.n, self.turns = eng, sem, 0, 0

    def __call__(self, ins):
        ins.then_inc(self.sem, 1)
        self.n += 1
        self.eng.wait_ge(self.sem, self.turns + self.n)

    def later(self, ins):
        ins.then_inc(self.sem, 1)
        self.n += 1

    def wait_for(self, behind):
        self.eng.wait_ge(self.sem, self.turns + self.n - behind)

    def begin_loop(self, turn, per_turn):
        self.turns, self.start, self.per_turn = turn * per_turn, self.n, per_turn

    def end_loop(self, turns):
        assert self.n - self.start == self.per_turn, (self.n - self.start, self.per_turn)
        self.n, self.turns = self.start + self.per_turn * turns, 0


def block_one_stages(a):
    stages = []

    def weight_unit(source, cols):
        lo, hi = cols

        def load(slot):
            out = slot.rearrange("p (k n) -> p k n", k=KD)[:, :, 0:hi - lo]
            return out, source[:, lo:hi].rearrange("(k p) n -> p k n", p=P)

        return load

    for l in range(LAYERS):
        tiles = ST + CT if l == 0 else ST
        all_tiles = ST + CT
        n_ada = 6 * D // 512
        if l:
            stages.append(Stage("angles", signals=dict(tables_loaded=16 * 5, angles=1, sines=1, lam_sum=1, lam_exp=1)))
        stages.append(Stage(
            "ada", l, bank_uses=[(n_ada - b + BANKS - 1) // BANKS for b in range(BANKS)],
            signals=dict(rows_loaded=32, mods_rows=1, mods_stored=16),
            units=[(weight_unit(a["ada_w"][l], (512 * n, 512 * n + 512)), (n % BANKS, n // BANKS))
                   for n in range(n_ada)]))
        for first, last, row in ((0, ST, 0), (ST, ST + CT, 1)):
            stages.append(norm_stage("norm", l, range(first, last), row=row, scale=1, shift=0, store=False))
        n_chunks = CONV_COLS // P
        parts = 2 if l == 0 else 1
        groups = n_chunks * parts
        spans = [(0, 512), (512, 1024), (1024, CONV_COLS)]
        units = []
        for lo, hi in spans:
            g = (hi // P) * parts - 1
            units.append((weight_unit(a["w_in"][l], (lo, hi)), (g % BANKS, g // BANKS)))
        stages.append(Stage("conv_in", l, bank_uses=[(groups - b + BANKS - 1) // BANKS for b in range(BANKS)],
                            units=units, parts=parts))
        last_pair = ((all_tiles - 1) % 3 * 2, (all_tiles - 1) // 3)
        stages.append(Stage(
            "qkv", l, bank_uses=[2, 0, 2, 0, 2, 0, all_tiles, all_tiles],
            signals=dict(head_sums=all_tiles, head_roots=all_tiles, qk_ready=all_tiles),
            units=[(weight_unit(a["w_in"][l], (CONV_COLS + 512 * j, CONV_COLS + 512 * j + 512)), last_pair)
                   for j in range(2)]))
        units = heads_of(l)
        n_units = len(units)
        groups = n_units // HEADS
        wide = [len(key_tiles(qt, kind)) > 4 for qt, kind, _ in units]
        sinks = sum(kind == 0 for _, kind, _ in units)
        stages.append(Stage(
            "attend", l, bank_uses=[n_units // 2, 0, n_units // 2, 0, n_units, sum(wide), groups, groups],
            signals=dict(neg_max=n_units, sink_exp=sinks),
            wide=wide))
        stages.append(Stage("conv_out", l, bank_uses=[2], signals=dict(centered=1, squared=2, normed=2)))
        uses = [0] * BANKS
        for i in range(tiles):
            uses[2 * (i % 4)] += 1
        last_pair = (2 * ((tiles - 1) % 4), (tiles - 1) // 4)
        stages.append(Stage(
            "w_out", l, bank_uses=uses, signals=dict(rows_loaded=32),
            units=[(weight_unit(a["w_out"][l], (512 * j, 512 * j + 512)), last_pair) for j in range(2)], tiles=tiles))
        stages.append(norm_stage("norm", l, range(0, ST), row=0, scale=4, shift=3, store=True))
        if l == 0:
            stages.append(norm_stage("norm", l, range(ST, ST + CT), row=1, scale=4, shift=3, store=True))
        stages.append(Stage("route", l, bank_uses=[1, 1, 1 if l == 0 else 0, 1],
                            signals=dict(logit_exp=1, affinity=1, ranked=1), tiles=tiles))
        uses = [EXPERTS + 1, EXPERTS + 1, EXPERTS, 2 * EXPERTS, EXPERTS, 2 * EXPERTS, EXPERTS, EXPERTS]
        stages.append(Stage("experts", l, bank_uses=uses, repeat_units=6 * EXPERTS,
                            signals=dict(gathered0=8 * EXPERTS + 16, gathered1=8 * EXPERTS + 16, scattered=16 * EXPERTS, y_free=EXPERTS + 2,
                                         x_high=2 * (EXPERTS + 1), w_high=12 * EXPERTS, w_split=12 * EXPERTS, half_read=6 * EXPERTS,
                                         act_high=2 * EXPERTS), tiles=tiles))
        stages.append(Stage("combine", l, signals=dict(rows_loaded=32, moe_rows0=16 * (tiles // 2), moe_rows1=16 * (tiles // 2), added=tiles), tiles=tiles))
    return stages


def block_two_stages(a):
    def unit(source, rows, cols):
        (r0, r1), (c0, c1) = rows, cols
        k = (r1 - r0) // P

        def load(slot):
            out = slot[:, 0:k * (c1 - c0)].rearrange("p (k n) -> p k n", k=k)
            return out, source[r0:r1, c0:c1].rearrange("(k p) n -> p k n", p=P)

        return load

    def gain_norm(gain, turned=True, split=False):
        st = norm_stage("norm" if turned else "norm_rows", 0, range(ST), row=0, scale=0, shift=None, store=False)
        st.facts["gain"] = gain
        st.facts["split"] = split
        if split:
            st.signals["h_high"] = 2 * ST
        if not turned:
            st.signals = dict(rows_loaded=16, mean_root=ST)
        return st

    def ffn(which):
        units = []
        for u in range((F_CHUNKS + 3) // 4):
            last = min(F_CHUNKS, 4 * u + 4) - 1
            for n, name in enumerate(("gate", "up")):
                units.append((unit(a[f"ffn{which}_w_{name}_2"], (0, D), (512 * u, 128 * (last + 1))),
                              (2 * (last % 4) + n, last // 4)))
        up = Stage("ffn_up", which, bank_uses=[len(range(b // 2, F_CHUNKS, 4)) for b in range(BANKS)],
                   signals=dict(w_high=2 * F_CHUNKS, w_split=2 * F_CHUNKS), units=units)
        units = []
        for k0 in range(0, F_CHUNKS, 4):
            k1 = min(F_CHUNKS, k0 + 4)
            reader = (BANKS - 1, 0) if k1 == F_CHUNKS else ("down_read", k1 - 1)
            units.append((unit(a[f"ffn{which}_w_down_2"], (k0 * P, k1 * P), (0, D)), reader))
        down = Stage("ffn_down", which, bank_uses=[1] * BANKS, units=units,
                     signals=dict(down_read=F_CHUNKS - 1, w_high=F_CHUNKS, w_split=F_CHUNKS))
        return [up, down]

    w_in = a["w_in_2"]
    merge_units = []
    for half in range(2):
        c = 4 * half + 3
        cols = (512 * half, 512 * half + 512)
        merge_units.append((unit(a["w_proj_2"], (0, D), cols), (4 * (c % 2) + 3, c // 2)))
        for n, start in enumerate((GATES, GATES + D)):
            merge_units.append((unit(w_in, (0, D), (start + cols[0], start + cols[1])), (4 * (c % 2) + 2 * n, c // 2)))
    groups = 4 * L_HEADS // 2 + 4 * D_HEADS
    n_units = 2 * groups
    last_pair = (2 * (ST - 1), 0)
    return [
        gain_norm("final_g", turned=False),
        gain_norm("ffn1_norm_2", split=True), *ffn(1),
        gain_norm("mix_norm_2"),
        Stage("latent_in", bank_uses=[ST // 2, ST // 2, ST // 2, ST // 2], signals=dict(latent_root=2 * ST, latent_sum=2 * ST, latent=ST),
              units=[(unit(w_in, (0, D), (0, LATENT)), ((ST - 1) % 2, (ST - 1) // 2))]),
        Stage("latent_qk", bank_uses=[ST, 0, ST, 0, ST, ST, ST, ST], signals=dict(q_rows=ST, k_rows=ST),
              units=[(unit(a["mla_w_uq_2"], (0, Q_RANK), (0, L_HEADS * L_QK)), (0, ST - 1)),
                     (unit(a["mla_w_ukv_2"], (0, KV_RANK), (0, L_HEADS * (NOPE + L_V))), (2, ST - 1))]),
        Stage("diff_in", bank_uses=[ST, 0, ST, 0, ST, ST], signals=dict(qk_rows=ST),
              units=[(unit(w_in, (0, D), (LATENT + D_W * j, LATENT + D_W * j + D_W)), (0 if j < 2 else 2, ST - 1))
                     for j in range(3)]),
        Stage("attend_two", bank_uses=[n_units // 2] * 4 + [groups // 2] * 4,
              signals=dict(neg_max=n_units, y_sum=4 * D_HEADS, y_root=4 * D_HEADS, y_rows=groups)),
        Stage("merge", bank_uses=[KD // 2] * BANKS,
              signals=dict(merged=KD, w_high=3 * KD, w_split=3 * KD, rows_high=2 * KD, rows_split=2 * KD), units=merge_units),
        Stage("project", bank_uses=[1, 0, 1, 0, 1, 0, 1, 0],
              units=[(unit(a["w_out_2"], (0, D), (512 * j, 512 * j + 512)), last_pair) for j in range(2)]),
        gain_norm("ffn2_norm_2", split=True), *ffn(2),
        gain_norm("final_norm_2", turned=False),
        Stage("store", signals=dict(stored=16)),
    ]


def units_two():
    latent = [(0, qt, 2 * pair + s, s) for qt in range(ST) for pair in range(L_HEADS // 2) for s in range(2)]
    diff = [(1, qt, h, s) for qt in range(ST) for h in range(D_HEADS) for s in range(2)]
    return latent + diff


def norm_stage(name, layer, tiles, row, scale, shift, store):
    tiles = list(tiles)
    uses = [0] * BANKS
    for i in range(len(tiles)):
        uses[2 * (i % 4)] += 1
        uses[2 * (i % 4) + 1] += 1
    signals = dict(rows_loaded=32 if shift is not None else 16, mean_root=len(tiles), h_ready=len(tiles))
    if store:
        for q in range(2):
            signals[f"h_stored{q}"] = 16 * len(tiles[q::2])
    return Stage(name, layer, bank_uses=uses, signals=signals, tiles=tiles, row=row, scale=scale, shift=shift, store=store)


def two_blocks_kernel(nc, a, out, stages):
    with ExitStack() as ctx:
        def sb(name, shape, dtype=F32):
            return ctx.enter_context(nc.sbuf_tensor(name, shape, dtype))

        class Semaphores(dict):

            def __missing__(self, name):
                self[name] = ctx.enter_context(nc.semaphore(name))
                return self[name]

        sem = Semaphores()

        mods_rows = [nc.dram_tensor(f"mods_rows{l}", [2, 6 * D], F32).ap() for l in range(LAYERS)]
        h_rows = [nc.dram_tensor(f"h_rows{l}", [NTOK, D], F32).ap() for l in range(LAYERS)]
        moe_rows = [nc.dram_tensor(f"moe_rows{l}", [NTOK, D], F32).ap() for l in range(LAYERS)]

        bank = ctx.enter_context(nc.psum_tensor("bank", [P, BANKS, BANK], F32))

        slots_at = (nc.sbuf_base + 31) // 32 * 32
        slots = sb("slots", [P, SLOTS, SLOT])
        X_at = (nc.sbuf_base + 31) // 32 * 32
        X = sb("X", [P, ST + CT, D])
        HT_at = (nc.sbuf_base + 31) // 32 * 32
        HT = sb("HT", [P, KD, NTOK])
        ident = sb("ident", [P, P])
        band = sb("band", [P, 2, P])
        mean_of = sb("mean_of", [P, P])
        rope_cos = sb("rope_cos", [P, ST, HD])
        rope_sin = sb("rope_sin", [P, ST, HD])
        head_gain = sb("head_gain", [P, LAYERS, 6, HD])
        conv_a_w = sb("conv_a_w", [P, LAYERS, 2, TAPS_A])
        conv_b_w = sb("conv_b_w", [P, LAYERS, 2, TAPS_B])
        conv_vec = sb("conv_vec", [P, 3, LAYERS, 2])
        sink = sb("sink", [P, LAYERS, HEADS])
        router = sb("router", [P, LAYERS, KD, EXPERTS])
        silu_c = sb("silu_c", [P, KD, 2])
        eps = sb("eps", [P, 1])
        junk = sb("junk", [P, D], BF16)
        small = sb("small", [P, 96])
        done_mark = sb("done_mark", [P, 4])
        arena_at = (nc.sbuf_base + 31) // 32 * 32
        arena = sb("arena", [P, 20800])

        def rounded(name, base, first, *shape):
            return nc.alloc_sbuf_tensor_at(name, [P, *shape], F32R, offset=base + 4 * first)

        low_slots = rounded("low_slots", slots_at, 0, SLOTS, KD, 512)

        at = [0]

        def carve_rounded(name, *shape):
            first = at[0]
            at[0] += int(np.prod(shape))
            assert at[0] <= arena.shape[1], at[0]
            return rounded(name, arena_at, first, *shape)

        def carve(*shape):
            n = int(np.prod(shape))
            v = arena[:, at[0]:at[0] + n]
            at[0] += n
            assert at[0] <= arena.shape[1], at[0]
            if len(shape) == 2:
                return v.rearrange("p (a b) -> p a b", a=shape[0])
            if len(shape) == 3:
                return v.rearrange("p (a b c) -> p a b c", a=shape[0], b=shape[1])
            return v

        PAD_A, PAD_B = TAPS_A // 2, TAPS_B // 2
        LEN_A, LEN_B = NTOK + 4 * PAD_A, NTOK + 4 * PAD_B
        conv_a_in = carve(2, LEN_A)
        conv_b_in = carve(2, LEN_B)
        conv_a_gate = carve(2, NTOK)
        V = carve(ST + CT, 2 * P)
        h_tok = carve(2, D)
        mod = carve(2, D)
        probs = carve(2, NTOK)
        probsT = carve(2, NTOK)
        at_moe = at[0]
        QKT = carve(6, NTOK)
        ada_bias = arena[:, at_moe - 6 * D:at_moe]
        norm_gain = QKT.rearrange("p a b -> p (a b)")[:, 0:2 * D].rearrange("p (a b) -> p a b", a=2)
        sig = h_tok.rearrange("p a b -> p (a b)")[:, 0:2 * NTOK].rearrange("p (a b) -> p a b", a=2)
        z_tok = sig
        tap_out = h_tok.rearrange("p a b -> p (a b)")[:, 0:3 * SEQ].rearrange("p (a b) -> p a b", a=3)
        qk_tok = mod.rearrange("p a b -> p (a b)")[:, 0:2 * NTOK].rearrange("p (a b) -> p a b", a=2)
        rope_a, rope_b = probs[:, 0, :], probs[:, 1, :]
        squares = probsT[:, 0, 0:6 * HD]
        y_tok = mod.rearrange("p a b -> p (a b)")[:, 0:4 * P].rearrange("p (a b) -> p a b", a=2)
        u_sq = sig
        u_rstd = mod.rearrange("p a b -> p (a b)")[:, 0:NTOK]
        NS = CAP_X + CAP_C
        at[0] = 2 * LEN_A + 2 * LEN_B
        xs = carve(2, D)
        y_rows = carve(2, D)
        w_high = [carve_rounded("w_high0", KD, 512), carve_rounded("w_high1", KD, 512), rounded("w_high2", HT_at, 0, KD, 512)]
        xT_high = rounded("xT_high", HT_at, SLOT, KD, NS)
        xT_low = rounded("xT_low", HT_at, SLOT + KD * NS, KD, NS)
        gate_rows = carve(D)
        act_rows = carve(D)
        actT_high, actT_low = carve_rounded("actT_high", KD, NS), carve_rounded("actT_low", KD, NS)
        aff = carve(ST + CT, EXPERTS)
        affT = carve(NTOK)
        top = carve(NS)
        top_at = carve(NS)
        index_t = carve(EXPERTS + 2).bitcast(U32)
        gate_t = carve(EXPERTS)
        now = carve(4)

        at[0] = 0
        q_latT = carve(L_HEADS, SEQ)
        k_latT = carve(L_HEADS, SEQ)
        v_lat = carve(ST, L_HEADS * L_V)
        q_diffT = carve(D_HEADS, SEQ)
        k_diffT = carve(D_HEADS, SEQ)
        v_diff = carve(ST, D_HEADS * 2 * HD)
        at_y = at[0]
        yT = carve(KD, SEQ)
        y_rows2 = carve(2, P)
        at[0] = at_y
        q_rows = carve(2, L_HEADS * L_QK)
        k_rows = carve(2, L_HEADS * L_QK)
        z_lat = q_rows[:, :, 0:LATENT]
        turn_a, turn_b = carve(L_HEADS * ROT), carve(L_HEADS * ROT)
        at[0] = at_y
        qk_diff = carve(2, 2 * D_W)
        at[0] = 0
        ffnT = carve(F_CHUNKS, SEQ)
        ffn_gate = carve(2, SEQ)
        chunk_high = carve_rounded("chunk_high", SPLIT_RING, KD, P)
        ffnT_low = rounded("ffnT_low", arena_at, 0, F_CHUNKS, SEQ)
        ffnT_high = rounded("ffnT_high", HT_at, 0, SPLIT_RING, SEQ)
        down_high = rounded("down_high", arena_at, at[0] - SPLIT_RING * D, SPLIT_RING, D)
        hT_high = rounded("hT_high", HT_at, 0, KD, SEQ)
        hT_low = [rounded("hT_low0", HT_at, KD * SEQ, KD // 2, SEQ), rounded("hT_low1", X_at, ST * D, KD // 2, SEQ)]
        at[0] = 0
        mergedT = carve(KD, SEQ)
        merge_gate = carve(2, 2 * SEQ)
        mergeT_high = [carve_rounded("merge_hT_high", KD, SEQ), carve_rounded("merge_yT_high", KD, SEQ)]
        mergeT_low = [rounded("merge_hT_low", HT_at, 0, KD, NTOK), rounded("merge_yT_low", arena_at, at_y, KD, SEQ)]
        merge_high = [carve_rounded("merge_high0", KD, P), carve_rounded("merge_high1", KD, P),
                      rounded("merge_high2", X_at, ST * D, KD, P), rounded("merge_high3", X_at, ST * D + KD * P, KD, P)]
        assert at[0] <= at_y
        spare = X[:, ST:ST + CT, :].rearrange("p t d -> p (t d)")
        latentT = spare[:, 0:3 * SEQ].rearrange("p (k n) -> p k n", k=3)
        rot_k = spare[:, 3 * SEQ:3 * SEQ + ST * ROT].rearrange("p (t n) -> p t n", t=ST)
        probs2 = spare[:, 0:2 * SEQ].rearrange("p (a n) -> p a n", a=2)
        probs2T = spare[:, 2 * SEQ:4 * SEQ].rearrange("p (a n) -> p a n", a=2)
        cos2 = sb("cos2", [P, ST, ANGLES])
        sin2 = sb("sin2", [P, ST, ANGLES])
        lam = sb("lam", [P, 4])
        latent_gain = sb("latent_gain", [P, 3])
        subln = sb("subln", [P, 2 * HD])
        squares2 = sb("squares2", [P, 2 * HD])
        zeros = squares2
        positions = h_tok[:, 0, 0:ST].bitcast(I32)
        pos_f = h_tok[:, 0, 8:8 + ST]
        freq = h_tok[:, 0, 16:16 + ANGLES]
        angle = h_tok[:, 0, 128:128 + ST * ANGLES].rearrange("p (t n) -> p t n", t=ST)
        whole = h_tok[:, 0, 256:256 + ST * ANGLES].rearrange("p (t n) -> p t n", t=ST)
        lam_in = h_tok[:, 0, 512:512 + 4 * HD].rearrange("p (a n) -> p a n", a=4)
        def at_bank(stage, b, use):
            return stage.at(f"bank{b}", use + 1)

        def pe_may_fill(pe, stage, b, use):
            if isinstance(use, int) and stage.at(f"bank{b}", use) == 0:
                return
            pe.wait_ge(sem[f"free{b}"], stage.at(f"bank{b}", use))

        def slot_of(unit):
            return slots[:, unit % SLOTS, :]

        def merge_turn(c, m):
            return 3 * c + (1, 0, 2)[m]

        def low_flat(unit):
            return low_slots[:, unit % SLOTS, :, :].rearrange("p k n -> p (k n)")

        def ffn_columns(slot, c):
            width = min(512, D_FF - 512 * (c // 4))
            return slot[:, 0:KD * width].rearrange("p (k n) -> p k n", k=KD)[:, :, c % 4 * P:c % 4 * P + P]

        def low_of(unit):
            return low_slots[:, unit % SLOTS, :, :]

        def expert_unit_read(eng, st, pair, q):
            e, j = q // 6, q % 6
            b = 2 + j
            eng.wait_ge(sem[f"full{b}"], at_bank(st, b, (2 * pair + e) * (2 if j in (1, 3) else 1)))

        def pe_wait_unit(pe, unit):
            pe.wait_ge(sem[f"loaded{unit % SLOTS}"], 16 * (unit // SLOTS + 1))

        def enter(eng, stage):
            if stage.number:
                for other in ("scalar", "vector", "gpsimd"):
                    eng.wait_ge(sem[f"{other}_finished"], stage.number)

        def tile_cols(t):
            return slice(t * P, t * P + P)

        block = ctx.enter_context(nc.Block())

        @block.sync
        def _(sp):
            readers = []

            def load(unit, out_in):
                out_, in_ = out_in
                if unit >= SLOTS:
                    name, value = readers[unit - SLOTS]
                    sp.wait_ge(name, value)
                sp.dma_start(out_, in_).then_inc(sem[f"loaded{unit % SLOTS}"], 16)

            sp.dma_start(silu_c[:, :, :], a["c_pair"]).then_inc(sem["c_loaded"], 16)
            for stage in stages:
                for j, (make, (b, use)) in enumerate(stage.units):
                    unit = stage.first_unit + j
                    load(unit, make(slot_of(unit)))
                    if isinstance(b, int):
                        readers.append((sem[f"full{b}"], at_bank(stage, b, use)))
                    else:
                        readers.append((sem[b], stage.at(b, use + 1)))
                if stage.name != "experts":
                    continue
                l, first = stage.layer, stage.first_unit
                mats = (a["w_gate"], a["w_up"], a["w_gate"], a["w_up"], a["w_down"], a["w_down"])

                def part(expert, j):
                    half = j // 2 if j < 4 else j - 4
                    source = mats[j][l]
                    if isinstance(expert, int):
                        source = source[expert]
                    else:
                        source = source[bass.ds(expert, 1), :, :].rearrange("a d f -> (a d) f")
                    return source[:, 512 * half:512 * half + 512].rearrange("(k p) n -> p k n", p=P)

                def reader(e, j):
                    return 2 + j, e * (2 if j in (1, 3) else 1)

                def load_half(expert, u, half):
                    slot = slot_of(first + u).rearrange("p (k n) -> p k n", k=KD)
                    name = "loaded" if half else "half_loaded"
                    rows = slice(KD // 2 * half, KD // 2 * half + KD // 2)
                    sp.dma_start(slot[:, rows, :], part(expert, u % 6)[:, rows, :])\
                        .then_inc(sem[f"{name}{(first + u) % SLOTS}"], 16)

                for u in range(SLOTS):
                    name, value = readers[first + u - SLOTS]
                    sp.wait_ge(name, value)
                    readers.append(None)
                    for half in range(2):
                        load_half(0, u, half)

                def rest_of_pair(pair, last):
                    for u in range(SLOTS, 12 if last else 12 + SLOTS):
                        sp.wait_ge(sem["half_read"], stage.at("half_read", u - SLOTS + 1) + pair * 12)
                        load_half(2 * pair + u // 6, u, 0)
                        b, use = reader(2 * pair + (u - SLOTS) // 6, (u - SLOTS) % 6)
                        sp.wait_ge(sem[f"full{b}"], at_bank(stage, b, use))
                        load_half(2 * pair + u // 6, u, 1)

                with sp.Fori(0, EXPERTS // 2 - 1) as pair:
                    rest_of_pair(pair, False)
                rest_of_pair(EXPERTS // 2 - 1, True)
                del readers[-SLOTS:]
                for e in range(EXPERTS):
                    for j in range(6):
                        b, use = reader(e, j)
                        readers.append((sem[f"full{b}"], at_bank(stage, b, use)))

        @block.tensor
        def _(pe):
            def product(out_, pairs, signal=None):
                for n, (lhsT, rhs) in enumerate(pairs):
                    mm = pe.matmul(out_, lhsT, rhs, start=(n == 0), stop=(n == len(pairs) - 1))
                if signal is not None:
                    mm.then_inc(signal, 1)

            def ada(st):
                pe.wait_ge(sem["silu_c"], 1)
                for n in range(6 * D // 512):
                    unit, b = st.first_unit + n, n % BANKS
                    pe_wait_unit(pe, unit)
                    pe_may_fill(pe, st, b, n // BANKS)
                    w = slot_of(unit).rearrange("p (k n) -> p k n", k=KD)
                    product(bank[0:2, b, :], [(silu_c[:, k, :], w[:, k, :]) for k in range(KD)], sem[f"full{b}"])

            def norm(st):
                for i, t in enumerate(st.facts["tiles"]):
                    pe.wait_ge(sem["h_ready"], st.at("h_ready", i + 1))
                    for half in range(2):
                        b = 2 * (i % 4) + half
                        pe_may_fill(pe, st, b, i // 4)
                        for c in range(4):
                            k = 4 * half + c
                            mm = pe.transpose(bank[:, b, tile_cols(c)], h_tok[:, i % 2, tile_cols(k)], ident[:, :])
                        mm.then_inc(sem[f"full{b}"], 1)

            def conv_in(st):
                parts = st.facts["parts"]
                for c in range(CONV_COLS // P):
                    unit = st.first_unit + c // 4
                    pe_wait_unit(pe, unit)
                    w = slot_of(unit).rearrange("p (k n) -> p k n", k=KD)[:, :, tile_cols(c % 4)]
                    for part in range(parts):
                        g = c * parts + part
                        b = g % BANKS
                        lo, hi = (0, SEQ) if part == 0 else (SEQ, NTOK)
                        pe_may_fill(pe, st, b, g // BANKS)
                        product(bank[:, b, 0:hi - lo], [(w[:, k, :], HT[:, k, lo:hi]) for k in range(KD)],
                                sem[f"full{b}"])

            def qkv(st):
                def turned(i):
                    pe.wait_ge(sem["qk_ready"], st.at("qk_ready", i + 1))
                    keys_only = st.layer == 1 and i >= ST
                    for kind in range(2):
                        pe_may_fill(pe, st, 6 + kind, i)
                        for c in ([2] if keys_only else range(3)):
                            mm = pe.transpose(bank[:, 6 + kind, tile_cols(c)],
                                              qk_tok[:, i % 2, tile_cols(3 * kind + c)], ident[:, :])
                        mm.then_inc(sem[f"full{6 + kind}"], 1)

                for i in range(ST + CT):
                    b, use = 2 * (i % 3), i // 3
                    lo = 256 if st.layer == 1 and i >= ST else 0
                    pe_may_fill(pe, st, b, use)
                    for j in range(2):
                        pe_wait_unit(pe, st.first_unit + j)
                        w = slot_of(st.first_unit + j).rearrange("p (k n) -> p k n", k=KD)
                        product(bank[:, b + j, lo:512], [(HT[:, k, tile_cols(i)], w[:, k, lo:512]) for k in range(KD)],
                                sem[f"full{b}"] if j else None)
                    if i:
                        turned(i - 1)
                turned(ST + CT - 1)

            def attend(st):
                units = heads_of(st.layer)
                wide = st.facts["wide"]

                def scores(i):
                    qt, kind, h = units[i]
                    b, g = 2 * (i % 2), h // 2
                    rows = slice(HD * g, HD * g + HD)
                    q = QKT[rows, 3 * kind + h % 2, tile_cols(qt)]
                    kT = QKT[rows, 3 * kind + 2, :]
                    pe_may_fill(pe, st, b, i // 2)
                    local = key_tiles(qt, kind)[:-CT]
                    if kind:
                        if local:
                            pe.matmul(bank[:, b, :], q, kT[:, 0:SEQ], start=True, stop=True)
                    else:
                        for n, t in enumerate(local):
                            scores_of_tile = bank[:, b, BANK - (len(local) - n) * P:][:, 0:P]
                            pe.matmul(scores_of_tile, q, kT[:, tile_cols(t)], start=True, stop=(t == qt))
                            if t != qt:
                                pe.matmul(scores_of_tile, ident[:, :], band[:, 0 if t < qt else 1, :], start=False, stop=True)
                    pe.matmul(bank[:, b + 1, 0:CTX], q, kT[:, SEQ:NTOK], start=True, stop=True).then_inc(sem[f"full{b}"], 1)

                def turn_probs(i):
                    n = len(key_tiles(*units[i][:2]))
                    b = 2 * (i % 2)
                    pe.wait_ge(sem[f"free{b}"], at_bank(st, b, i // 2))
                    pe_may_fill(pe, st, 4, i)
                    for c in range(min(n, 4)):
                        mm = pe.transpose(bank[:, 4, tile_cols(c)], probs[:, i % 2, tile_cols(c)], ident[:, :])
                    mm.then_inc(sem["full4"], 1)
                    if wide[i]:
                        pe_may_fill(pe, st, 5, sum(wide[:i]))
                        for c in range(4, n):
                            mm = pe.transpose(bank[:, 5, tile_cols(c - 4)], probs[:, i % 2, tile_cols(c)], ident[:, :])
                        mm.then_inc(sem["full5"], 1)

                def mix(i):
                    qt, kind, h = units[i]
                    tiles = key_tiles(qt, kind)
                    pe.wait_ge(sem["free4"], at_bank(st, 4, i))
                    if wide[i]:
                        pe.wait_ge(sem["free5"], at_bank(st, 5, sum(wide[:i])))
                    if h == 0:
                        pe_may_fill(pe, st, 6, i // HEADS)
                    v0 = P * kind + HD * (h // 2)
                    product(bank[:, 6, h * HD:h * HD + HD],
                            [(probsT[:, i % 2, tile_cols(c)], V[:, t, v0:v0 + HD]) for c, t in enumerate(tiles)],
                            sem["full6"] if h == HEADS - 1 else None)

                def turn_y(g):
                    pe.wait_ge(sem["free6"], at_bank(st, 6, g))
                    pe_may_fill(pe, st, 7, g)
                    for c in range(2):
                        mm = pe.transpose(bank[:, 7, tile_cols(c)], y_tok[:, g % 2, tile_cols(c)], ident[:, :])
                    mm.then_inc(sem["full7"], 1)

                n = len(units)
                for i in range(n + 3):
                    if i < n:
                        scores(i)
                    if 1 <= i <= n:
                        turn_probs(i - 1)
                    if 2 <= i <= n + 1:
                        mix(i - 2)
                    if i >= 3 and (i - 3) % HEADS == HEADS - 1:
                        turn_y((i - 3) // HEADS)

            def conv_out(st):
                parts = [(0, SEQ)] + ([(SEQ, NTOK)] if st.layer == 0 else [])
                for n, (source, ready) in enumerate((([HT[:, 2, :], HT[:, 3, :]], None),
                                                     ([u_sq[:, 0, :], u_sq[:, 1, :]], "squared"))):
                    if ready:
                        pe.wait_ge(sem[ready], st.at(ready, 2))
                    pe_may_fill(pe, st, 0, n)
                    for q, (lo, hi) in enumerate(parts):
                        product(bank[:, q, 0:hi - lo], [(mean_of[:, :], s[:, lo:hi]) for s in source],
                                sem["full0"] if q == len(parts) - 1 else None)

            def w_out(st):
                for i in range(st.facts["tiles"]):
                    b = 2 * (i % 4)
                    pe_may_fill(pe, st, b, i // 4)
                    for j in range(2):
                        pe_wait_unit(pe, st.first_unit + j)
                        w = slot_of(st.first_unit + j).rearrange("p (k n) -> p k n", k=KD)
                        product(bank[:, b + j, :], [(HT[:, k, tile_cols(i)], w[:, k, :]) for k in range(KD)],
                                sem[f"full{b}"] if j else None)

            def route(st):
                tiles = st.facts["tiles"]
                pe_may_fill(pe, st, 0, 0)
                for t in range(tiles):
                    product(bank[:, 0, t * EXPERTS:(t + 1) * EXPERTS],
                            [(HT[:, k, tile_cols(t)], router[:, st.layer, k, :]) for k in range(KD)],
                            sem["full0"] if t == tiles - 1 else None)
                pe.wait_ge(sem["affinity"], st.at("affinity", 1))
                pe_may_fill(pe, st, 1, 0)
                for t in range(ST):
                    mm = pe.transpose(bank[0:EXPERTS, 1, tile_cols(t)], aff[:, t, :], ident[:, :])
                mm.then_inc(sem["full1"], 1)
                if tiles > ST:
                    pe_may_fill(pe, st, 2, 0)
                    for t in range(CT):
                        mm = pe.transpose(bank[0:EXPERTS, 2, tile_cols(t)], aff[:, ST + t, :], ident[:, :])
                    mm.then_inc(sem["full2"], 1)
                n = NS if tiles > ST else CAP_X
                pe.wait_ge(sem["ranked"], st.at("ranked", 1))
                pe_may_fill(pe, st, 3, 0)
                pe.transpose(bank[0:n, 3, 0:EXPERTS], top_at[0:EXPERTS, 0:n], ident[0:EXPERTS, 0:EXPERTS])
                pe.transpose(bank[0:n, 3, EXPERTS:2 * EXPERTS], top[0:EXPERTS, 0:n],
                             ident[0:EXPERTS, 0:EXPERTS]).then_inc(sem["full3"], 1)

            def experts(st):
                n = NS if st.facts["tiles"] > ST else CAP_X
                first = st.first_unit

                def turn_rows(e, half, turn):
                    pe.wait_ge(sem[f"gathered{half}"], st.at(f"gathered{half}", 16) + turn * 16)
                    for b in range(2):
                        pe_may_fill(pe, st, b, e)
                        for c in range(4):
                            mm = pe.matmul(bank[:, b, c * n:(c + 1) * n], xs[0:n, half, tile_cols(4 * b + c)],
                                           ident[0:n, 0:n], start=True, stop=True)
                        mm.then_inc(sem[f"full{b}"], 1)

                def by_halves(out_, pair, q, x_high, x_low, signal, act_of=None):
                    high, low = w_high[q % 3], low_of(first + q)
                    for half in range(2):
                        pe.wait_ge(sem["w_split"], st.at("w_split", 2 * q + half + 1) + pair * 24)
                        if act_of is not None:
                            b = 3 + 2 * half
                            pe.wait_ge(sem[f"free{b}"], at_bank(st, b, 2 * act_of + 1))
                        for k in range(4 * half, 4 * half + 4):
                            for m, (x, w) in enumerate(((x_high, high), (x_high, low), (x_low, high))):
                                mm = pe.matmul(out_, x[:, k, 0:n], w[:, k, :],
                                               start=(k == 0 and m == 0), stop=(k == KD - 1 and m == 2))
                        mm.then_inc(signal if half else sem["half_read"], 1)

                def turn_act(e, half):
                    b = 3 + 2 * half
                    pe_may_fill(pe, st, b, 2 * e + 1)
                    for c in range(4):
                        mm = pe.matmul(bank[:, b, c * n:(c + 1) * n], act_rows[0:n, tile_cols(4 * half + c)],
                                       ident[0:n, 0:n], start=True, stop=True)
                    mm.then_inc(sem[f"full{b}"], 1)

                turn_rows(0, 0, 0)
                with pe.Fori(0, EXPERTS // 2) as pair:
                    for h in range(2):
                        e = pair * 2 + h
                        for b in range(2):
                            pe.wait_ge(sem[f"free{b}"], at_bank(st, b, e))
                        for j in range(4):
                            q = 6 * h + j
                            pe_may_fill(pe, st, 2 + j, 2 * e if j in (1, 3) else e)
                            by_halves(bank[0:n, 2 + j, :], pair, q, xT_high, xT_low, sem[f"full{2 + j}"])
                        turn_act(e, 0)
                        turn_rows(e + 1, 1 - h, pair + h)
                        turn_act(e, 1)
                        for j in range(2):
                            q = 6 * h + 4 + j
                            pe_may_fill(pe, st, 6 + j, e)
                            by_halves(bank[0:n, 6 + j, :], pair, q, actT_high, actT_low, sem[f"full{6 + j}"],
                                      act_of=e if j == 0 else None)

            def ffn_up(st):
                for c in range(F_CHUNKS):
                    u, b = c // 4, 2 * (c % 4)
                    for n in range(2):
                        g = 2 * c + n
                        pe.wait_ge(sem["w_split"], st.at("w_split", g + 1))
                        pe_may_fill(pe, st, b + n, c // 4)
                        high = chunk_high[:, g % SPLIT_RING, :, :]
                        low = ffn_columns(low_flat(st.first_unit + 2 * u + n), c)
                        product(bank[:, b + n, :],
                                [(w[:, k, :], x) for k in range(KD)
                                 for w, x in ((high, hT_high[:, k, :]), (high, hT_low[k // 4][:, k % 4, :]),
                                              (low, hT_high[:, k, :]))],
                                sem[f"full{b + n}"])

            def ffn_down(st):
                for k in range(F_CHUNKS):
                    pe.wait_ge(sem["w_split"], st.at("w_split", k + 1))
                    w_parts = (down_high[:, k % SPLIT_RING, :], low_flat(st.first_unit + k // 4)[:, k % 4 * D:k % 4 * D + D])
                    for b in range(BANKS):
                        half, t = b // ST, b % ST
                        if k == 0:
                            pe_may_fill(pe, st, b, 0)
                        for m, (x, part) in enumerate(((ffnT_high[:, k % SPLIT_RING, tile_cols(t)], 0),
                                                       (ffnT_high[:, k % SPLIT_RING, tile_cols(t)], 1),
                                                       (ffnT_low[:, k, tile_cols(t)], 0))):
                            mm = pe.matmul(bank[:, b, :], x, w_parts[part][:, 512 * half:512 * half + 512],
                                           start=(k == 0 and m == 0), stop=(k == F_CHUNKS - 1 and m == 2))
                        if k == F_CHUNKS - 1:
                            mm.then_inc(sem[f"full{b}"], 1)
                    if k < F_CHUNKS - 1:
                        mm.then_inc(sem["down_read"], 1)

            def latent_in(st):
                pe_wait_unit(pe, st.first_unit)
                w = slot_of(st.first_unit)[:, 0:KD * LATENT].rearrange("p (k n) -> p k n", k=KD)

                def turned(i):
                    b = 2 + i % 2
                    pe.wait_ge(sem["latent"], st.at("latent", i + 1))
                    pe_may_fill(pe, st, b, i // 2)
                    for c in range(3):
                        mm = pe.transpose(bank[:, b, tile_cols(c)], z_lat[:, i % 2, tile_cols(c)], ident[:, :])
                    mm.then_inc(sem[f"full{b}"], 1)

                for i in range(ST):
                    b = i % 2
                    pe_may_fill(pe, st, b, i // 2)
                    product(bank[:, b, 0:LATENT], [(HT[:, k, tile_cols(i)], w[:, k, :]) for k in range(KD)], sem[f"full{b}"])
                    if i:
                        turned(i - 1)
                turned(ST - 1)

            def latent_qk(st):
                pe_wait_unit(pe, st.first_unit)
                pe_wait_unit(pe, st.first_unit + 1)
                n_q = L_HEADS * L_QK
                w_q = slot_of(st.first_unit)[:, 0:2 * n_q].rearrange("p (k n) -> p k n", k=2)
                w_kv = slot_of(st.first_unit + 1)

                def turned(i):
                    for n, (rows, name) in enumerate(((q_rows, "q_rows"), (k_rows, "k_rows"))):
                        pe.wait_ge(sem[name], st.at(name, i + 1))
                        for half in range(2):
                            b = 4 + 2 * n + half
                            pe_may_fill(pe, st, b, i)
                            for c in range(4):
                                h = 4 * half + c
                                mm = pe.transpose(bank[0:L_QK, b, tile_cols(c)], rows[:, i % 2, h * L_QK:(h + 1) * L_QK], ident[:, :])
                            mm.then_inc(sem[f"full{b}"], 1)

                for i in range(ST):
                    pe_may_fill(pe, st, 0, i)
                    for j, (lo, hi) in enumerate(((0, 512), (512, n_q))):
                        product(bank[:, j, 0:hi - lo], [(latentT[:, k, tile_cols(i)], w_q[:, k, lo:hi]) for k in range(2)],
                                sem["full0"] if j else None)
                    pe_may_fill(pe, st, 2, i)
                    for j in range(2):
                        product(bank[:, 2 + j, :], [(latentT[:, 2, tile_cols(i)], w_kv[:, 512 * j:512 * j + 512])],
                                sem["full2"] if j else None)
                    if i:
                        turned(i - 1)
                turned(ST - 1)

            def diff_in(st):
                def turned(i):
                    pe.wait_ge(sem["qk_rows"], st.at("qk_rows", i + 1))
                    for n in range(2):
                        pe_may_fill(pe, st, 4 + n, i)
                        for c in range(4):
                            mm = pe.transpose(bank[:, 4 + n, tile_cols(c)], qk_diff[:, i % 2, tile_cols(4 * n + c)], ident[:, :])
                        mm.then_inc(sem[f"full{4 + n}"], 1)

                for i in range(ST):
                    for j in range(3):
                        if j != 1:
                            pe_may_fill(pe, st, j, i)
                        pe_wait_unit(pe, st.first_unit + j)
                        w = slot_of(st.first_unit + j).rearrange("p (k n) -> p k n", k=KD)
                        product(bank[:, j, :], [(HT[:, k, tile_cols(i)], w[:, k, :]) for k in range(KD)],
                                None if j == 0 else sem["full0" if j == 1 else "full2"])
                    if i:
                        turned(i - 1)
                turned(ST - 1)

            def attend_two(st):
                units = units_two()

                def scores(i):
                    kind, qt, h, s = units[i]
                    rows = slice(0, L_QK) if kind == 0 else slice(HD * s, HD * s + HD)
                    qT, kT = (q_latT, k_latT) if kind == 0 else (q_diffT, k_diffT)
                    b = i % 2
                    q = qT[rows, h, tile_cols(qt)]
                    pe_may_fill(pe, st, b, i // 2)
                    if qt:
                        pe.matmul(bank[:, b, 0:qt * P], q, kT[rows, h, 0:qt * P], start=True, stop=True)
                    pe.matmul(bank[:, b, tile_cols(qt)], q, kT[rows, h, tile_cols(qt)], start=True, stop=False)
                    pe.matmul(bank[:, b, tile_cols(qt)], ident[:, :], band[:, 1, :], start=False, stop=True)\
                        .then_inc(sem[f"full{b}"], 1)

                def turn_probs(i):
                    qt, b = units[i][1], 2 + i % 2
                    pe.wait_ge(sem[f"free{i % 2}"], at_bank(st, i % 2, i // 2))
                    pe_may_fill(pe, st, b, i // 2)
                    for c in range(qt + 1):
                        mm = pe.transpose(bank[:, b, tile_cols(c)], probs2[:, i % 2, tile_cols(c)], ident[:, :])
                    mm.then_inc(sem[f"full{b}"], 1)

                def mix(i):
                    kind, qt, h, s = units[i]
                    g = i // 2
                    b = 4 + g % 2
                    pe.wait_ge(sem[f"free{2 + i % 2}"], at_bank(st, 2 + i % 2, i // 2))
                    if s == 0:
                        pe_may_fill(pe, st, b, g // 2)
                    v, width = (v_lat, L_V) if kind == 0 else (v_diff, 2 * HD)
                    product(bank[:, b, s * width:(s + 1) * width],
                            [(probs2T[:, i % 2, tile_cols(c)], v[:, c, h * width:(h + 1) * width]) for c in range(qt + 1)],
                            sem[f"full{b}"] if s else None)

                def turn_y(g):
                    b = 6 + g % 2
                    pe.wait_ge(sem["y_rows"], st.at("y_rows", g + 1))
                    pe_may_fill(pe, st, b, g // 2)
                    pe.transpose(bank[:, b, 0:P], y_rows2[:, g % 2, :], ident[:, :]).then_inc(sem[f"full{b}"], 1)

                n = len(units)
                for i in range(n + 4):
                    if i < n:
                        scores(i)
                    if 1 <= i <= n:
                        turn_probs(i - 1)
                    if 2 <= i <= n + 1:
                        mix(i - 2)
                    if i >= 4 and (i - 4) % 2 == 1:
                        turn_y((i - 4) // 2)

            def merge(st):
                for c in range(KD):
                    b, cols = 4 * (c % 2), tile_cols(c % 4)
                    unit = st.first_unit + 3 * (c // 4)
                    for n, (m, source, ks) in enumerate(((1, 0, range(KD)), (0, 1, range(KD // 2)),
                                                         (2, 0, range(KD)), (0, 1, range(KD // 2, KD)))):
                        turn = merge_turn(c, m)
                        pe.wait_ge(sem["w_split"], st.at("w_split", turn + 1))
                        if c == 0 and n < 2:
                            pe.wait_ge(sem["rows_split"], st.at("rows_split", KD * (source + 1)))
                        pe_may_fill(pe, st, b + n, c // 2)
                        high, low = merge_high[turn % 4], low_of(unit + m)
                        x_high, x_low = mergeT_high[source], mergeT_low[source]
                        product(bank[:, b + n, :],
                                [(w, x) for k in ks
                                 for w, x in ((high[:, k, :], x_high[:, k, :]), (high[:, k, :], x_low[:, k, 0:SEQ]),
                                              (low[:, k, cols], x_high[:, k, :]))],
                                sem[f"full{b + n}"])

            def project(st):
                for i in range(ST):
                    b = 2 * i
                    pe_may_fill(pe, st, b, 0)
                    for j in range(2):
                        pe_wait_unit(pe, st.first_unit + j)
                        w = slot_of(st.first_unit + j).rearrange("p (k n) -> p k n", k=KD)
                        product(bank[:, b + j, :], [(mergedT[:, k, tile_cols(i)], w[:, k, :]) for k in range(KD)],
                                sem[f"full{b}"] if j else None)

            programs = dict(ada=ada, norm=norm, conv_in=conv_in, qkv=qkv, attend=attend, conv_out=conv_out,
                            w_out=w_out, route=route, experts=experts, ffn_up=ffn_up, ffn_down=ffn_down,
                            latent_in=latent_in, latent_qk=latent_qk, diff_in=diff_in, attend_two=attend_two,
                            merge=merge, project=project)
            for st in stages:
                if st.name in programs and st.name != "ada":
                    enter(pe, st)
                if st.name in programs:
                    programs[st.name](st)

        @block.scalar
        def _(act):
            step = Steps(act, sem["scalar_steps"])
            flat_bank = bank[:, :, :].rearrange("p b n -> p (b n)")

            def init(st):
                act.wait_ge(sem["c_loaded"], 16)
                act.wait_ge(sem["gpsimd_steps"], 1)
                act.activation(silu_c[:, :, :], silu_c[:, :, :], ACT.Silu).then_inc(sem["silu_c"], 1)

            def norm(st):
                tiles = st.facts["tiles"]
                for i, t in enumerate(tiles):
                    step(act.activation(junk[:, :], X[:, t, :], ACT.Square, accum_out=small[:, i:i + 1]))
                    act.activation(small[:, 8 + i:9 + i], small[:, i:i + 1], ACT.Sqrt, bias=eps[:, :],
                                   scale=1.0 / D).then_inc(sem["mean_root"], 1)
                for i, t in enumerate(tiles):
                    b = 2 * (i % 4)
                    if st.facts.get("split"):
                        for half in range(2):
                            act.wait_ge(sem[f"full{b + half}"], at_bank(st, b + half, i // 4))
                            act.activation(hT_high[:, 4 * half:4 * half + 4, tile_cols(t)],
                                           bank[:, b + half, :].rearrange("p (k n) -> p k n", k=4), ACT.Copy)\
                                .then_inc(sem["h_high"], 1)
                        continue
                    act.wait_ge(sem[f"full{b}"], at_bank(st, b, i // 4))
                    act.activation(HT[:, 0:4, tile_cols(t)], bank[:, b, :].rearrange("p (k n) -> p k n", k=4),
                                   ACT.Copy).then_inc(sem[f"free{b}"], 1)

            def conv_in(st):
                parts = st.facts["parts"]
                for c in range(CONV_COLS // P):
                    what, half = c // 2, c % 2
                    if what not in (0, 1, 4):
                        continue
                    for part in range(parts):
                        g = c * parts + part
                        b = g % BANKS
                        lo, hi = (0, SEQ) if part == 0 else (SEQ, NTOK)
                        start = part * (SEQ + 2 * PAD_A) + PAD_A
                        act.wait_ge(sem[f"full{b}"], at_bank(st, b, g // BANKS))
                        dst, func = {0: (conv_a_gate[:, half, lo:hi], ACT.Copy),
                                     1: (conv_a_in[:, half, start:start + hi - lo], ACT.Copy),
                                     4: (sig[:, half, lo:hi], ACT.Sigmoid)}[what]
                        act.activation(dst, bank[:, b, 0:hi - lo], func).then_inc(sem[f"free{b}"], 1)

            def qkv(st):
                def take_turned(i):
                    keys_only = st.layer == 1 and i >= ST
                    c0 = 2 if keys_only else 0
                    for kind in range(2):
                        b = 6 + kind
                        act.wait_ge(sem[f"full{b}"], at_bank(st, b, i))
                        act.activation(QKT[:, 3 * kind + c0:3 * kind + 3, tile_cols(i)],
                                       bank[:, b, c0 * P:3 * P].rearrange("p (k n) -> p k n", n=P),
                                       ACT.Copy).then_inc(sem[f"free{b}"], 1)

                for i in range(ST + CT):
                    b, use = 2 * (i % 3), i // 3
                    lo = 256 if st.layer == 1 and i >= ST else 0
                    act.wait_ge(sem[f"full{b}"], at_bank(st, b, use))
                    if i >= 2:
                        act.wait_ge(sem["qk_ready"], st.at("qk_ready", i - 1))
                    z = z_tok[:, i % 2, :].rearrange("p (a n) -> p a n", a=2)
                    act.activation(z[:, :, lo:384], bank[:, b:b + 2, lo:384], ACT.Copy)
                    act.activation(V[:, i, :].rearrange("p (a n) -> p a n", a=2), bank[:, b:b + 2, 384:512],
                                   ACT.Copy).then_inc(sem[f"free{b}"], 1)
                    act.wait_ge(sem["head_sums"], st.at("head_sums", i + 1))
                    act.activation(small[:, 8:14], small[:, 0:6], ACT.Sqrt, bias=eps[:, :],
                                   scale=1.0 / HD).then_inc(sem["head_roots"], 1)
                    if i:
                        take_turned(i - 1)
                take_turned(ST + CT - 1)

            def attend(st):
                units = heads_of(st.layer)
                wide = st.facts["wide"]

                def exponentials(i):
                    qt, kind, h = units[i]
                    n = len(key_tiles(qt, kind)) * P
                    b, g = 2 * (i % 2), i // HEADS
                    act.wait_ge(sem["neg_max"], st.at("neg_max", i + 1))
                    if i >= 2:
                        act.wait_ge(sem["full4"], at_bank(st, 4, i - 2))
                        if wide[i - 2]:
                            act.wait_ge(sem["full5"], at_bank(st, 5, sum(wide[:i - 2])))
                    lo = (b + 1) * BANK + CTX - n
                    col = 16 + 4 * (g % 2) + h
                    act.activation(probs[:, i % 2, 0:n], flat_bank[:, lo:lo + n], ACT.Exp, bias=small[:, i % 8:i % 8 + 1],
                                   scale=HD ** -0.5, accum_out=small[:, col:col + 1]).then_inc(sem[f"free{b}"], 1)
                    if kind == 0:
                        act.activation(small[:, col + 8:col + 9], sink[:, st.layer, h:h + 1], ACT.Exp,
                                       bias=small[:, i % 8:i % 8 + 1]).then_inc(sem["sink_exp"], 1)

                def take_probs(i):
                    n = len(key_tiles(*units[i][:2]))
                    act.wait_ge(sem["full5"], at_bank(st, 5, sum(wide[:i])))
                    act.activation(probsT[:, i % 2, 4 * P:n * P], bank[:, 5, 0:(n - 4) * P], ACT.Copy)\
                       .then_inc(sem["free5"], 1)

                def take_y(g):
                    qt, kind, _ = units[g * HEADS]
                    act.wait_ge(sem["full7"], at_bank(st, 7, g))
                    act.activation(HT[:, 4 + 2 * kind:6 + 2 * kind, tile_cols(qt)],
                                   bank[:, 7, 0:2 * P].rearrange("p (k n) -> p k n", k=2), ACT.Copy)\
                       .then_inc(sem["free7"], 1)

                n = len(units)
                for i in range(n + 3):
                    if i < n:
                        exponentials(i)
                    if 1 <= i <= n and wide[i - 1]:
                        take_probs(i - 1)
                    if i >= 3 and (i - 3) % HEADS == HEADS - 1:
                        take_y((i - 3) // HEADS)

            def conv_out(st):
                n = NTOK if st.layer == 0 else SEQ
                for c in range(2):
                    if c == 0:
                        act.wait_ge(sem["centered"], st.at("centered", 1))
                    else:
                        act.wait_ge(sem["free0"], at_bank(st, 0, 0))
                    act.activation(u_sq[:, c, 0:n], HT[:, 2 + c, 0:n], ACT.Square).then_inc(sem["squared"], 1)
                act.wait_ge(sem["full0"], at_bank(st, 0, 1))
                act.activation(u_rstd[:, 0:n], flat_bank[:, 0:n], ACT.Sqrt, bias=eps[:, :]).then_inc(sem["free0"], 1)
                for c in range(2):
                    act.wait_ge(sem["normed"], st.at("normed", c + 1))
                    act.activation(HT[:, 2 + c, 0:n], HT[:, 2 + c, 0:n], ACT.Silu, bias=conv_vec[:, 2, st.layer, c:c + 1],
                                   scale=conv_vec[:, 1, st.layer, c:c + 1])

            def route(st):
                act.wait_ge(sem["free0"], at_bank(st, 0, 0))
                v = aff[:, 0:st.facts["tiles"], :]
                act.activation(v, v, ACT.Exp).then_inc(sem["logit_exp"], 1)

            def experts(st):
                n = NS if st.facts["tiles"] > ST else CAP_X

                def split(pair, q):
                    unit = st.first_unit + q
                    w = slot_of(unit).rearrange("p (k n) -> p k n", k=KD)
                    for half in range(2):
                        if half:
                            act.wait_ge(sem[f"loaded{unit % SLOTS}"], pair * (16 * 12 // SLOTS) + 16 * (unit // SLOTS + 1))
                        else:
                            act.wait_ge(sem[f"half_loaded{unit % SLOTS}"],
                                        pair * (16 * 12 // SLOTS) + 16 * (6 * EXPERTS // SLOTS * st.layer + q // SLOTS + 1))
                        if q == 2 or (q > 2 and half):
                            expert_unit_read(act, st, pair, q - 3)
                        elif q > 2:
                            act.wait_ge(sem["half_read"], st.at("half_read", q - 2) + pair * 12)
                        rows = slice(4 * half, 4 * half + 4)
                        act.activation(w_high[q % 3][:, rows, :], w[:, rows, :], ACT.Copy).then_inc(sem["w_high"], 1)

                def take_rows(e):
                    for b in range(2):
                        act.wait_ge(sem[f"full{b}"], at_bank(st, b, e))
                        act.activation(xT_high[:, 4 * b:4 * b + 4, 0:n], bank[:, b, 0:4 * n].rearrange("p (k n) -> p k n", k=4),
                                       ACT.Copy).then_inc(sem["x_high"], 1)

                def silu(e, half):
                    b = 2 + 2 * half
                    act.wait_ge(sem[f"full{b}"], at_bank(st, b, e))
                    act.wait_ge(sem[f"free{b + 1}"], st.at(f"bank{b + 1}", 2 * e))
                    act.activation(gate_rows[0:n, 512 * half:512 * half + 512], bank[0:n, b, :], ACT.Silu)\
                        .then_inc(sem[f"free{b}"], 1)

                def take_act(e, half):
                    b = 3 + 2 * half
                    act.wait_ge(sem[f"full{b}"], at_bank(st, b, 2 * e + 1))
                    act.wait_ge(sem["full7"], st.at("bank7", e))
                    act.activation(actT_high[:, 4 * half:4 * half + 4, 0:n],
                                   bank[:, b, 0:4 * n].rearrange("p (k n) -> p k n", k=4), ACT.Copy).then_inc(sem["act_high"], 1)

                def two_experts(pair, last):
                    for h in range(2):
                        e = 2 * pair + h
                        split(pair, 6 * h + 2)
                        split(pair, 6 * h + 3)
                        silu(e, 0)
                        split(pair, 6 * h + 4)
                        silu(e, 1)
                        split(pair, 6 * h + 5)
                        take_act(e, 0)
                        take_rows(e + 1)
                        take_act(e, 1)
                        if not (last and h):
                            split(pair, 6 * h + 6)
                            split(pair, 6 * h + 7)

                for q in range(2):
                    split(0, q)
                take_rows(0)
                with act.Fori(0, EXPERTS // 2 - 1) as pair:
                    two_experts(pair, False)
                two_experts(EXPERTS // 2 - 1, True)

            def norm_rows(st):
                for t in range(ST):
                    step(act.activation(junk[:, :], X[:, t, :], ACT.Square, accum_out=small[:, t:t + 1]))
                    act.activation(small[:, 8 + t:9 + t], small[:, t:t + 1], ACT.Sqrt, bias=eps[:, :],
                                   scale=1.0 / D).then_inc(sem["mean_root"], 1)

            def angles(st):
                act.wait_ge(sem["lam_sum"], st.at("lam_sum", 1))
                act.activation(lam[:, 0:2], lam[:, 0:2], ACT.Exp).then_inc(sem["lam_exp"], 1)
                act.wait_ge(sem["angles"], st.at("angles", 1))
                act.activation(cos2[:, :, :], cos2[:, :, :], ACT.Sin)
                act.activation(sin2[:, :, :], sin2[:, :, :], ACT.Sin).then_inc(sem["sines"], 1)

            def ffn_up(st):
                def split(g):
                    c, n = g // 2, g % 2
                    unit = st.first_unit + 2 * (c // 4) + n
                    act.wait_ge(sem[f"loaded{unit % SLOTS}"], 16 * (unit // SLOTS + 1))
                    if g >= SPLIT_RING:
                        act.wait_ge(sem[f"full{g % BANKS}"], at_bank(st, g % BANKS, g // BANKS - 1))
                    act.activation(chunk_high[:, g % SPLIT_RING, :, :], ffn_columns(slot_of(unit), c), ACT.Copy)\
                        .then_inc(sem["w_high"], 1)

                for g in range(4):
                    split(g)
                for c in range(F_CHUNKS):
                    b = 2 * (c % 4)
                    for g in (2 * c + 4, 2 * c + 5):
                        if g < 2 * F_CHUNKS:
                            split(g)
                    act.wait_ge(sem[f"full{b}"], at_bank(st, b, c // 4))
                    if c >= 2:
                        q = 2 * ((c - 2) % 4) + 1
                        act.wait_ge(sem[f"free{q}"], at_bank(st, q, (c - 2) // 4))
                    act.activation(ffn_gate[:, c % 2, :], bank[:, b, :], ACT.Silu).then_inc(sem[f"free{b}"], 1)

            def ffn_down(st):
                for k in range(F_CHUNKS):
                    unit = st.first_unit + k // 4
                    if k >= SPLIT_RING:
                        act.wait_ge(sem["down_read"], st.at("down_read", k - SPLIT_RING + 1))
                    act.activation(ffnT_high[:, k % SPLIT_RING, :], ffnT[:, k, :], ACT.Copy)
                    act.wait_ge(sem[f"loaded{unit % SLOTS}"], 16 * (unit // SLOTS + 1))
                    act.activation(down_high[:, k % SPLIT_RING, :], slot_of(unit)[:, k % 4 * D:k % 4 * D + D], ACT.Copy)\
                        .then_inc(sem["w_high"], 1)

            def latent_in(st):
                def take(i):
                    b = 2 + i % 2
                    act.wait_ge(sem[f"full{b}"], at_bank(st, b, i // 2))
                    for c in range(3):
                        ins = act.activation(latentT[:, c, tile_cols(i)], bank[:, b, tile_cols(c)], ACT.Copy,
                                             scale=latent_gain[:, c:c + 1])
                    ins.then_inc(sem[f"free{b}"], 1)

                for i in range(ST):
                    b = i % 2
                    act.wait_ge(sem[f"full{b}"], at_bank(st, b, i // 2))
                    for n, (lo, width) in enumerate(((0, Q_RANK), (Q_RANK, KV_RANK))):
                        act.activation(junk[:, 0:width], bank[:, b, lo:lo + width], ACT.Square,
                                       accum_out=small[:, 2 * i + n:2 * i + n + 1]).then_inc(sem["latent_sum"], 1)
                        act.wait_ge(sem["latent_sum"], st.at("latent_sum", 2 * i + n + 1))
                        act.activation(small[:, 16 + 2 * i + n:17 + 2 * i + n], small[:, 2 * i + n:2 * i + n + 1], ACT.Sqrt,
                                       bias=eps[:, :], scale=1.0 / width).then_inc(sem["latent_root"], 1)
                    if i:
                        take(i - 1)
                take(ST - 1)

            def latent_qk(st):
                def take(i):
                    for b, dst in ((4, q_latT), (5, q_latT), (6, k_latT), (7, k_latT)):
                        act.wait_ge(sem[f"full{b}"], at_bank(st, b, i))
                        act.activation(dst[0:L_QK, 4 * (b % 2):4 * (b % 2) + 4, tile_cols(i)],
                                       bank[0:L_QK, b, :].rearrange("p (h n) -> p h n", h=4), ACT.Copy)\
                            .then_inc(sem[f"free{b}"], 1)

                for i in range(ST):
                    act.wait_ge(sem["free2"], at_bank(st, 2, i))
                    if i:
                        take(i - 1)
                take(ST - 1)

            def diff_in(st):
                def take(i):
                    for n, dst in enumerate((q_diffT, k_diffT)):
                        b = 4 + n
                        act.wait_ge(sem[f"full{b}"], at_bank(st, b, i))
                        act.activation(dst[:, :, tile_cols(i)], bank[:, b, :].rearrange("p (h n) -> p h n", h=4), ACT.Copy)\
                            .then_inc(sem[f"free{b}"], 1)

                for i in range(ST):
                    act.wait_ge(sem["full2"], at_bank(st, 2, i))
                    act.activation(v_diff[:, i, :], bank[:, 2, :], ACT.Copy).then_inc(sem["free2"], 1)
                    if i:
                        take(i - 1)
                take(ST - 1)

            def attend_two(st):
                units = units_two()
                scales = (L_QK ** -0.5, HD ** -0.5)

                def exponentials(i):
                    kind, qt, h, s = units[i]
                    n, b = (qt + 1) * P, i % 2
                    act.wait_ge(sem["neg_max"], st.at("neg_max", i + 1))
                    if i >= 2:
                        act.wait_ge(sem[f"full{2 + b}"], at_bank(st, 2 + b, i // 2 - 1))
                    act.activation(probs2[:, b, 0:n], bank[:, b, 0:n], ACT.Exp, bias=small[:, i % 8:i % 8 + 1],
                                   scale=scales[kind], accum_out=small[:, 16 + i % 8:17 + i % 8]).then_inc(sem[f"free{b}"], 1)

                def root(g):
                    k = g - 4 * L_HEADS // 2
                    act.wait_ge(sem["y_sum"], st.at("y_sum", k + 1))
                    act.activation(small[:, 64 + g % 2:65 + g % 2], small[:, 62 + g % 2:63 + g % 2], ACT.Sqrt,
                                   bias=eps[:, :], scale=1.0 / (2 * HD)).then_inc(sem["y_root"], 1)

                def take_y(g):
                    kind, qt, h, _ = units[2 * g]
                    b = 6 + g % 2
                    act.wait_ge(sem[f"full{b}"], at_bank(st, b, g // 2))
                    chunk = h // 2 if kind == 0 else 4 + h
                    act.activation(yT[:, chunk, tile_cols(qt)], bank[:, b, 0:P], ACT.Copy).then_inc(sem[f"free{b}"], 1)

                n = len(units)
                for i in range(n + 4):
                    if i < n:
                        exponentials(i)
                    if i >= 3 and (i - 3) % 2 == 0 and (i - 3) // 2 < n // 2 and units[i - 3][0]:
                        root((i - 3) // 2)
                    if i >= 4 and (i - 4) % 2 == 1:
                        take_y((i - 4) // 2)

            def merge(st):
                def split(c, m):
                    unit, turn = st.first_unit + 3 * (c // 4) + m, merge_turn(c, m)
                    act.wait_ge(sem[f"loaded{unit % SLOTS}"], 16 * (unit // SLOTS + 1))
                    if turn >= 4:
                        before = turn - 4
                        n = (0, 3, 2)[before % 3]
                        b = 4 * (before // 3 % 2) + n
                        act.wait_ge(sem[f"full{b}"], at_bank(st, b, before // 3 // 2))
                    w = slot_of(unit).rearrange("p (k n) -> p k n", k=KD)
                    act.activation(merge_high[turn % 4][:, :, :], w[:, :, tile_cols(c % 4)], ACT.Copy).then_inc(sem["w_high"], 1)

                def rows(source, x):
                    for k in range(KD):
                        act.activation(mergeT_high[source][:, k, :], x[:, k, 0:SEQ], ACT.Copy).then_inc(sem["rows_high"], 1)

                split(0, 1)
                rows(0, HT)
                split(0, 0)
                rows(1, yT)
                split(0, 2)
                for c in range(KD):
                    b, use = 4 * (c % 2), c // 2
                    if c + 1 < KD:
                        split(c + 1, 1)
                    for n in range(2):
                        act.wait_ge(sem[f"full{b + 2 * n}"], at_bank(st, b + 2 * n, use))
                        if c >= 2:
                            act.wait_ge(sem["merged"], st.at("merged", c - 1))
                        act.activation(merge_gate[:, c % 2, n * SEQ:(n + 1) * SEQ], bank[:, b + 2 * n, :], ACT.Sigmoid)\
                            .then_inc(sem[f"free{b + 2 * n}"], 1)
                        if c + 1 < KD:
                            split(c + 1, 0 if n == 0 else 2)

            programs = dict(init=init, norm=norm, conv_in=conv_in, qkv=qkv, attend=attend, conv_out=conv_out,
                            route=route, experts=experts, norm_rows=norm_rows, angles=angles, ffn_up=ffn_up, ffn_down=ffn_down,
                            latent_in=latent_in, latent_qk=latent_qk, diff_in=diff_in, attend_two=attend_two, merge=merge)
            for st in stages:
                if st.name in programs:
                    enter(act, st)
                    programs[st.name](st)
                elif st.number:
                    act.wait_ge(sem["scalar_finished"], st.number)
                act.activation(done_mark[:, 0:1], eps[:, :], ACT.Copy).then_inc(sem["scalar_finished"], 1)

        @block.vector
        def _(dve):
            step = Steps(dve, sem["vector_steps"])
            flat_bank = bank[:, :, :].rearrange("p b n -> p (b n)")

            def per_row(column, n, m):
                return column.unsqueeze(2).broadcast_to([P, n, m])

            def init(st):
                dve.memset(mean_of[:, :], 1.0 / (D // 4))
                dve.memset(conv_a_in[:, :, :], 0.0)
                dve.memset(conv_b_in[:, :, :], 0.0)

            def ada(st):
                l = st.layer
                rows = HT[:, :, :].rearrange("p k n -> p (k n)")
                dve.wait_ge(sem["rows_loaded"], st.at("rows_loaded", 32))
                for n in range(6 * D // 512):
                    b = n % BANKS
                    cols = slice(512 * n, 512 * n + 512)
                    dve.wait_ge(sem[f"full{b}"], at_bank(st, b, n // BANKS))
                    dve.tensor_tensor(rows[0:2, cols], bank[0:2, b, :], ada_bias[0:2, cols], ALU.add)\
                       .then_inc(sem[f"free{b}"], 1)
                for b in range(BANKS):
                    dve.wait_ge(sem[f"free{b}"], st.at(f"bank{b}", st.signals[f"bank{b}"]))
                for n, comp in enumerate((1, 4)):
                    v = rows[0:2, comp * D:comp * D + D]
                    ins = dve.scalar_tensor_tensor(v, v, 1.0, norm_gain[0:2, n, :], ALU.add, ALU.mult)
                ins.then_inc(sem["mods_rows"], 1)

            def norm(st):
                tiles, shift = st.facts["tiles"], st.facts["shift"]

                def take(i):
                    if st.facts.get("split"):
                        for half in range(2):
                            b = 2 * (i % 4) + half
                            cols = tile_cols(tiles[i])
                            dve.wait_ge(sem["h_high"], st.at("h_high", 2 * i + half + 1))
                            dve.tensor_tensor(hT_low[half][:, :, cols], bank[:, b, :].rearrange("p (k n) -> p k n", k=4),
                                              hT_high[:, 4 * half:4 * half + 4, cols].bitcast(F32), ALU.subtract)\
                                .then_inc(sem[f"free{b}"], 1)
                        return
                    b = 2 * (i % 4) + 1
                    dve.wait_ge(sem[f"full{b}"], at_bank(st, b, i // 4))
                    dve.tensor_copy(HT[:, 4:8, tile_cols(tiles[i])], bank[:, b, :].rearrange("p (k n) -> p k n", k=4))\
                       .then_inc(sem[f"free{b}"], 1)

                dve.wait_ge(sem["rows_loaded"], st.at("rows_loaded", 32 if shift is not None else 16))
                for i, t in enumerate(tiles):
                    dve.wait_ge(sem["mean_root"], st.at("mean_root", i + 1))
                    step(dve.reciprocal(small[:, 16 + i:17 + i], small[:, 8 + i:9 + i]))
                    if i >= 2:
                        b = 2 * ((i - 2) % 4) + 1
                        dve.wait_ge(sem[f"full{b}"], at_bank(st, b, (i - 2) // 4))
                        if st.facts["store"]:
                            dve.wait_ge(sem[f"h_stored{i % 2}"], st.at(f"h_stored{i % 2}", 16 * (i // 2)))
                    h = h_tok[:, i % 2, :]
                    ins = dve.scalar_tensor_tensor(h, X[:, t, :], small[:, 16 + i:17 + i], mod[:, 0, :], ALU.mult, ALU.mult)
                    if shift is not None:
                        step(ins)
                        ins = dve.tensor_tensor(h, h, mod[:, 1, :], ALU.add)
                    ins.then_inc(sem["h_ready"], 1)
                    if i:
                        take(i - 1)
                take(len(tiles) - 1)

            def conv_in(st):
                parts = st.facts["parts"]

                def group(c, part):
                    g = c * parts + part
                    return g % BANKS, g // BANKS

                for c in range(4, CONV_COLS // P):
                    what, half = c // 2, c % 2
                    for part in range(parts):
                        b, use = group(c, part)
                        lo, hi = (0, SEQ) if part == 0 else (SEQ, NTOK)
                        n = hi - lo
                        start_a = part * (SEQ + 2 * PAD_A) + PAD_A
                        start_b = part * (SEQ + 2 * PAD_B) + PAD_B
                        va = conv_a_in[:, half, start_a:start_a + n]
                        vb = conv_b_in[:, half, start_b:start_b + n]
                        if what == 2:
                            b_c, use_c = group(c - 2, part)
                            dve.wait_ge(sem[f"free{b_c}"], at_bank(st, b_c, use_c))
                            dve.wait_ge(sem[f"full{b}"], at_bank(st, b, use))
                            dve.tensor_tensor(va, bank[:, b, 0:n], va, ALU.mult).then_inc(sem[f"free{b}"], 1)
                        elif what == 3:
                            dve.wait_ge(sem[f"full{b}"], at_bank(st, b, use))
                            dve.tensor_copy(vb, bank[:, b, 0:n]).then_inc(sem[f"free{b}"], 1)
                        else:
                            b_v, use_v = group(c - 2, part)
                            dve.wait_ge(sem[f"free{b_v}"], at_bank(st, b_v, use_v))
                            dve.wait_ge(sem[f"free{b}"], at_bank(st, b, use))
                            dve.tensor_tensor(vb, vb, sig[:, half, lo:hi], ALU.mult)

            def qkv(st):
                l = st.layer
                for i in range(ST + CT):
                    b, use = 2 * (i % 3), i // 3
                    keys_only = l == 1 and i >= ST
                    h0 = 4 if keys_only else 0
                    nh = 6 - h0
                    z = z_tok[:, i % 2, :].rearrange("p (a n) -> p a n", a=2)
                    heads = z[:, 1, h0 * HD:].rearrange("p (h d) -> p h d", d=HD)
                    sq = squares[:, h0 * HD:].rearrange("p (h d) -> p h d", d=HD)
                    dve.wait_ge(sem[f"free{b}"], at_bank(st, b, use))
                    step(dve.tensor_tensor(sq, heads, heads, ALU.mult))
                    dve.tensor_reduce(small[:, h0:6], sq, AX.X, ALU.add).then_inc(sem["head_sums"], 1)
                    dve.wait_ge(sem["head_roots"], st.at("head_roots", i + 1))
                    step(dve.reciprocal(small[:, 16 + h0:22], small[:, 8 + h0:14]))
                    step(dve.tensor_tensor(heads, heads, per_row(small[:, 16 + h0:22], nh, HD), ALU.mult))
                    step(dve.tensor_tensor(heads, heads, head_gain[:, l, h0:6, :], ALU.mult))
                    if i < ST:
                        all_heads = z_tok[:, i % 2, :].rearrange("p (h d) -> p h d", d=HD)
                        swap = z_tok[:, i % 2, :].rearrange("p (h b d) -> p h b d", b=2, d=HD // 4)
                        turned = rope_b.rearrange("p (h b d) -> p h b d", b=2, d=HD // 4)
                        sin = rope_sin[:, i, :].rearrange("p (a b d) -> p a b d", a=2, b=2)
                        step(dve.tensor_tensor(rope_a.rearrange("p (h d) -> p h d", d=HD), all_heads,
                                               rope_cos[:, i, :].unsqueeze(1).broadcast_to([P, 12, HD]), ALU.mult))
                        for a_ in range(2):
                            for to in range(2):
                                step(dve.tensor_tensor(
                                    turned[:, a_::2, to, :], swap[:, a_::2, 1 - to, :],
                                    sin[:, a_, to, :].unsqueeze(1).broadcast_to([P, 12, HD // 4]), ALU.mult))
                    if i >= 2:
                        for kind in range(2):
                            dve.wait_ge(sem[f"full{6 + kind}"], at_bank(st, 6 + kind, i - 2))
                    for kind in range(2):
                        c0 = 384 * kind
                        pieces = [(slice(c0 + 256, c0 + 384), None)]
                        if not keys_only:
                            pieces.append((slice(c0, c0 + 256), "q"))
                        for cols, q in pieces:
                            def view(v, order):
                                v = v[:, cols]
                                return v.rearrange(order, g=2, j=2) if q else v
                            dst = view(qk_tok[:, i % 2, :], "p (j g d) -> p g j d")
                            if i < ST:
                                ins = dve.tensor_tensor(dst, view(rope_a, "p (g j d) -> p g j d"),
                                                        view(rope_b, "p (g j d) -> p g j d"), ALU.add)
                            else:
                                ins = dve.tensor_copy(dst, view(z_tok[:, i % 2, :], "p (g j d) -> p g j d"))
                    ins.then_inc(sem["qk_ready"], 1)
                    dve.wait_ge(sem["qk_ready"], st.at("qk_ready", i + 1))

            def attend(st):
                l = st.layer
                units = heads_of(l)

                def maximum(i):
                    qt, kind, h = units[i]
                    n = len(key_tiles(qt, kind)) * P
                    b = 2 * (i % 2)
                    lo = (b + 1) * BANK + CTX - n
                    dve.wait_ge(sem[f"full{b}"], at_bank(st, b, i // 2))
                    m = small[:, 40 + i % 8:41 + i % 8]
                    step(dve.tensor_reduce(m, flat_bank[:, lo:lo + n], AX.X, ALU.max))
                    scale = -HD ** -0.5
                    if kind == 0:
                        step(dve.tensor_scalar(m, m, -scale, sink[:, l, h:h + 1], ALU.mult, ALU.max))
                        scale = -1.0
                    dve.tensor_scalar(small[:, i % 8:i % 8 + 1], m, scale, None, ALU.mult).then_inc(sem["neg_max"], 1)

                def tap(k):
                    for part, (lo, hi) in enumerate([(0, SEQ)] + ([(SEQ, NTOK)] if l == 0 else [])):
                        start = part * (SEQ + 2 * PAD_B)
                        dst = HT[:, 3, lo:hi]
                        v, w = conv_b_in[:, 1, start + k:start + k + hi - lo], conv_b_w[:, l, 1, k:k + 1]
                        if k:
                            step.later(dve.scalar_tensor_tensor(dst, v, w, dst, ALU.mult, ALU.add))
                        else:
                            step.later(dve.tensor_scalar(dst, v, w, conv_vec[:, 0, l, 1:2], ALU.mult, ALU.add))

                def take_probs(i):
                    n = min(4, len(key_tiles(*units[i][:2])))
                    dve.wait_ge(sem["full4"], at_bank(st, 4, i))
                    dve.tensor_copy(probsT[:, i % 2, 0:n * P], bank[:, 4, 0:n * P]).then_inc(sem["free4"], 1)

                def rows_of_y(g):
                    kind = units[g * HEADS][1]
                    c = 16 + 4 * (g % 2)
                    total = small[:, c:c + 4]
                    dve.wait_ge(sem["full6"], at_bank(st, 6, g))
                    if kind == 0:
                        sinks = sum(k == 0 for _, k, _ in units[:(g + 1) * HEADS])
                        dve.wait_ge(sem["sink_exp"], st.at("sink_exp", sinks))
                        step(dve.tensor_tensor(total, total, small[:, c + 8:c + 12], ALU.add))
                    step(dve.reciprocal(small[:, c + 16:c + 20], total))
                    if g >= 2:
                        dve.wait_ge(sem["full7"], at_bank(st, 7, g - 2))
                    dve.tensor_tensor(y_tok[:, g % 2, :].rearrange("p (h d) -> p h d", d=HD),
                                      bank[:, 6, 0:HEADS * HD].rearrange("p (h d) -> p h d", d=HD),
                                      per_row(small[:, c + 16:c + 20], HEADS, HD), ALU.mult).then_inc(sem["free6"], 1)

                n = len(units)
                for i in range(n + 2):
                    if i < n:
                        maximum(i)
                    if 1 <= i <= n:
                        take_probs(i - 1)
                    if i < TAPS_B:
                        tap(i)
                    if i >= 2 and (i - 2) % HEADS == HEADS - 1:
                        rows_of_y((i - 2) // HEADS)

            def conv_out(st):
                n = NTOK if st.layer == 0 else SEQ
                dve.wait_ge(sem["full0"], at_bank(st, 0, 0))
                for c in range(2):
                    ins = dve.tensor_tensor(HT[:, 2 + c, 0:n], HT[:, 2 + c, 0:n], flat_bank[:, 0:n], ALU.subtract)
                    ins.then_inc(sem["centered" if c == 0 else "free0"], 1)
                dve.wait_ge(sem["free0"], at_bank(st, 0, 1))
                step(dve.reciprocal(u_rstd[:, 0:n], u_rstd[:, 0:n]))
                for c in range(2):
                    dve.tensor_tensor(HT[:, 2 + c, 0:n], HT[:, 2 + c, 0:n], u_rstd[:, 0:n], ALU.mult)\
                       .then_inc(sem["normed"], 1)

            def w_out(st):
                dve.wait_ge(sem["rows_loaded"], st.at("rows_loaded", 32))
                for i in range(st.facts["tiles"]):
                    b = 2 * (i % 4)
                    dve.wait_ge(sem[f"full{b}"], at_bank(st, b, i // 4))
                    dve.tensor_tensor(h_tok[:, i % 2, :], flat_bank[:, b * BANK:b * BANK + D],
                                      mod[:, 0 if i < ST else 1, :], ALU.mult).then_inc(sem[f"free{b}"], 1)
                    dve.wait_ge(sem[f"free{b}"], at_bank(st, b, i // 4))
                    step(dve.tensor_tensor(X[:, i, :], X[:, i, :], h_tok[:, i % 2, :], ALU.add))

            def route(st):
                tiles = st.facts["tiles"]
                dve.wait_ge(sem["full0"], at_bank(st, 0, 0))
                logits = bank[:, 0, 0:tiles * EXPERTS].rearrange("p (t e) -> p t e", e=EXPERTS)
                v = aff[:, 0:tiles, :]
                step(dve.tensor_reduce(small[:, 0:tiles], logits, AX.X, ALU.max))
                dve.tensor_tensor(v, logits, per_row(small[:, 0:tiles], tiles, EXPERTS), ALU.subtract)\
                   .then_inc(sem["free0"], 1)
                dve.wait_ge(sem["logit_exp"], st.at("logit_exp", 1))
                step(dve.tensor_reduce(small[:, 8:8 + tiles], v, AX.X, ALU.add))
                step(dve.reciprocal(small[:, 16:16 + tiles], small[:, 8:8 + tiles]))
                dve.tensor_tensor(v, v, per_row(small[:, 16:16 + tiles], tiles, EXPERTS), ALU.mult)\
                   .then_inc(sem["affinity"], 1)
                places = y_rows[0:EXPERTS, 0, 0:NS].bitcast(U32)
                for part, (lo, hi, cap, c0) in enumerate(((0, SEQ, CAP_X, 0), (SEQ, NTOK, CAP_C, CAP_X))):
                    if part * ST >= tiles:
                        continue
                    b = 1 + part
                    values = affT[0:EXPERTS, lo:hi]
                    dve.wait_ge(sem[f"full{b}"], at_bank(st, b, 0))
                    dve.tensor_copy(values, bank[0:EXPERTS, b, 0:hi - lo]).then_inc(sem[f"free{b}"], 1)
                    dve.wait_ge(sem[f"free{b}"], at_bank(st, b, 0))
                    for r in range(cap // 8):
                        cols = slice(c0 + 8 * r, c0 + 8 * r + 8)
                        step(dve.max(top[0:EXPERTS, cols], values))
                        step(dve.max_index(places[:, cols], top[0:EXPERTS, cols], values))
                        step(dve.match_replace(values, top[0:EXPERTS, cols], values, -1.0))
                n = NS if tiles > ST else CAP_X
                ins = dve.tensor_copy(top_at[0:EXPERTS, 0:n], places[:, 0:n])
                if tiles > ST:
                    step(ins)
                    v = top_at[0:EXPERTS, CAP_X:NS]
                    ins = dve.tensor_scalar(v, v, float(SEQ), None, ALU.add)
                ins.then_inc(sem["ranked"], 1)
                dve.wait_ge(sem["full3"], at_bank(st, 3, 0))
                dve.tensor_copy(index_t[0:n, 0:EXPERTS], bank[0:n, 3, 0:EXPERTS])
                dve.tensor_copy(index_t[0:n, EXPERTS:EXPERTS + 2], bank[0:n, 3, 0:2])
                dve.tensor_copy(gate_t[0:n, :], bank[0:n, 3, EXPERTS:2 * EXPERTS]).then_inc(sem["free3"], 1)

            def experts(st):
                n = NS if st.facts["tiles"] > ST else CAP_X

                def split(pair, q):
                    w = slot_of(st.first_unit + q).rearrange("p (k n) -> p k n", k=KD)
                    for half in range(2):
                        rows = slice(4 * half, 4 * half + 4)
                        dve.wait_ge(sem["w_high"], st.at("w_high", 2 * q + half + 1) + pair * 24)
                        dve.tensor_tensor(low_of(st.first_unit + q)[:, rows, :], w[:, rows, :],
                                          w_high[q % 3][:, rows, :].bitcast(F32), ALU.subtract).then_inc(sem["w_split"], 1)

                def take_rows(e):
                    for b in range(2):
                        rows = slice(4 * b, 4 * b + 4)
                        dve.wait_ge(sem["x_high"], st.at("x_high", b + 1) + e * 2)
                        dve.tensor_tensor(xT_low[:, rows, 0:n], bank[:, b, 0:4 * n].rearrange("p (k n) -> p k n", k=4),
                                          xT_high[:, rows, 0:n].bitcast(F32), ALU.subtract).then_inc(sem[f"free{b}"], 1)

                def product_of(e, half):
                    b = 3 + 2 * half
                    dve.wait_ge(sem[f"free{b - 1}"], at_bank(st, b - 1, e))
                    dve.wait_ge(sem[f"full{b}"], at_bank(st, b, 2 * e))
                    cols = slice(512 * half, 512 * half + 512)
                    dve.tensor_tensor(act_rows[0:n, cols], bank[0:n, b, :], gate_rows[0:n, cols], ALU.mult)\
                        .then_inc(sem[f"free{b}"], 1)

                def take_act(e, half):
                    b, rows = 3 + 2 * half, slice(4 * half, 4 * half + 4)
                    dve.wait_ge(sem["act_high"], st.at("act_high", half + 1) + e * 2)
                    dve.tensor_tensor(actT_low[:, rows, 0:n], bank[:, b, 0:4 * n].rearrange("p (k n) -> p k n", k=4),
                                      actT_high[:, rows, 0:n].bitcast(F32), ALU.subtract).then_inc(sem[f"free{b}"], 1)

                def two_experts(pair, last):
                    for h in range(2):
                        e = pair * 2 + h
                        split(pair, 6 * h + 2)
                        split(pair, 6 * h + 3)
                        product_of(e, 0)
                        split(pair, 6 * h + 4)
                        split(pair, 6 * h + 5)
                        product_of(e, 1)
                        take_act(e, 0)
                        take_rows(e + 1)
                        take_act(e, 1)
                        if not (last and h):
                            split(pair, 6 * h + 6)
                        step(dve.tensor_copy(now[0:n, h:h + 1], gate_t[0:n, bass.ds(e, 1)]))
                        dve.wait_ge(sem["y_free"], st.at("y_free", 1) + e)
                        for j in range(2):
                            if j and not (last and h):
                                split(pair, 6 * h + 7)
                            dve.wait_ge(sem[f"full{6 + j}"], at_bank(st, 6 + j, e))
                            dve.tensor_scalar(y_rows[0:n, h, 512 * j:512 * j + 512], bank[0:n, 6 + j, :],
                                              now[0:n, h:h + 1], None, ALU.mult).then_inc(sem[f"free{6 + j}"], 1)

                for q in range(2):
                    split(0, q)
                take_rows(0)
                turns = EXPERTS // 2 - 1
                with dve.Fori(0, turns) as pair:
                    step.begin_loop(pair, 2)
                    two_experts(pair, False)
                step.end_loop(turns)
                two_experts(turns, True)

            def combine(st):
                dve.wait_ge(sem["rows_loaded"], st.at("rows_loaded", 32))
                for i in range(st.facts["tiles"]):
                    q = i % 2
                    dve.wait_ge(sem[f"moe_rows{q}"], st.at(f"moe_rows{q}", 16 * (i // 2 + 1)))
                    h = h_tok[:, q, :]
                    step(dve.tensor_tensor(h, h, mod[:, 0 if i < ST else 1, :], ALU.mult))
                    dve.tensor_tensor(X[:, i, :], X[:, i, :], h, ALU.add).then_inc(sem["added"], 1)

            def norm_rows(st):
                dve.wait_ge(sem["rows_loaded"], st.at("rows_loaded", 16))
                for t in range(ST):
                    dve.wait_ge(sem["mean_root"], st.at("mean_root", t + 1))
                    step(dve.reciprocal(small[:, 16 + t:17 + t], small[:, 8 + t:9 + t]))
                    step(dve.scalar_tensor_tensor(X[:, t, :], X[:, t, :], small[:, 16 + t:17 + t], mod[:, 0, :],
                                                  ALU.mult, ALU.mult))

            def angles(st):
                dve.wait_ge(sem["tables_loaded"], st.at("tables_loaded", 16 * 5))
                step(dve.tensor_tensor(lam_in[:, 0:2, :], lam_in[:, 0:2, :], lam_in[:, 2:4, :], ALU.mult))
                dve.tensor_reduce(lam[:, 0:2], lam_in[:, 0:2, :], AX.X, ALU.add).then_inc(sem["lam_sum"], 1)
                step(dve.tensor_copy(pos_f, positions))
                step(dve.tensor_tensor(angle, pos_f.unsqueeze(2).broadcast_to([P, ST, ANGLES]),
                                       freq.unsqueeze(1).broadcast_to([P, ST, ANGLES]), ALU.mult))
                turn = 2 * np.pi
                parts = [6.28125]
                parts.append(float(np.float32(np.round((turn - parts[0]) * 2 ** 21) / 2 ** 21)))
                parts.append(float(np.float32(turn - parts[0] - parts[1])))
                for table, quarter in ((sin2, 0.0), (cos2, 0.25)):
                    v = table[:, :, :]
                    step(dve.tensor_scalar(whole, angle, float(1 / turn), quarter, ALU.mult, ALU.add))
                    step(dve.tensor_scalar(whole, whole, ROUND, None, ALU.add))
                    step(dve.tensor_scalar(whole, whole, ROUND, None, ALU.subtract))
                    source = angle
                    for part in parts:
                        step(dve.scalar_tensor_tensor(v, whole, -part, source, ALU.mult, ALU.add))
                        source = v
                    step(dve.tensor_scalar(v, v, float(quarter * turn), None, ALU.add))
                    ins = dve.tensor_scalar(v, v, 3.1415925, -3.1415925, ALU.min, ALU.max)
                    if table is sin2:
                        step(ins)
                ins.then_inc(sem["angles"], 1)
                dve.wait_ge(sem["lam_exp"], st.at("lam_exp", 1))
                step(dve.tensor_tensor(lam[:, 2:3], lam[:, 1:2], lam[:, 0:1], ALU.subtract))
                step(dve.tensor_scalar(lam[:, 2:3], lam[:, 2:3], LAM_INIT, None, ALU.subtract))
                step(dve.tensor_scalar(subln[:, :], subln[:, :], 1.0 - LAM_INIT, None, ALU.mult))

            def ffn_up(st):
                def split(g):
                    c, n = g // 2, g % 2
                    unit = st.first_unit + 2 * (c // 4) + n
                    dve.wait_ge(sem["w_high"], st.at("w_high", g + 1))
                    dve.tensor_tensor(ffn_columns(low_flat(unit), c), ffn_columns(slot_of(unit), c),
                                      chunk_high[:, g % SPLIT_RING, :, :].bitcast(F32), ALU.subtract).then_inc(sem["w_split"], 1)

                for g in range(4):
                    split(g)
                for c in range(F_CHUNKS):
                    b = 2 * (c % 4)
                    for g in (2 * c + 4, 2 * c + 5):
                        if g < 2 * F_CHUNKS:
                            split(g)
                    dve.wait_ge(sem[f"free{b}"], at_bank(st, b, c // 4))
                    dve.wait_ge(sem[f"full{b + 1}"], at_bank(st, b + 1, c // 4))
                    dve.tensor_tensor(ffnT[:, c, :], bank[:, b + 1, :], ffn_gate[:, c % 2, :], ALU.mult)\
                        .then_inc(sem[f"free{b + 1}"], 1)

            def ffn_down(st):
                for k in range(F_CHUNKS):
                    unit, cols = st.first_unit + k // 4, slice(k % 4 * D, k % 4 * D + D)
                    dve.wait_ge(sem["w_high"], st.at("w_high", k + 1))
                    dve.tensor_tensor(ffnT_low[:, k, :], ffnT[:, k, :], ffnT_high[:, k % SPLIT_RING, :].bitcast(F32), ALU.subtract)
                    dve.tensor_tensor(low_flat(unit)[:, cols], slot_of(unit)[:, cols],
                                      down_high[:, k % SPLIT_RING, :].bitcast(F32), ALU.subtract).then_inc(sem["w_split"], 1)
                for half in range(2):
                    for t in range(ST):
                        b = 4 * half + t
                        v = X[:, t, 512 * half:512 * half + 512]
                        dve.wait_ge(sem[f"full{b}"], at_bank(st, b, 0))
                        dve.scalar_tensor_tensor(v, bank[:, b, :], 0.5, v, ALU.mult, ALU.add).then_inc(sem[f"free{b}"], 1)

            def rotate(i, dst, src, heads, half, first):
                def per_head(table):
                    return table[:, i, first:first + half].unsqueeze(1).broadcast_to([P, heads, half])

                def temp(v):
                    return v[:, 0:heads * half].rearrange("p (h d) -> p h d", d=half)
                x1, x2 = src[:, :, 0:half], src[:, :, half:2 * half]
                ta, tb = temp(turn_a), temp(turn_b)
                step(dve.tensor_tensor(ta, x2, per_head(sin2), ALU.mult))
                step(dve.tensor_tensor(tb, x1, per_head(sin2), ALU.mult))
                step(dve.tensor_tensor(dst[:, :, 0:half], x1, per_head(cos2), ALU.mult))
                step(dve.tensor_tensor(dst[:, :, half:2 * half], x2, per_head(cos2), ALU.mult))
                step(dve.tensor_tensor(dst[:, :, 0:half], dst[:, :, 0:half], ta, ALU.subtract))
                return dve.tensor_tensor(dst[:, :, half:2 * half], dst[:, :, half:2 * half], tb, ALU.add)

            def latent_in(st):
                for i in range(ST):
                    b = i % 2
                    dve.wait_ge(sem["latent_root"], st.at("latent_root", 2 * i + 2))
                    r = small[:, 32 + 2 * i:34 + 2 * i]
                    step(dve.reciprocal(r, small[:, 16 + 2 * i:18 + 2 * i]))
                    if i >= 2:
                        dve.wait_ge(sem[f"full{2 + b}"], at_bank(st, 2 + b, i // 2 - 1))
                    step(dve.tensor_scalar(z_lat[:, b, 0:Q_RANK], bank[:, b, 0:Q_RANK], r[:, 0:1], None, ALU.mult))
                    dve.tensor_scalar(z_lat[:, b, Q_RANK:Q_RANK + KV_RANK], bank[:, b, Q_RANK:Q_RANK + KV_RANK], r[:, 1:2],
                                      None, ALU.mult).then_inc(sem["latent"], 1)
                    step(dve.tensor_copy(z_lat[:, b, Q_RANK + KV_RANK:LATENT], bank[:, b, Q_RANK + KV_RANK:LATENT]))
                    step(rotate(i, rot_k[:, i:i + 1, :], z_lat[:, b, Q_RANK + KV_RANK:LATENT].unsqueeze(1), 1, ROT // 2, 0))
                    dve.memset(small[:, 90:91], 0.0).then_inc(sem[f"free{b}"], 1)

            def latent_qk(st):
                for i in range(ST):
                    q = q_rows[:, i % 2, :].rearrange("p (h d) -> p h d", d=L_QK)
                    k = k_rows[:, i % 2, :].rearrange("p (h d) -> p h d", d=L_QK)
                    if i >= 2:
                        for b in range(4, 8):
                            dve.wait_ge(sem[f"full{b}"], at_bank(st, b, i - 2))
                    dve.wait_ge(sem["full0"], at_bank(st, 0, i))
                    dve.tensor_copy(q_rows[:, i % 2, :], flat_bank[:, 0:L_HEADS * L_QK]).then_inc(sem["free0"], 1)
                    dve.wait_ge(sem["free0"], at_bank(st, 0, i))
                    rotate(i, q[:, :, NOPE:L_QK], q[:, :, NOPE:L_QK], L_HEADS, ROT // 2, 0).then_inc(sem["q_rows"], 1)
                    dve.wait_ge(sem["q_rows"], st.at("q_rows", i + 1))
                    kv = flat_bank[:, 2 * BANK:2 * BANK + L_HEADS * (NOPE + L_V)].rearrange("p (h d) -> p h d", h=L_HEADS)
                    dve.wait_ge(sem["full2"], at_bank(st, 2, i))
                    dve.tensor_copy(k[:, :, 0:NOPE], kv[:, :, 0:NOPE])
                    dve.tensor_copy(v_lat[:, i, :].rearrange("p (h d) -> p h d", h=L_HEADS), kv[:, :, NOPE:])\
                        .then_inc(sem["free2"], 1)
                    dve.tensor_copy(k[:, :, NOPE:L_QK], rot_k[:, i:i + 1, :].broadcast_to([P, L_HEADS, ROT]))\
                        .then_inc(sem["k_rows"], 1)

            def diff_in(st):
                for i in range(ST):
                    rows = qk_diff[:, i % 2, :]
                    heads = rows.rearrange("p (h d) -> p h d", d=HD)
                    if i >= 2:
                        for b in (4, 5):
                            dve.wait_ge(sem[f"full{b}"], at_bank(st, b, i - 2))
                    dve.wait_ge(sem["full0"], at_bank(st, 0, i))
                    dve.tensor_copy(rows, flat_bank[:, 0:2 * D_W]).then_inc(sem["free0"], 1)
                    dve.wait_ge(sem["free0"], at_bank(st, 0, i))
                    n = 2 * D_W // HD
                    rotate(i, heads[:, :, 0:D_ROT], heads[:, :, 0:D_ROT], n, D_ROT // 2, ROT // 2)\
                        .then_inc(sem["qk_rows"], 1)
                    dve.wait_ge(sem["qk_rows"], st.at("qk_rows", i + 1))

            def attend_two(st):
                units = units_two()
                scales = (L_QK ** -0.5, HD ** -0.5)

                def maximum(i):
                    kind, qt, h, s = units[i]
                    n, b = (qt + 1) * P, i % 2
                    dve.wait_ge(sem[f"full{b}"], at_bank(st, b, i // 2))
                    m = small[:, 40 + i % 8:41 + i % 8]
                    step(dve.tensor_reduce(m, bank[:, b, 0:n], AX.X, ALU.max))
                    dve.tensor_scalar(small[:, i % 8:i % 8 + 1], m, -scales[kind], None, ALU.mult).then_inc(sem["neg_max"], 1)

                def take_probs(i):
                    n, b = (units[i][1] + 1) * P, 2 + i % 2
                    dve.wait_ge(sem[f"full{b}"], at_bank(st, b, i // 2))
                    dve.tensor_copy(probs2T[:, i % 2, 0:n], bank[:, b, 0:n]).then_inc(sem[f"free{b}"], 1)

                def rows_of_y(g):
                    kind = units[2 * g][0]
                    b = 4 + g % 2
                    c = 2 * (g % 4)
                    r = small[:, 24 + c:26 + c]
                    y = y_rows2[:, g % 2, :]
                    dve.wait_ge(sem[f"full{b}"], at_bank(st, b, g // 2))
                    step(dve.reciprocal(r, small[:, 16 + c:18 + c]))
                    if g >= 2:
                        dve.wait_ge(sem[f"full{6 + g % 2}"], at_bank(st, 6 + g % 2, g // 2 - 1))
                    if kind == 0:
                        step(dve.tensor_tensor(y.rearrange("p (s d) -> p s d", s=2),
                                               bank[:, b, 0:P].rearrange("p (s d) -> p s d", s=2), per_row(r, 2, L_V), ALU.mult))
                    else:
                        step(dve.tensor_tensor(small[:, 60:61], r[:, 1:2], lam[:, 2:3], ALU.mult))
                        step(dve.tensor_scalar(y, bank[:, b, 0:P], r[:, 0:1], None, ALU.mult))
                        step(dve.scalar_tensor_tensor(y, bank[:, b, P:2 * P], small[:, 60:61], y, ALU.mult, ALU.add))
                        step(dve.tensor_tensor(squares2[:, :], y, y, ALU.mult))
                        k = g - 4 * L_HEADS // 2
                        dve.tensor_reduce(small[:, 62 + g % 2:63 + g % 2], squares2[:, :], AX.X, ALU.add).then_inc(sem["y_sum"], 1)
                        dve.wait_ge(sem["y_root"], st.at("y_root", k + 1))
                        step(dve.reciprocal(small[:, 66:67], small[:, 64 + g % 2:65 + g % 2]))
                        step(dve.scalar_tensor_tensor(y, y, small[:, 66:67], subln[:, :], ALU.mult, ALU.mult))
                    dve.memset(small[:, 90:91], 0.0).then_inc(sem[f"free{b}"], 1)
                    dve.wait_ge(sem[f"free{b}"], at_bank(st, b, g // 2))
                    dve.memset(small[:, 90:91], 0.0).then_inc(sem["y_rows"], 1)
                    dve.wait_ge(sem["y_rows"], st.at("y_rows", g + 1))

                n = len(units)
                for i in range(n + 2):
                    if i < n:
                        maximum(i)
                    if 1 <= i <= n:
                        take_probs(i - 1)
                    if i >= 2 and (i - 2) % 2 == 1:
                        rows_of_y((i - 2) // 2)

            def merge(st):
                def split(c, m):
                    unit, turn = st.first_unit + 3 * (c // 4) + m, merge_turn(c, m)
                    cols = tile_cols(c % 4)
                    dve.wait_ge(sem["w_high"], st.at("w_high", turn + 1))
                    dve.tensor_tensor(low_of(unit)[:, :, cols], slot_of(unit).rearrange("p (k n) -> p k n", k=KD)[:, :, cols],
                                      merge_high[turn % 4][:, :, :].bitcast(F32), ALU.subtract).then_inc(sem["w_split"], 1)

                def rows(source, x):
                    for k in range(KD):
                        dve.wait_ge(sem["rows_high"], st.at("rows_high", KD * source + k + 1))
                        dve.tensor_tensor(mergeT_low[source][:, k, 0:SEQ], x[:, k, 0:SEQ],
                                          mergeT_high[source][:, k, :].bitcast(F32), ALU.subtract).then_inc(sem["rows_split"], 1)

                split(0, 1)
                rows(0, HT)
                split(0, 0)
                rows(1, yT)
                split(0, 2)
                for c in range(KD):
                    b, use = 4 * (c % 2), c // 2
                    if c + 1 < KD:
                        split(c + 1, 1)
                    gates = merge_gate[:, c % 2, :].rearrange("p (a n) -> p a n", a=2)
                    out_ = mergedT[:, c, :]
                    for n in range(2):
                        dve.wait_ge(sem[f"free{b + 2 * n}"], at_bank(st, b + 2 * n, use))
                        dve.wait_ge(sem[f"full{b + 2 * n + 1}"], at_bank(st, b + 2 * n + 1, use))
                        dve.tensor_tensor(gates[:, n, :] if n else out_, bank[:, b + 2 * n + 1, :], gates[:, n, :], ALU.mult)\
                            .then_inc(sem[f"free{b + 2 * n + 1}"], 1)
                        if c + 1 < KD:
                            split(c + 1, 0 if n == 0 else 2)
                    dve.wait_ge(sem[f"free{b + 3}"], at_bank(st, b + 3, use))
                    dve.tensor_tensor(out_, out_, gates[:, 1, :], ALU.add).then_inc(sem["merged"], 1)

            def project(st):
                for i in range(ST):
                    b = 2 * i
                    dve.wait_ge(sem[f"full{b}"], at_bank(st, b, 0))
                    dve.tensor_tensor(X[:, i, :], X[:, i, :], flat_bank[:, b * BANK:b * BANK + D], ALU.add)\
                        .then_inc(sem[f"free{b}"], 1)

            programs = dict(init=init, ada=ada, norm=norm, conv_in=conv_in, qkv=qkv, attend=attend, conv_out=conv_out,
                            w_out=w_out, route=route, experts=experts, combine=combine, norm_rows=norm_rows,
                            angles=angles, ffn_up=ffn_up, ffn_down=ffn_down, latent_in=latent_in, latent_qk=latent_qk,
                            diff_in=diff_in, attend_two=attend_two, merge=merge, project=project)
            for st in stages:
                if st.name in programs:
                    enter(dve, st)
                    programs[st.name](st)
                elif st.number:
                    dve.wait_ge(sem["vector_finished"], st.number)
                dve.memset(done_mark[:, 1:2], 0.0).then_inc(sem["vector_finished"], 1)

        @block.gpsimd
        def _(pool):
            step = Steps(pool, sem["gpsimd_steps"])

            def init(st):
                step(pool.memset(eps[:, :], EPS))
                step(pool.memset(zeros[:, :], 0.0))

            def load_mods(st, rows):
                for n, (row, comp) in enumerate(rows):
                    pool.dma_start(mod[:, n, :], mods_rows[st.layer][row, comp * D:comp * D + D].partition_broadcast(P))\
                        .then_inc(sem["rows_loaded"], 16)

            def ada(st):
                pool.dma_start(ada_bias[0:2, :], a["ada_b"][st.layer]).then_inc(sem["rows_loaded"], 16)
                pool.dma_start(norm_gain[0:2, :, :], a["norm_gains"][st.layer]).then_inc(sem["rows_loaded"], 16)
                if st.layer == 0:
                    constants = (
                        (ident, a["ident"]), (band, a["band"]), (rope_cos, a["rope_cos"]), (rope_sin, a["rope_sin"]),
                        (head_gain, a["head_gain"]), (conv_a_w, a["conv_a_w"]), (conv_b_w, a["conv_b_w"]),
                        (conv_vec, a["conv_vec"]), (sink, a["sink"]), (router, a["router_w"]))
                    for dst, src in constants:
                        pool.dma_start(dst[tuple([slice(None)] * len(dst.shape))], src).then_inc(sem["constants"], 16)
                    for lo, hi, src in ((0, ST, a["x"]), (ST, ST + CT, a["ctx"])):
                        pool.dma_start(X[:, lo:hi, :], src.rearrange("(t p) d -> p t d", p=P)).then_inc(sem["constants"], 16)
                    pool.wait_ge(sem["constants"], 16 * (len(constants) + 2))
                pool.wait_ge(sem["mods_rows"], st.at("mods_rows", 1))
                pool.dma_start(mods_rows[st.layer], HT[0:2, :, :].rearrange("p k n -> p (k n)")).then_inc(sem["mods_stored"], 16)
                pool.wait_ge(sem["mods_stored"], st.at("mods_stored", 16))

            def norm(st):
                tiles, row = st.facts["tiles"], st.facts["row"]
                if st.facts["shift"] is not None:
                    load_mods(st, [(row, st.facts["scale"]), (row, st.facts["shift"])])
                if st.facts["store"]:
                    for i, t in enumerate(tiles):
                        pool.wait_ge(sem["h_ready"], st.at("h_ready", i + 1))
                        pool.dma_start(h_rows[st.layer][t * P:(t + 1) * P, :], h_tok[:, i % 2, :])\
                            .then_inc(sem[f"h_stored{i % 2}"], 16)
                    for q in range(2):
                        pool.wait_ge(sem[f"h_stored{q}"], st.at(f"h_stored{q}", 16 * len(tiles[q::2])))
                elif st.facts["shift"] is None:
                    pool.dma_start(mod[:, 0, :], a[st.facts["gain"]].partition_broadcast(P)).then_inc(sem["rows_loaded"], 16)
                pool.wait_ge(sem["rows_loaded"], st.at("rows_loaded", st.signals["rows_loaded"]))

            def angles(st):
                for dst, src in ((positions, a["positions_2"]), (freq, a["freq"]), (lam_in, a["lam_2"]),
                                 (latent_gain[:, :], a["latent_gain"]), (subln[:, :], a["subln_2"])):
                    pool.dma_start(dst, src).then_inc(sem["tables_loaded"], 16)
                pool.wait_ge(sem["tables_loaded"], st.at("tables_loaded", 16 * 5))

            def attend(st):
                l = st.layer
                parts = [(0, SEQ)] + ([(SEQ, NTOK)] if l == 0 else [])
                for part, (lo, hi) in enumerate(parts):
                    n = hi - lo
                    for c, source, weights, taps, pad, dst in (
                            (0, conv_a_in, conv_a_w, TAPS_A, PAD_A, HT[:, 0, lo:hi]),
                            (1, conv_a_in, conv_a_w, TAPS_A, PAD_A, HT[:, 1, lo:hi]),
                            (0, conv_b_in, conv_b_w, TAPS_B, PAD_B, HT[:, 2, lo:hi])):
                        start = part * (SEQ + 2 * pad)

                        def tap(k, dst):
                            return pool.tensor_tensor(dst, source[:, c, start + k:start + k + n],
                                                      weights[:, l, c, k:k + 1].broadcast_to([P, n]), ALU.mult)

                        step.later(tap(0, dst))
                        step.later(tap(1, tap_out[:, 1, 0:n]))
                        for k in range(1, taps):
                            if k + 1 < taps:
                                step.later(tap(k + 1, tap_out[:, (k + 1) % 3, 0:n]))
                            step.wait_for(1 if k + 1 < taps else 0)
                            step.later(pool.tensor_tensor(dst, dst, tap_out[:, k % 3, 0:n], ALU.add))
                        step.wait_for(0)
                        other = conv_vec[:, 0, l, 0:1].broadcast_to([P, n]) if taps == TAPS_B else conv_a_gate[:, c, lo:hi]
                        step(pool.tensor_tensor(dst, dst, other, ALU.add if taps == TAPS_B else ALU.mult))

            def qkv(st):
                if st.layer:
                    return
                for l in range(LAYERS):
                    for t in range(ST + CT if l == 0 else ST):
                        pool.dma_start(moe_rows[l][t * P:(t + 1) * P, :].rearrange("p (a b) -> p a b", b=P),
                                       zeros[:, :].unsqueeze(1).broadcast_to([P, KD, P])).then_inc(sem["moe_cleared"], 16)
                pool.wait_ge(sem["moe_cleared"], 16 * (ST + CT + ST))

            def w_out(st):
                load_mods(st, [(0, 2), (1, 2)])
                pool.wait_ge(sem["rows_loaded"], st.at("rows_loaded", 32))

            def experts(st):
                n = NS if st.facts["tiles"] > ST else CAP_X
                tail = now.bitcast(U32)
                tokens = st.facts["tiles"] * P
                rows, sums = h_rows[st.layer][0:tokens, :], moe_rows[st.layer][0:tokens, :]

                def gather(index, half):
                    pool.indirect_dma_start(xs[0:n, half, :], None, rows, bass.IndirectOffsetOnAxis(ap=index, axis=0))\
                        .then_inc(sem[f"gathered{half}"], 16)

                def index_ready():
                    step.later(pool.tensor_tensor(done_mark[:, 3:4], eps[:, :], eps[:, :], ALU.add))

                for half in range(2):
                    gather(index_t[0:n, half:half + 1], half)
                step.wait_for(0)
                pool.tensor_copy(done_mark[:, 2:3], eps[:, :]).then_inc(sem["y_free"], 2)
                with pool.Fori(0, EXPERTS // 2) as pair:
                    step.begin_loop(pair, 8)
                    for h in range(2):
                        e = pair * 2 + h
                        for b in range(2):
                            pool.wait_ge(sem[f"full{b}"], at_bank(st, b, e))
                        step(pool.tensor_copy(tail[0:n, 2:3], index_t[0:n, bass.ds(e + 2, 1)]))
                        index_ready()
                        gather(tail[0:n, 2:3], h)
                        step(pool.tensor_copy(tail[0:n, 3:4], index_t[0:n, bass.ds(e, 1)]))
                        for j in range(2):
                            pool.wait_ge(sem[f"free{6 + j}"], at_bank(st, 6 + j, e))
                        index_ready()
                        pool.indirect_dma_start(sums, bass.IndirectOffsetOnAxis(ap=tail[0:n, 3:4], axis=0),
                                                y_rows[0:n, h, :], None, compute_op=ALU.add).then_inc(sem["scattered"], 16)
                        pool.wait_ge(sem["scattered"], st.at("scattered", 16) + e * 16)
                        pool.tensor_tensor(done_mark[:, 2:3], eps[:, :], eps[:, :], ALU.add).then_inc(sem["y_free"], 1)
                step.end_loop(EXPERTS // 2)
                pool.wait_ge(sem["y_free"], st.at("y_free", EXPERTS + 2))
                for half in range(2):
                    pool.wait_ge(sem[f"gathered{half}"], st.at(f"gathered{half}", 8 * EXPERTS + 16))

            def combine(st):
                load_mods(st, [(0, 5), (1, 5)])
                for i in range(st.facts["tiles"]):
                    q = i % 2
                    if i >= 2:
                        pool.wait_ge(sem["added"], st.at("added", i - 1))
                    pool.dma_start(h_tok[:, q, :], moe_rows[st.layer][i * P:(i + 1) * P, :]).then_inc(sem[f"moe_rows{q}"], 16)
                pool.wait_ge(sem["rows_loaded"], st.at("rows_loaded", 32))

            def store(st):
                pool.dma_start(out.rearrange("(t p) d -> p t d", p=P), X[:, 0:ST, :]).then_inc(sem["stored"], 16)
                pool.wait_ge(sem["stored"], 16)

            programs = dict(init=init, ada=ada, norm=norm, qkv=qkv, attend=attend, w_out=w_out, experts=experts,
                            combine=combine, store=store, norm_rows=norm, angles=angles)
            for st in stages:
                if st.name in programs:
                    enter(pool, st)
                    programs[st.name](st)
                elif st.number:
                    pool.wait_ge(sem["gpsimd_finished"], st.number)
                pool.memset(done_mark[:, 2:3], 0.0).then_inc(sem["gpsimd_finished"], 1)


def rope_tables():
    quarter = HD // 4
    inv = np.float32(10000.0) ** (-np.arange(quarter, dtype=np.float32) / np.float32(quarter))
    row = np.repeat(np.arange(SEQ // GRID_W), GRID_W).astype(np.float32)
    col = (np.arange(SEQ) % GRID_W).astype(np.float32)
    ar, ac = row[:, None] * inv, col[:, None] * inv
    ang = np.concatenate([ar, ar, ac, ac], axis=-1)
    sign = np.repeat(np.array([-1, 1, -1, 1], np.float32), quarter)
    return np.cos(ang), np.sin(ang) * sign


def host_arrays(i):
    def tiles(v):
        return np.ascontiguousarray(v.reshape(ST, P, -1).transpose(1, 0, 2))

    def by_channel(v):
        v = v.reshape(LAYERS, 2, P, *v.shape[2:])
        return np.ascontiguousarray(np.moveaxis(v, 2, 0))

    cos, sin = rope_tables()
    j, q = np.arange(P)[None, :], np.arange(P)[:, None]
    band = np.stack([np.where(j >= q, 0.0, MASKED), np.where(j <= q, 0.0, MASKED)], 1).astype(np.float32)
    pair = np.stack([i["c"].reshape(D), i["c_ctx"]])
    gains = np.concatenate([np.repeat(i["q_norm_g"][:, None], 4, 1), np.repeat(i["k_norm_g"][:, None], 2, 1)], 1)
    host = dict(
        x=i["x"][0], ctx=i["ctx"][0], c_pair=np.ascontiguousarray(pair.reshape(2, KD, P).transpose(2, 1, 0)),
        ident=np.eye(P, dtype=np.float32), band=band, rope_cos=tiles(cos), rope_sin=tiles(sin),
        head_gain=np.ascontiguousarray(np.broadcast_to(gains[None], (P, LAYERS, 6, HD))),
        conv_a_w=by_channel(i["conv_a_w"].transpose(0, 2, 1)), conv_b_w=by_channel(i["conv_b_w"].transpose(0, 2, 1)),
        conv_vec=np.ascontiguousarray(np.stack([by_channel(i[n]) for n in ("conv_b_b", "conv_ln_g", "conv_ln_b")], 1)),
        sink=np.ascontiguousarray(np.broadcast_to(i["sink"][None], (P, LAYERS, HEADS))),
        router_w=np.ascontiguousarray(i["router_w"].reshape(LAYERS, KD, P, EXPERTS).transpose(2, 0, 1, 3)),
        ada_b=np.ascontiguousarray(np.broadcast_to(i["ada_b"][:, None], (LAYERS, 2, 6 * D))),
        norm_gains=np.ascontiguousarray(np.broadcast_to(
            np.stack([i["norm1_g"], i["norm2_g"]], 1)[:, None], (LAYERS, 2, 2, D))))
    inv = np.concatenate([np.power(np.float32(THETA), np.float32(-2.0) * np.arange(r // 2, dtype=np.float32) / np.float32(r))
                          for r in (ROT, D_ROT)]).astype(np.float32)
    lams = np.stack([i[f"diff_lam_{n}_2"][0] for n in ("q1", "q2", "k1", "k2")])

    def rows(v):
        return np.ascontiguousarray(np.broadcast_to(v[None], (P, *v.shape)))

    host.update(
        freq=rows(inv), lam_2=rows(lams), subln_2=rows(i["diff_subln_2"][0]),
        positions_2=np.ascontiguousarray(i["positions_2"].reshape(ST, P).T),
        latent_gain=np.ascontiguousarray(np.concatenate([i["mla_q_norm_2"][0], i["mla_kv_norm_2"][0]]).reshape(3, P).T),
        w_proj_2=np.concatenate([i["w_proj_mla_2"][0], i["w_proj_diff_2"][0]]), final_g=i["final_g"],
        ffn1_norm_2=i["ffn1_norm_2"][0], mix_norm_2=i["mix_norm_2"][0], ffn2_norm_2=i["ffn2_norm_2"][0],
        final_norm_2=i["final_norm_2"])
    for name in ("ffn1_w_gate_2", "ffn1_w_up_2", "ffn1_w_down_2", "w_in_2", "mla_w_uq_2", "mla_w_ukv_2", "w_out_2",
                 "ffn2_w_gate_2", "ffn2_w_up_2", "ffn2_w_down_2"):
        host[name] = i[name][0]
    for name in ("ada_w", "w_in", "w_out", "w_gate", "w_up", "w_down"):
        host[name] = i[name]
    return host


def kernel(**inputs):
    import concourse.bacc as bacc
    from concourse.bass_utils import run_bass_kernel_spmd

    host = host_arrays({name: np.asarray(v) for name, v in inputs.items()})
    nc = bacc.Bacc("TRN2", target_bir_lowering=False, num_devices=1)
    arrays, dram = {}, {}
    for name, v in host.items():
        v = np.ascontiguousarray(v)
        arrays[f"in_{name}_dram"] = v
        dram[name] = nc.dram_tensor(f"in_{name}_dram", v.shape, mybir.dt.from_np(v.dtype), kind="ExternalInput").ap()
    out = nc.dram_tensor("out_dram", (SEQ, D), F32, kind="ExternalOutput").ap()
    stages = [Stage("init")] + block_one_stages(dram) + block_two_stages(dram)
    place_stages(stages)
    two_blocks_kernel(nc, dram, out, stages)
    result = run_bass_kernel_spmd(nc, [arrays], core_ids=[0])
    return result.results[0]["out_dram"].reshape(1, SEQ, D)
```
